# Optimizing a Trainium2 kernel written in Bass

```python
import math
import functools
import jax
import jax.numpy as jnp
from jax import lax
import numpy as np

D_MODEL = 1024
BATCH = 1
SEQ = 512
DEPTH = 1
DEC_BATCH = 8
DEC_SEQ = 1
PAST_LEN = 512
PAGE_SIZE = 128

HEAD_DIM = 64
A_HEADS = 8
A_WIDTH = A_HEADS * HEAD_DIM
B_WINDOWS = (128, 512, 2048)
B_DILATIONS = (1, 4, 16)
B_GROUPS = 3
B_HPG = 4
B_HEADS = B_GROUPS * B_HPG
B_QKV_WIDTH = B_HEADS * HEAD_DIM
B_OUT_WIDTH = B_HPG * HEAD_DIM
PLE_DIM = 256
REL_BUCKETS = 32
REL_MAX_DIST = 2048
QBLK = 128
RMS_EPS = 1e-6
NEG_INF = -1e30
ATTN_SCALE = HEAD_DIM ** -0.5
FORGET_BIAS_CENTER = 3.0
IN_SIZES = (A_WIDTH, A_WIDTH, A_WIDTH, A_HEADS, A_WIDTH,
            B_QKV_WIDTH, B_QKV_WIDTH, B_QKV_WIDTH, B_OUT_WIDTH,
            D_MODEL, D_MODEL)
IN_WIDTH = sum(IN_SIZES)

kernel_name = "fox_dilated_gated_hybrid_step"

def rmsnorm(x, g):
    xf = x.astype(jnp.float32)
    y = xf * lax.rsqrt(jnp.mean(xf * xf, axis=-1, keepdims=True) + RMS_EPS)
    return (y * g.astype(jnp.float32)).astype(x.dtype)

def t5_bucket(dist):
    max_exact = REL_BUCKETS // 2
    d = jnp.maximum(dist, 1).astype(jnp.float32)
    large = max_exact + (jnp.log(d / max_exact) / math.log(REL_MAX_DIST / max_exact)
                         * (REL_BUCKETS - max_exact)).astype(jnp.int32)
    large = jnp.minimum(large, REL_BUCKETS - 1)
    return jnp.where(dist < max_exact, dist, large)

def dilated_bias(rel_bias, g):
    r = B_DILATIONS[g]
    n_slots = B_WINDOWS[g] // r + 1
    b = rel_bias[t5_bucket(jnp.arange(n_slots, dtype=jnp.int32) * r)]
    return b[:, g * B_HPG:(g + 1) * B_HPG].T.astype(jnp.float32)

def fox_prompt(q, k, v, logf):
    N, S, H, dh = q.shape
    nb = S // QBLK
    cT = jnp.cumsum(logf, axis=1).transpose(0, 2, 1)
    qb = q.reshape(N, nb, QBLK, H, dh).swapaxes(0, 1)
    cb = cT.reshape(N, H, nb, QBLK).transpose(2, 0, 1, 3)
    k_pos = jnp.arange(S)

    def block(args):
        qi, ci, i = args
        q_pos = i * QBLK + jnp.arange(QBLK)
        s = jnp.einsum("nqhd,nkhd->nhqk", qi, k).astype(jnp.float32) * ATTN_SCALE
        s = s + ci[..., :, None] - cT[:, :, None, :]
        s = jnp.where(k_pos[None, :] <= q_pos[:, None], s, NEG_INF)
        p = jax.nn.softmax(s, axis=-1)
        return jnp.einsum("nhqk,nkhd->nqhd", p, v).astype(q.dtype)

    o = lax.map(block, (qb, cb, jnp.arange(nb)))
    return o.swapaxes(0, 1).reshape(N, S, H, dh)

def fox_sample(q, k_new, v_new, logf_new, kv_pool, logf_pool, page_table):
    DB, T, H, dh = q.shape
    past = kv_pool[page_table]
    P = past.shape[1] * past.shape[2]
    past = past.reshape(DB, P, 2, H, dh)
    k = jnp.concatenate([past[:, :, 0], k_new], axis=1)
    v = jnp.concatenate([past[:, :, 1], v_new], axis=1)
    logf = jnp.concatenate(
        [logf_pool[page_table].reshape(DB, P, H).astype(jnp.float32), logf_new], axis=1)
    cT = jnp.cumsum(logf, axis=1).transpose(0, 2, 1)
    s = jnp.einsum("nqhd,nkhd->nhqk", q, k).astype(jnp.float32) * ATTN_SCALE
    s = s + cT[:, :, P:, None] - cT[:, :, None, :]
    mask = jnp.arange(P + T)[None, :] <= (P + jnp.arange(T))[:, None]
    s = jnp.where(mask, s, NEG_INF)
    p = jax.nn.softmax(s, axis=-1)
    return jnp.einsum("nhqk,nkhd->nqhd", p, v).astype(q.dtype)

def dilated_group(q, k, v, idx, valid, bias):
    kg = k[:, idx]
    vg = v[:, idx]
    s = jnp.einsum("nqhd,nqjhd->nhqj", q, kg).astype(jnp.float32) * ATTN_SCALE
    s = s + bias[None, :, None, :]
    s = jnp.where(valid[None, None], s, NEG_INF)
    m = jnp.max(s, axis=-1)
    e = jnp.exp(s - m[..., None])
    l = jnp.sum(e, axis=-1)
    o = jnp.einsum("nhqj,nqjhd->nqhd", e, vg)
    return m, l, o

def combine_groups(parts, dtype):
    m = jnp.stack([pt[0] for pt in parts])
    l = jnp.stack([pt[1] for pt in parts])
    o = jnp.stack([pt[2] for pt in parts])
    w = jnp.exp(m - jnp.max(m, axis=0, keepdims=True))
    den = jnp.sum(w * l, axis=0)
    num = jnp.sum(w.transpose(0, 1, 3, 2)[..., None] * o, axis=0)
    return (num / den.transpose(0, 2, 1)[..., None]).astype(dtype)

def dilated_prompt(q, k, v, rel_bias):
    N, S = q.shape[:2]
    nb = S // QBLK
    qb = q.reshape(N, nb, QBLK, B_GROUPS, B_HPG, HEAD_DIM).swapaxes(0, 1)
    k_g = [k[:, :, g] for g in range(B_GROUPS)]
    v_g = [v[:, :, g] for g in range(B_GROUPS)]
    biases = [dilated_bias(rel_bias, g) for g in range(B_GROUPS)]

    def block(args):
        qi, i = args
        q_pos = i * QBLK + jnp.arange(QBLK)
        parts = []
        for g in range(B_GROUPS):
            n_slots = B_WINDOWS[g] // B_DILATIONS[g] + 1
            key_pos = q_pos[:, None] - jnp.arange(n_slots)[None, :] * B_DILATIONS[g]
            parts.append(dilated_group(qi[:, :, g], k_g[g], v_g[g],
                                       jnp.maximum(key_pos, 0), key_pos >= 0, biases[g]))
        return combine_groups(parts, q.dtype)

    o = lax.map(block, (qb, jnp.arange(nb)))
    return o.swapaxes(0, 1).reshape(N, S, B_HPG, HEAD_DIM)

def dilated_sample(q, k_new, v_new, bufs, rel_bias):
    T = q.shape[1]
    parts, new_bufs = [], []
    for g in range(B_GROUPS):
        buf = bufs[g]
        wb = buf.shape[1]
        ext = jnp.concatenate([buf, jnp.stack([k_new[:, :, g], v_new[:, :, g]], axis=2)], axis=1)
        n_slots = B_WINDOWS[g] // B_DILATIONS[g] + 1
        e_pos = wb + jnp.arange(T)[:, None] - jnp.arange(n_slots)[None, :] * B_DILATIONS[g]
        parts.append(dilated_group(q[:, :, g], ext[:, :, 0], ext[:, :, 1],
                                   jnp.maximum(e_pos, 0), e_pos >= 0, dilated_bias(rel_bias, g)))
        new_bufs.append(ext[:, T:])
    return combine_groups(parts, q.dtype), new_bufs

def attend_prompt(qa, ka, va, logf, qb, kb, vb, rel_bias):
    S = qa.shape[1]
    o_a = fox_prompt(qa, ka, va, logf)
    o_b = dilated_prompt(qb, kb, vb, rel_bias)
    kv_b = jnp.stack([kb, vb], axis=2)
    bufs = [kv_b[:, S - min(B_WINDOWS[g], S):, :, g] for g in range(B_GROUPS)]
    return o_a, o_b, [jnp.stack([ka, va], axis=2), logf, *bufs]

def attend_sample(qa, ka, va, logf, qb, kb, vb, rel_bias, kv_pool, logf_pool, page_table, bufs):
    o_a = fox_sample(qa, ka, va, logf, kv_pool, logf_pool, page_table)
    o_b, new_bufs = dilated_sample(qb, kb, vb, bufs, rel_bias)
    return o_a, o_b, [jnp.stack([ka, va], axis=2), logf, *new_bufs]

def hybrid_layer(x, p_i, attend, g_pre, w_in, b_f, w_br_a, w_br_b, w_out, g_post,
                 w_ple, g_ple, w_ple_gate):
    N, L, _ = x.shape
    h = rmsnorm(x, g_pre)
    cuts = [int(c) for c in np.cumsum(IN_SIZES)[:-1]]
    qa, ka, va, fa, za, qb, kb, vb, zb, ga, gb = jnp.split(h @ w_in, cuts, axis=-1)
    a_shape = (N, L, A_HEADS, HEAD_DIM)
    b_shape = (N, L, B_GROUPS, B_HPG, HEAD_DIM)
    logf = jax.nn.log_sigmoid(fa.astype(jnp.float32) + b_f.astype(jnp.float32))
    o_a, o_b, state = attend(qa.reshape(a_shape), ka.reshape(a_shape), va.reshape(a_shape), logf,
                             qb.reshape(b_shape), kb.reshape(b_shape), vb.reshape(b_shape))
    u_a = (o_a.reshape(N, L, A_WIDTH) * jax.nn.silu(za)) @ w_br_a
    u_b = (o_b.reshape(N, L, B_OUT_WIDTH) * jax.nn.silu(zb)) @ w_br_b
    merged = jax.nn.sigmoid(ga) * u_a + jax.nn.sigmoid(gb) * u_b
    x = x + rmsnorm(merged @ w_out, g_post)
    x = x + jax.nn.sigmoid(x @ w_ple_gate) * rmsnorm(p_i @ w_ple, g_ple)
    return x, state

def setup_inputs(seed: int = 0) -> dict:
    key = jax.random.key(seed)
    ks = jax.random.split(key, 24)
    f32 = jnp.float32
    n_pages = PAST_LEN // PAGE_SIZE
    n_used = DEC_BATCH * n_pages
    n_pool = n_used + n_used // 4
    nrm = lambda k, shape: jax.random.normal(k, shape, f32)
    page_table = jax.random.permutation(ks[0], n_pool)[:n_used].reshape(DEC_BATCH, n_pages).astype(jnp.int32)
    return {
        "x_prompt": nrm(ks[1], (BATCH, SEQ, D_MODEL)),
        "x_sample": nrm(ks[2], (DEC_BATCH, DEC_SEQ, D_MODEL)),
        "cache_a_kv": nrm(ks[3], (DEPTH, n_pool, PAGE_SIZE, 2, A_HEADS, HEAD_DIM)),
        "cache_a_logf": jax.nn.log_sigmoid(FORGET_BIAS_CENTER + nrm(ks[4], (DEPTH, n_pool, PAGE_SIZE, A_HEADS))),
        "cache_b0_kv": nrm(ks[5], (DEPTH, DEC_BATCH, min(B_WINDOWS[0], PAST_LEN), 2, B_HPG, HEAD_DIM)),
        "cache_b1_kv": nrm(ks[6], (DEPTH, DEC_BATCH, min(B_WINDOWS[1], PAST_LEN), 2, B_HPG, HEAD_DIM)),
        "cache_b2_kv": nrm(ks[7], (DEPTH, DEC_BATCH, min(B_WINDOWS[2], PAST_LEN), 2, B_HPG, HEAD_DIM)),
        "page_table": page_table,
        "p_prompt": nrm(ks[8], (DEPTH, BATCH, SEQ, PLE_DIM)),
        "p_sample": nrm(ks[9], (DEPTH, DEC_BATCH, DEC_SEQ, PLE_DIM)),
        "rel_bias": 0.2 * nrm(ks[10], (REL_BUCKETS, B_HEADS)),
        "g_pre": 1.0 + 0.05 * nrm(ks[11], (DEPTH, D_MODEL)),
        "w_in": nrm(ks[12], (DEPTH, D_MODEL, IN_WIDTH)) * D_MODEL ** -0.5,
        "b_f": FORGET_BIAS_CENTER + 0.1 * nrm(ks[13], (DEPTH, A_HEADS)),
        "w_br_a": nrm(ks[14], (DEPTH, A_WIDTH, D_MODEL)) * A_WIDTH ** -0.5,
        "w_br_b": nrm(ks[15], (DEPTH, B_OUT_WIDTH, D_MODEL)) * B_OUT_WIDTH ** -0.5,
        "w_out": nrm(ks[16], (DEPTH, D_MODEL, D_MODEL)) * D_MODEL ** -0.5,
        "g_post": 1.0 + 0.05 * nrm(ks[17], (DEPTH, D_MODEL)),
        "w_ple": nrm(ks[18], (DEPTH, PLE_DIM, D_MODEL)) * PLE_DIM ** -0.5,
        "g_ple": 1.0 + 0.05 * nrm(ks[19], (DEPTH, D_MODEL)),
        "w_ple_gate": nrm(ks[20], (DEPTH, D_MODEL, D_MODEL)) * D_MODEL ** -0.5,
    }

def reference(x_prompt, x_sample, cache_a_kv, cache_a_logf, cache_b0_kv, cache_b1_kv, cache_b2_kv,
              page_table, p_prompt, p_sample, rel_bias, g_pre, w_in, b_f, w_br_a, w_br_b, w_out,
              g_post, w_ple, g_ple, w_ple_gate):
    xp, xs = x_prompt, x_sample
    states_p, states_s = [], []
    for i in range(DEPTH):
        weights = (g_pre[i], w_in[i], b_f[i], w_br_a[i], w_br_b[i], w_out[i], g_post[i],
                   w_ple[i], g_ple[i], w_ple_gate[i])
        att_p = functools.partial(attend_prompt, rel_bias=rel_bias)
        att_s = functools.partial(attend_sample, rel_bias=rel_bias, kv_pool=cache_a_kv[i],
                                  logf_pool=cache_a_logf[i], page_table=page_table,
                                  bufs=[cache_b0_kv[i], cache_b1_kv[i], cache_b2_kv[i]])
        xp, st_p = hybrid_layer(xp, p_prompt[i], att_p, *weights)
        xs, st_s = hybrid_layer(xs, p_sample[i], att_s, *weights)
        states_p.append(st_p)
        states_s.append(st_s)
    a_kv_p, a_logf_p, b0_p, b1_p, b2_p = [jnp.stack([st[j] for st in states_p]) for j in range(5)]
    a_kv_s, a_logf_s, b0_s, b1_s, b2_s = [jnp.stack([st[j] for st in states_s]) for j in range(5)]
    return (xp, xs, a_kv_p, a_logf_p, b0_p, b1_p, b2_p, a_kv_s, a_logf_s, b0_s, b1_s, b2_s)


_drawn_inputs = setup_inputs


def setup_inputs(seed=0):
    import zlib

    import numpy as np

    out = dict(_drawn_inputs(seed))
    spreads = {}
    factors = {'g_ple': 2.978}
    for name, (base, spread) in spreads.items():
        noise = np.random.default_rng([zlib.crc32(name.encode()), seed]).standard_normal(out[name].shape)
        drawn = base * np.exp(spread * noise) if base else spread * noise
        out[name] = jnp.asarray(drawn.astype(out[name].dtype))
    for name, factor in factors.items():
        out[name] = (out[name] * factor).astype(out[name].dtype)
    return out
```

```python
from contextlib import ExitStack

import numpy as np

import concourse.bass as bass
from concourse import mybir

F32 = mybir.dt.float32
F32R = mybir.dt.float32r
BF16 = mybir.dt.bfloat16
I32 = mybir.dt.int32
ALU = mybir.AluOpType
ACT = mybir.ActivationFunctionType
AX = mybir.AxisListType

P = 128
D = 1024
DC = D // P
SEQ = 512
NB = SEQ // P
DEC = 8
T = SEQ + DEC
HALF = T // 2
HALVES = ((0, HALF), (HALF, T))
HD = 64
AH = 8
AW = AH * HD
BG, BH = 3, 4
DIL = (1, 4, 16)
WIN = (128, 512, 2048)
BQ = BG * BH * HD
BO = BH * HD
PLE = 256
PAGES, PAGE = 4, 128
PAST = PAGES * PAGE
POOL_PAGES = 40
CLS = 4
SCALE = HD ** -0.5
EPS = 1e-6
NEG = -1e30

COL_QA, COL_KA, COL_VA = 0, AW, 2 * AW
COL_F = 3 * AW
COL_ZA = COL_F + AH
COL_QB = COL_ZA + AW
COL_KB, COL_VB = COL_QB + BQ, COL_QB + 2 * BQ
COL_ZB = COL_QB + 3 * BQ
COL_GA = COL_ZB + BO
IN_W = COL_GA + 2 * D

RING = 3
ROUNDS_A, ROUNDS_B = AH // 2, BG * BH // 2
ROUNDS = ROUNDS_A + ROUNDS_B
N_G, N_Z = 16, 6
TILE_G = 3 * ROUNDS
TILE_Z = TILE_G + N_G
TILE_BR = TILE_Z + N_Z
TILE_PLE = TILE_BR + DC
TILE_OUT = TILE_PLE + DC
TILE_GATE = TILE_OUT + DC
TILES = TILE_GATE + DC

TOEP = (256, 128, 128)
PITCH = (384, 256, 256)
SLOTS = (128, 128, 32)


def bucket(dist):
    d = np.maximum(dist, 1).astype(np.float32)
    large = 16 + (np.log(d / np.float32(16)) / np.float32(np.log(2048 / 16)) * np.float32(16)).astype(np.int32)
    return np.where(dist < 16, dist, np.minimum(large, 31))


CONST_COLS = {}
TABLE_COLS = {}


def constants():
    parts, tables = [], []

    def add(name, m, to=parts, cols=CONST_COLS):
        full = np.zeros((P if to is parts else 33, m.shape[1]), np.float32)
        full[:m.shape[0]] = m
        at = sum(x.shape[1] for x in to)
        cols[name] = (at, at + m.shape[1])
        to.append(full)

    i = np.arange(P)
    add("ident", np.eye(P))
    add("ones", np.ones((P, P)))
    add("later", (i[:, None] > i[None, :]) * 1.0)
    add("causal", np.where(i[None, :] <= i[:, None], 0.0, NEG))
    add("row_a", (np.arange(64)[:, None] // AH == np.arange(DEC)) * 1.0)
    add("row_b", (np.arange(32)[:, None] // BH == np.arange(DEC)) * 1.0)
    for g in range(BG):
        y = np.arange(PITCH[g])
        dist = 255 - y if g == 0 else (127 - y) * CLS
        seen = (dist >= 0) & (dist <= WIN[g]) & (dist % DIL[g] == 0)
        hot = np.zeros((33, PITCH[g]))
        hot[np.where(seen, bucket(np.maximum(dist, 0)), 32), y] = 1
        add(f"toep{g}", hot, tables, TABLE_COLS)
    for g in range(BG):
        n = SLOTS[g]
        dist = np.concatenate([(n - np.arange(n)) * DIL[g], [0]])
        hot = np.zeros((33, n + 1))
        hot[bucket(dist), np.arange(n + 1)] = 1
        add(f"slots{g}", hot, tables, TABLE_COLS)
    return np.concatenate(parts, axis=1), np.concatenate(tables, axis=1)


CONST, TABLES = constants()


class Tally:

    def __init__(self, sem):
        self.sem, self.n = sem, 0

    def up(self, ins):
        ins.then_inc(self.sem, 1)
        self.n = self.n + 1
        return ins


def build(nc, A, O, const_in):
    with ExitStack() as ctx:
        cursor = [nc.sbuf_base + 31 & ~31]
        top = [cursor[0]]

        def sb(name, shape, dt=F32, at=None):
            size = int(np.prod(shape[1:])) * (2 if dt == BF16 else 4)
            size = size + 31 & ~31
            if at is not None:
                cursor[0] = at
            t = nc.alloc_sbuf_tensor_at(name, shape, dt, offset=cursor[0])
            cursor[0] += size
            top[0] = max(top[0], cursor[0])
            return t

        def bank(name):
            return ctx.enter_context(nc.psum_tensor(name, [P, 512], F32))

        def sem(name):
            return ctx.enter_context(nc.semaphore(name))

        def sems(name, n):
            return [sem(f"{name}{i}") for i in range(n)]

        pj = [bank("pj0"), bank("pj1")]
        sc = [bank("sc0"), bank("sc1")]
        tr = [bank("tr0"), bank("tr1")]
        pv = [bank("pv0"), bank("pv1")]

        const = sb("const", [P, CONST.shape[1]])
        cst = lambda name, rows=P: const[0:rows, CONST_COLS[name][0]:CONST_COLS[name][1]]
        ident, ones = cst("ident"), cst("ones")
        identb = sb("identb", [P, P], BF16)
        causalb = sb("causalb", [P, P], BF16)
        gpre, gpost, gple = sb("gpre", [P, DC]), sb("gpost", [P, DC]), sb("gple", [P, DC])
        xT = sb("xT", [P, DC, T])
        h_hi, h_lo = sb("h_hi", [P, DC, T], F32R), sb("h_lo", [P, DC, T], F32R)
        w_raw = [sb(f"w_raw{i}", [P, DC, P]) for i in range(RING)]
        w_hi = [sb(f"w_hi{i}", [P, DC, P], F32R) for i in range(RING)]
        w_lo = [sb(f"w_lo{i}", [P, DC, P], F32R) for i in range(RING)]
        samp = sb("samp", [P, 3 * ROUNDS, DEC])
        lg_a = sb("lg_a", [P, PAGES, DEC, AH])
        lg_b = sb("lg_b", [P, BG, DEC, BH])
        lf_small = sb("lf_small", [P, NB + 1, AH])
        oaT, obT = sb("oaT", [P, AW // P, T]), sb("obT", [P, BO // P, T])
        zsil = sb("zsil", [P, N_Z, T])
        at_g = cursor[0]
        gsig = sb("gsig", [P, N_G, T])
        after_g = cursor[0]
        yT, eT = (sb("yT", [P, DC, T], at=at_g), sb("eT", [P, DC, T], at=at_g + DC * T * 4))
        x_in = sb("x_in", [P, NB, D], at=at_g)
        xs_in = sb("xs_in", [DEC, D])
        cursor[0] = after_g
        at_2 = cursor[0]
        mbuf, lbuf = sb("mbuf", [P, BG, CLS, BH]), sb("lbuf", [P, BG, CLS, BH])
        obuf = sb("obuf", [P, BG, CLS, BO])
        toep = [sb(f"toep{g}", [P, BH, TOEP[g]]) for g in range(BG)]
        at_3 = cursor[0]
        q_aug = [sb(f"q_aug{i}", [HD + 2, 2, T]) for i in range(2)]
        k_aug = [sb(f"k_aug{i}", [HD + 2, 2, T]) for i in range(2)]
        kT, vT = sb("kT", [P, T]), sb("vT", [P, T])
        k_tok, v_tok = sb("k_tok", [P, NB, P]), sb("v_tok", [P, NB, P])
        prob = [sb(f"prob{i}", [P, 512]) for i in range(2)]
        probT = [sb(f"probT{i}", [P, 512]) for i in range(2)]
        at_4 = cursor[0]
        biased = [sb(f"biased{i}", [P, 512]) for i in range(2)]
        o_tok = sb("o_tok", [P, NB, P], at=at_4)
        top_m, den_m = sb("top_m", [P, CLS * BH], at=at_4), sb("den_m", [P, CLS * BH])
        cursor[0] = at_4 + 4096
        l_a, r_a, nm_a = sb("l_a", [P, 8]), sb("r_a", [P, 8]), sb("nm_a", [P, 8])
        nm_b = sb("nm_b", [P, 8])
        wf_raw, wf_hi, wf_lo = sb("wf_raw", [P, DC, AH]), sb("wf_hi", [P, DC, AH], F32R), sb("wf_lo", [P, DC, AH], F32R)
        bf = sb("bf", [AH, 1])
        sq = [sb("sq0", [P, T], at=at_3), sb("sq1", [P, T])]
        sq_s = sb("sq_s", [P, DC, DEC])
        acc, rs, nv, nt = sb("acc", [P, T]), sb("rs", [P, T]), sb("nv", [P, T]), sb("nt", [P, T])
        h_raw = [sb("h_raw0", [P, T]), sb("h_raw1", [P, T])]
        gen = [sb(f"gen{g}", [BH, PITCH[g]]) for g in range(BG)]
        tables = sb("tables", [33, TABLES.shape[1]])
        relb = sb("relb", [33, 12])
        relb_rows = sb("relb_rows", [33, BG, DEC, BH])
        assert cursor[0] <= at_4
        fx = sb("fx", [AH, T], at=at_2)
        fa, fe, fu, fd, fr = (sb(n, [AH, T]) for n in ("fa", "fe", "fu", "fd", "fr"))
        assert cursor[0] <= at_2 + 384 + CLS * BG * BO * 4
        st = sb("st", [DEC, 3 * ROUNDS, P], at=at_3)
        kv_a = [sb(f"kv_a{i}", [P, PAGES, AW]) for i in range(2)]
        kv_b = [sb(f"kv_b{i}", [P, BG, BO]) for i in range(2)]
        self_p = sb("self_p", [DEC, ROUNDS, P], at=at_3 + 3 * ROUNDS * P * 4 + PAGES * AW * 4)
        qbc = [sb(f"qbc{i}", [P, AW + BQ], at=at_2 + i * 4 * (AW + BQ)) for i in range(2)]
        prod = [sb(f"prod{i}", [P, AW]) for i in range(2)]
        assert cursor[0] <= at_3
        cursor[0] = top[0]
        bias_s = sb("bias_s", [DEC * BH, sum(SLOTS) + BG])
        logf = sb("logf", [AH, T])
        cum, ncum = sb("cum", [AH, SEQ], at=at_4), sb("ncum", [AH, SEQ], at=at_4 + 2048)
        cursor[0] = top[0]
        pt = sb("pt", [1, DEC * PAGES], I32)
        pt_col = sb("pt_col", [DEC * PAGES, 1], I32)
        sm = sb("sm", [DEC * AH, 16])
        self_a, self_b = sb("self_a", [DEC, AH]), sb("self_b", [DEC, BH, BG])
        row_a = sb("row_a", [DEC * AH, PAST + 1], at=at_2)
        row_b = sb("row_b", [DEC * BH, sum(SLOTS) + BG])
        lf_rows = sb("lf_rows", [DEC * PAGES, PAGE * AH])
        lfT = sb("lfT", [P, PAGES, DEC, AH])
        pTa = sb("pTa", [P, PAGES, DEC, AH])
        pTb = sb("pTb", [P, BG, DEC, BH])
        dsel_a, dsel_b = sb("dsel_a", [64, DEC]), sb("dsel_b", [32, BG, DEC])
        d_a, d_b = sb("d_a", [DEC, 64]), sb("d_b", [DEC, BG, 32])
        os_a, os_b = sb("os_a", [P, 256]), sb("os_b", [P, 64])
        assert cursor[0] <= at_3
        og_hi, og_lo = sb("og_hi", [P, 6, T], F32R, at=at_2), sb("og_lo", [P, 6, T], F32R)
        og_raw = [sb(f"og_raw{i}", [P, T]) for i in range(2)]
        pT_hi, pT_lo = sb("pT_hi", [P, 2, T], F32R), sb("pT_lo", [P, 2, T], F32R)
        p_in, ps_in = sb("p_in", [P, NB, PLE]), sb("ps_in", [DEC, PLE])
        assert cursor[0] <= top[0], (cursor[0], top[0])
        sq2 = [sb("sq2_0", [P, T]), sb("sq2_1", [P, T])]
        acc_y, acc_e, rs_y, rs_e, nv2, nt2 = (sb(n, [P, T]) for n in ("acc_y", "acc_e", "rs_y", "rs_e", "nv2", "nt2"))
        assert cursor[0] <= top[0]
        sg = [sb("sg0", [P, T], at=at_2), sb("sg1", [P, T])]
        fin = [sb(f"fin{i}", [P, T]) for i in range(2)]
        tok_out = [sb(f"tok_out{i}", [P, NB, P]) for i in range(2)]
        toks_out = sb("toks_out", [DEC, D])
        assert cursor[0] <= top[0], (cursor[0], top[0])

        c_dram = nc.dram_tensor("c_dram", [2, AH, SEQ], F32).ap()
        toep_dram = [nc.dram_tensor(f"toep_dram{g}", [BH, P * PITCH[g]], F32).ap() for g in range(BG)]
        o0_dram = nc.dram_tensor("o0_dram", [SEQ, BO], F32).ap()
        m0_dram, l0_dram = (nc.dram_tensor(n, [SEQ, BH], F32).ap() for n in ("m0_dram", "l0_dram"))
        q_dram = nc.dram_tensor("q_dram", [DEC, ROUNDS * P], F32).ap()
        selfa_dram = nc.dram_tensor("selfa_dram", [DEC, AH], F32).ap()
        selfb_dram = nc.dram_tensor("selfb_dram", [DEC, BH * BG], F32).ap()
        lfn_dram = nc.dram_tensor("lfn_dram", [DEC, AH], F32).ap()

        (yp, ys, akv_p, alf_p, b0_p, b1_p, b2_p, akv_s, alf_s, b0_s, b1_s, b2_s) = O
        b_p, b_s = (b0_p, b1_p, b2_p), (b0_s, b1_s, b2_s)
        caches = (A["cache_b0_kv"], A["cache_b1_kv"], A["cache_b2_kv"])
        w_in = A["w_in"][0].rearrange("(c p) n -> p c n", p=P)
        w_br_a = A["w_br_a"][0].rearrange("(c p) n -> p c n", p=P)
        w_br_b = A["w_br_b"][0].rearrange("(c p) n -> p c n", p=P)
        w_out = A["w_out"][0].rearrange("(c p) n -> p c n", p=P)
        w_ple = A["w_ple"][0].rearrange("(c p) n -> p c n", p=P)
        w_gate = A["w_ple_gate"][0].rearrange("(c p) n -> p c n", p=P)

        def weight_parts(n):
            if n < TILE_G:
                r, j = n // 3, n % 3
                if r < ROUNDS_A:
                    col = (COL_QA, COL_KA, COL_VA)[j] + r * P
                else:
                    col = (COL_QB, COL_KB, COL_VB)[j] + (r - ROUNDS_A) * P
                return [(w_in[:, :, col:col + P], 0, DC)]
            if n < TILE_Z:
                col = COL_GA + (n - TILE_G) * P
                return [(w_in[:, :, col:col + P], 0, DC)]
            if n < TILE_BR:
                z = n - TILE_Z
                col = COL_ZA + z * P if z < AW // P else COL_ZB + (z - AW // P) * P
                return [(w_in[:, :, col:col + P], 0, DC)]
            m = (n - TILE_BR) % DC
            cols = slice(m * P, (m + 1) * P)
            if n < TILE_PLE:
                return [(w_br_a[:, :, cols], 0, 4), (w_br_b[:, :, cols], 4, 2)]
            if n < TILE_OUT:
                return [(w_ple[:, :, cols], 0, 2)]
            return [((w_out if n < TILE_GATE else w_gate)[:, :, cols], 0, DC)]

        def chunks(n):
            return sum(k for _, _, k in weight_parts(n))

        landed_at, total = {}, [0] * RING
        for n in range(TILES):
            total[n % RING] += 16 * len(weight_parts(n))
            landed_at[n] = total[n % RING]

        def units(r):
            if r == 0:
                return []
            return [(hd, qb) for qb in range(NB) for hd in range(2)] if r <= ROUNDS_A + 2 else [(0, None), (1, None)]

        unit0, use0, u, k = {}, {}, 0, DC + 1
        for r in range(1, ROUNDS + 1):
            unit0[r], use0[r] = u, k
            u += len(units(r))
            k += 2 + len(units(r)) + (r <= ROUNDS_A)
        UNITS, USE_COMBINE = u, k
        USE_SAMP = USE_COMBINE + 2
        USE_LF = USE_SAMP + 8
        pt_use = {unit0[r] + i: use0[r] + 2 + i for r in unit0 for i in range(len(units(r)))}
        is_a = lambda r: r <= ROUNDS_A
        unit_a = 8 * ROUNDS_A

        s_const, s_x, s_xs, s_wf, s_cd, s_cds = (sem(n) for n in ("s_const", "s_x", "s_xs", "s_wf", "s_cd", "s_cds"))
        s_w = sems("s_w", RING)
        s_crow = sems("s_crow", 2)
        s_hi, s_lo = sem("s_hi"), sem("s_lo")
        s_half, s_free = sems("s_half", 2), sems("s_free", 2)
        s_use, s_used = sem("s_use"), sem("s_used")
        s_sc, s_mx, s_ex, s_rc, s_pv, s_pve = (sem(n) for n in ("s_sc", "s_mx", "s_ex", "s_rc", "s_pv", "s_pve"))
        s_kst, s_vst = sem("s_kst"), sem("s_vst")
        s_v = sem("s_v")
        s_a = sem("s_a")
        s_p = sem("s_p")
        names = ("s_idb s_relb s_sq s_sqs s_accp s_accs s_ssum s_nv s_y0 s_rs s_hraw s_hhi s_hlo s_wfhi s_wflo s_gen s_gent s_gend s_toep "
                 "s_biasm s_bias s_fm s_fx s_fe s_fu s_fl s_logf s_cum s_lft s_clear s_xst s_xsd s_xsv s_copy s_ge s_gs s_zs "
                 "s_o0 s_o0r s_md s_wexp s_comb s_selfp s_sst s_qd s_qb0 s_qb1 s_kp0 s_kp1 s_bk0 s_bk1 s_prod s_red "
                 "s_lfr s_lfl s_suf s_lga s_rowt s_rowb s_selfr s_nma s_nmb s_exa s_exb s_pn s_pta s_dm s_dv s_ds s_samp s_ov s_slf s_slfd "
                 "s_ogr s_ogh s_ogl s_brb s_mr s_mh s_ml s_pin s_ptr s_pte s_pth s_ptl s_e0 s_e1 s_sqe s_ace s_sy0 s_sy1 s_sqy s_acy "
                 "s_sse s_nve s_y0e s_rse s_ssy s_nvy s_y0y s_rsy s_en s_x2 s_x2h s_x2l s_gte s_sig s_fin s_tt s_tte s_tts s_ttse s_yst0 s_yst1 s_ysst s_lfst").split()
        S = {n: sem(n) for n in names}

        N_CONST = 10
        block = ctx.enter_context(nc.Block())

        @block.sync
        def _(sp):
            def load(n):
                if n >= RING:
                    sp.wait_ge(s_lo, n - RING + 1)
                for src, c0, nk in weight_parts(n):
                    sp.dma_start(w_raw[n % RING][:, c0:c0 + nk, :], src).then_inc(s_w[n % RING], 16)

            for b in range(NB):
                sp.dma_start(x_in[:, b, :], A["x_prompt"][0, b * P:(b + 1) * P, :]).then_inc(s_x, 16)
            sp.dma_start(xs_in[:, :], A["x_sample"].rearrange("s o d -> (s o) d")).then_inc(s_xs, 16)
            sp.dma_start(wf_raw[:, :, :], w_in[:, :, COL_F:COL_F + AH]).then_inc(s_wf, 16)
            for n in range(RING):
                load(n)
            sp.wait_ge(S["s_cum"], 2)
            sp.dma_start(c_dram[0], cum[:, :]).then_inc(s_cd, 16)
            sp.dma_start(c_dram[1], ncum[:, :]).then_inc(s_cd, 16)
            sp.wait_ge(s_cd, 32)
            sp.wait_ge(S["s_clear"], 1)
            for r in range(ROUNDS_A):
                for n in range(3 * r + 3, 3 * r + 5):
                    load(n)
                if r >= 2:
                    sp.wait_ge(s_sc, 8 * (r - 1))
                s = r % 2
                sp.dma_start(q_aug[s][HD + 1:HD + 2, :, 0:SEQ], c_dram[0:1, 2 * r:2 * r + 2, :]).then_inc(s_crow[s], 16)
                sp.dma_start(k_aug[s][HD:HD + 1, :, 0:SEQ], c_dram[1:2, 2 * r:2 * r + 2, :]).then_inc(s_crow[s], 16)
                load(3 * r + 5)
            for n in range(3 * ROUNDS_A + 3, TILE_G + 9):
                load(n)

            def sample_queries(s):
                if s >= 2:
                    sp.wait_ge(S["s_prod"], 7 * (s - 1))
                sp.dma_start(qbc[s % 2][:, :], q_dram[s:s + 1, :].to_broadcast([P, ROUNDS * P])).then_inc(S[f"s_qb{s % 2}"], 16)

            def sample_rows(s, kv):
                for p in range(PAGES):
                    page = sp.value_load(pt[0:1, PAGES * s + p:PAGES * s + p + 1], min_val=0, max_val=POOL_PAGES - 1)
                    src = A["cache_a_kv"][0, bass.ds(page, 1), :, kv, :, :].rearrange("o t h d -> (o t) (h d)")
                    sp.dma_start(kv_a[s % 2][:, p, :], src).then_inc(S[f"s_kp{s % 2}"], 16)
                for g in range(BG):
                    n, step = SLOTS[g], DIL[g]
                    src = caches[g][0, s, 0:n * step:step, kv, :, :].rearrange("t h d -> t (h d)")
                    sp.dma_start(kv_b[s % 2][0:n, g, :], src).then_inc(S[f"s_bk{s % 2}"], 16)

            sp.wait_ge(s_const, 16 * 8)
            sp.wait_ge(S["s_qd"], 16)
            sp.wait_ge(S["s_comb"], 1)
            sp.wait_ge(S["s_selfp"], 1)
            n = TILE_G + 9
            for s in range(DEC):
                sample_queries(s)
                sample_rows(s, 0)
                load(n)
                n += 1
            sp.wait_ge(S["s_red"], 7 * DEC)
            sp.wait_ge(S["s_prod"], 7 * DEC)
            for i in range(DEC * PAGES):
                page = sp.value_load(pt[0:1, i:i + 1], min_val=0, max_val=POOL_PAGES - 1)
                sp.dma_start(lf_rows[i:i + 1, :], A["cache_a_logf"][0, bass.ds(page, 1), :, :].rearrange("o t h -> o (t h)")).then_inc(S["s_lfr"], 16)
            sp.wait_ge(S["s_slfd"], 48)
            sp.dma_start(row_a[:, PAST:PAST + 1], selfa_dram.rearrange("s (h o) -> (s h) o", o=1)).then_inc(S["s_selfr"], 16)
            sp.dma_start(sm[:, 0:1], lfn_dram.rearrange("s (h o) -> (s h) o", o=1)).then_inc(S["s_selfr"], 16)
            sp.dma_start(sm[0:DEC * BH, 1:1 + BG], selfb_dram.rearrange("s (h g) -> (s h) g", g=BG)).then_inc(S["s_selfr"], 16)
            for s in range(2):
                sample_rows(s, 1)
            while n < TILE_BR:
                load(n)
                n += 1
            for s in range(2, DEC):
                sp.wait_ge(S["s_samp"], s - 1)
                sample_rows(s, 1)
                if s >= 5:
                    load(n)
                    n += 1
            sp.wait_ge(S["s_ov"], 1)
            sp.dma_start(p_in[:, :, :], A["p_prompt"][0, 0].rearrange("(b p) d -> p b d", p=P)).then_inc(S["s_pin"], 16)
            sp.dma_start(ps_in[:, :], A["p_sample"][0].rearrange("s o d -> (s o) d")).then_inc(S["s_pin"], 16)
            while n < TILES:
                load(n)
                n += 1

        @block.gpsimd
        def _(pool):
            own = Tally(s_p)
            pool.dma_start(const[:, :], const_in[0]).then_inc(s_const, 16)
            pool.dma_start(tables[:, :], const_in[1]).then_inc(s_const, 16)
            for dst, name in ((gpre, "g_pre"), (gpost, "g_post"), (gple, "g_ple")):
                pool.dma_start(dst[:, :], A[name][0].rearrange("(c p) -> p c", p=P), allow_slow_non_contiguous=True).then_inc(s_const, 16)
            pool.dma_start(relb[0:32, :], A["rel_bias"]).then_inc(s_const, 16)
            pool.dma_start(bf[:, :], A["b_f"].rearrange("o h -> h o"), allow_slow_non_contiguous=True).then_inc(s_const, 16)
            pool.dma_start(pt[:, :], A["page_table"].rearrange("(o s) p -> o (s p)", o=1)).then_inc(s_const, 16)
            pool.wait_ge(s_const, 16 * 8)
            for c in range(DC):
                pool.wait_ge(S["s_sq"], c + 1)
                if c == 0:
                    nc.gpsimd.tensor_copy(acc[:, 0:SEQ], sq[0][:, 0:SEQ]).then_inc(S["s_accp"], 1)
                else:
                    pool.wait_ge(S["s_accp"], c)
                    nc.gpsimd.tensor_tensor(acc[:, 0:SEQ], acc[:, 0:SEQ], sq[c % 2][:, 0:SEQ], ALU.add).then_inc(S["s_accp"], 1)
            pool.wait_ge(S["s_gen"], BG)
            for g in range(BG):
                for h in range(BH):
                    src = gen[g][h:h + 1, :].unsqueeze(1).to_broadcast([1, P, PITCH[g]])
                    pool.dma_start(toep_dram[g][h:h + 1, :].rearrange("o (i y) -> o i y", i=P), src).then_inc(S["s_gend"], 16)
            for c in range(DC):
                pool.wait_ge(S["s_hhi"], c + 1)
                nc.gpsimd.tensor_tensor(h_lo[:, c, :], h_raw[c % 2][:, :], h_hi[:, c, :].bitcast(F32), ALU.subtract).then_inc(S["s_hlo"], 1)
            pool.wait_ge(S["s_gend"], 16 * BG * BH)
            pool.wait_ge(S["s_logf"], 1)
            for g in range(BG):
                for h in range(BH):
                    rows = toep_dram[g][h, P - 1:P - 1 + P * (PITCH[g] - 1)].rearrange("(i y) -> i y", i=P)
                    pool.dma_start(toep[g][:, h, :], rows[:, 0:TOEP[g]]).then_inc(S["s_toep"], 16)
            pool.wait_ge(s_used, DC + 1)
            pool.dma_start(alf_p[0, 0].rearrange("(b p) h -> p b h", p=P), lf_small[:, 0:NB, :]).then_inc(S["s_lfst"], 16)
            pool.dma_start(alf_s[0].rearrange("s o h -> (s o) h"), lf_small[0:DEC, NB, :]).then_inc(S["s_lfst"], 16)
            pool.dma_start(lfn_dram, lf_small[0:DEC, NB, :]).then_inc(S["s_slfd"], 16)

            for r in range(1, ROUNDS + 1):
                t = r - 1
                if r <= ROUNDS - 1:
                    for g in range(BG):
                        wb = caches[g].shape[2]
                        if g == 0 and r > 1:
                            continue
                        s0, s1 = (0, DEC) if g == 0 else (r - 1, r)
                        if s1 > DEC:
                            continue
                        a = 16 // (s1 - s0)
                        pool.dma_start(b_s[g][0, s0:s1, 0:wb - 1].rearrange("s t k h d -> s (t k h d)").rearrange("s (a n) -> s a n", a=a),
                                       caches[g][0, s0:s1, 1:wb].rearrange("s t k h d -> s (t k h d)").rearrange("s (a n) -> s a n", a=a)).then_inc(S["s_copy"], 16)
                pool.wait_ge(s_used, use0[r] + 1)
                for kv, (buf, done) in enumerate(((k_tok, s_kst), (v_tok, s_vst))):
                    if kv == 1:
                        pool.wait_ge(s_used, use0[r] + 2)
                    if is_a(r):
                        dst = akv_p[0, 0, :, kv, 2 * t:2 * t + 2, :].rearrange("(b p) h d -> p b (h d)", p=P)
                        pool.dma_start(dst, buf[:, :, :]).then_inc(done, 16)
                    else:
                        g, hp = divmod(t - ROUNDS_A, 2)
                        out = b_p[g][0, 0, :, kv, 2 * hp:2 * hp + 2, :]
                        if g == 0:
                            pool.dma_start(out.rearrange("p h d -> p (h d)"), buf[:, NB - 1, :]).then_inc(done, 16)
                        elif kv == 0:
                            pool.dma_start(out.rearrange("(b p) h d -> p b (h d)", p=P), buf[:, :, :]).then_inc(done, 16)
                        else:
                            pool.dma_start(out.rearrange("(p c) h d -> p c (h d)", c=CLS), buf[:, :, :]).then_inc(done, 16)
                if r == ROUNDS_A + 2:
                    pool.wait_ge(s_pve, unit0[r + 1])
                    pool.wait_ge(s_mx, unit0[r + 1])
                    pool.dma_start(o0_dram.rearrange("(b p) n -> p b n", p=P), obuf[:, 0]).then_inc(S["s_o0"], 16)
                    pool.dma_start(m0_dram.rearrange("(b p) n -> p b n", p=P), mbuf[:, 0]).then_inc(S["s_o0"], 16)
                    pool.dma_start(l0_dram.rearrange("(b p) n -> p b n", p=P), lbuf[:, 0]).then_inc(S["s_o0"], 16)
                    pool.wait_ge(S["s_o0"], 48)
                    pool.dma_start(obuf[:, 0], o0_dram.rearrange("(p c) n -> p c n", c=CLS)).then_inc(S["s_o0r"], 16)
                    pool.dma_start(mbuf[:, 0], m0_dram.rearrange("(p c) n -> p c n", c=CLS)).then_inc(S["s_o0r"], 16)
                    pool.dma_start(lbuf[:, 0], l0_dram.rearrange("(p c) n -> p c n", c=CLS)).then_inc(S["s_o0r"], 16)
            pool.wait_ge(s_used, USE_SAMP + 8)
            stv = st[:, :, :].rearrange("s (r j) c -> s j r c", j=3)
            pool.dma_start(q_dram.rearrange("s (r c) -> s r c", c=P), stv[:, 0]).then_inc(S["s_qd"], 16)
            for kv in range(2):
                pool.dma_start(akv_s[0, :, 0, kv].rearrange("s (r h) d -> s r (h d)", h=2), stv[:, 1 + kv, 0:ROUNDS_A]).then_inc(S["s_sst"], 16)
                for g in range(BG):
                    wb = caches[g].shape[2]
                    r0 = ROUNDS_A + 2 * g
                    pool.dma_start(b_s[g][0, :, wb - 1, kv].rearrange("s (r h) d -> s r (h d)", h=2), stv[:, 1 + kv, r0:r0 + 2]).then_inc(S["s_sst"], 16)
            pool.wait_ge(S["s_selfp"], 1)
            pool.dma_start(selfa_dram, self_a[:, :]).then_inc(S["s_slfd"], 16)
            pool.dma_start(selfb_dram, self_b[:, :, :].rearrange("s h g -> s (h g)")).then_inc(S["s_slfd"], 16)
            k = 0
            for s in range(DEC):
                pool.wait_ge(S[f"s_qb{s % 2}"], 16 * (s // 2 + 1))
                pool.wait_ge(S[f"s_kp{s % 2}"], 64 * (s // 2 + 1))
                pool.wait_ge(S[f"s_bk{s % 2}"], 48 * (s // 2 + 1))
                for i in range(PAGES + BG):
                    if k >= 2:
                        pool.wait_ge(S["s_red"], k - 1)
                    if i < PAGES:
                        nc.gpsimd.tensor_tensor(prod[k % 2][:, :], kv_a[s % 2][:, i, :], qbc[s % 2][:, 0:AW], ALU.mult).then_inc(S["s_prod"], 1)
                    else:
                        g = i - PAGES
                        n = SLOTS[g]
                        nc.gpsimd.tensor_tensor(prod[k % 2][0:n, 0:BO], kv_b[s % 2][0:n, g, :], qbc[s % 2][0:n, AW + g * BO:AW + (g + 1) * BO], ALU.mult).then_inc(S["s_prod"], 1)
                    k += 1
            for i in range(6):
                pool.wait_ge(S["s_ogh"], i + 1)
                nc.gpsimd.tensor_tensor(og_lo[:, i, :], og_raw[i % 2][:, :], og_hi[:, i, :].bitcast(F32), ALU.subtract).then_inc(S["s_ogl"], 1)
            for m in range(DC):
                pool.wait_ge(S["s_mh"], m + 1)
                nc.gpsimd.tensor_tensor(h_lo[:, m, :], gsig[:, m, :], h_hi[:, m, :].bitcast(F32), ALU.subtract).then_inc(S["s_ml"], 1)
            for name, total_, sems_ in (("e", acc_e, ("s_sqe", "s_ace")), ("y", acc_y, ("s_sqy", "s_acy"))):
                for m in range(DC):
                    pool.wait_ge(S[sems_[0]], m + 1)
                    if m == 0:
                        nc.gpsimd.tensor_copy(total_[:, :], sq2[0][:, :]).then_inc(S[sems_[1]], 1)
                    else:
                        pool.wait_ge(S[sems_[1]], m)
                        nc.gpsimd.tensor_tensor(total_[:, :], total_[:, :], sq2[m % 2][:, :], ALU.add).then_inc(S[sems_[1]], 1)
            for c in range(DC):
                pool.wait_ge(S["s_x2h"], c + 1)
                nc.gpsimd.tensor_tensor(h_lo[:, c, :], xT[:, c, :], h_hi[:, c, :].bitcast(F32), ALU.subtract).then_inc(S["s_x2l"], 1)
            for m in range(DC):
                pool.wait_ge(S["s_tte"], m + 1)
                pool.dma_start(yp[0, :, m * P:(m + 1) * P].rearrange("(b p) d -> p b d", p=P), tok_out[m % 2][:, :, :]).then_inc(S[f"s_yst{m % 2}"], 16)
            pool.wait_ge(S["s_ttse"], 2)
            pool.dma_start(ys.rearrange("s o d -> (s o) d"), toks_out[:, :]).then_inc(S["s_ysst"], 16)
            pool.wait_ge(S["s_lfst"], 32)
            pool.wait_ge(S["s_copy"], 16 * (1 + 2 * DEC))
            pool.wait_ge(s_kst, 16 * ROUNDS)
            pool.wait_ge(s_vst, 16 * ROUNDS)
            pool.wait_ge(S["s_sst"], 16 * 8)
            pool.wait_ge(S["s_yst0"], 16 * DC // 2)
            pool.wait_ge(S["s_yst1"], 16 * DC // 2)
            pool.wait_ge(S["s_ysst"], 16)

        def sample_rows_t(pe, turn):
            pe.wait_ge(S["s_lfr"], 16 * DEC * PAGES)
            turn([(P, h * 32, lf_rows[:, h:PAGE * AH:AH]) for h in range(AH)])
            pe.wait_ge(s_used, USE_LF + 1)
            pe.wait_ge(s_mx, UNITS)
            cols = lfT[:, :, :, :].rearrange("p g s h -> p (g s h)")
            nc.tensor.matmul(sc[0][:, 0:256], cst("later"), cols, start=True, stop=False)
            for k in range(1, PAGES):
                w = 256 - 64 * k
                last = nc.tensor.matmul(sc[0][:, 0:w], ones, cols[:, 64 * k:256], start=False, stop=k == PAGES - 1)
            last.then_inc(S["s_suf"], 1)
            pe.wait_ge(S["s_lga"], 1)
            turn([(DEC * AH, p * P, lg_a[:, p, :, :].rearrange("p s h -> p (s h)")) for p in range(PAGES)])
            at, outs = 0, []
            for g in range(BG):
                outs.append((DEC * BH, at, lg_b[0:SLOTS[g], g, :, :].rearrange("p s h -> p (s h)")))
                at += SLOTS[g] + 1
            turn(outs)

        def sample_probs_t(pe, turn):
            pe.wait_ge(S["s_pn"], 2)
            turn([(P, p * 64, row_a[:, p * P:(p + 1) * P]) for p in range(PAGES)])
            at, outs = 0, []
            for g in range(BG):
                outs.append((SLOTS[g], g * 32, row_b[:, at:at + SLOTS[g]]))
                at += SLOTS[g] + 1
            turn(outs)
            pe.wait_ge(S["s_ds"], 1 + BG)
            pe.wait_ge(S["s_lga"], 1)
            nc.tensor.matmul(pv[0][0:DEC, 0:64], dsel_a[:, :], ident[0:64, 0:64], start=True, stop=True)
            for g in range(BG):
                last = nc.tensor.matmul(pv[0][0:DEC, 64 + 32 * g:96 + 32 * g], dsel_b[:, g, :], ident[0:32, 0:32], start=True, stop=True)
            last.then_inc(S["s_dm"], 1)
            pe.wait_ge(S["s_dv"], 2)
            for cc in range(AW // P):
                nc.tensor.matmul(pv[1][:, cc * 64:(cc + 1) * 64], st[:, 3 * cc + 2, :], d_a[:, :], start=True, stop=True)
            for cc in range(BO // P):
                for g in range(BG):
                    last = nc.tensor.matmul(pv[1][:, 256 + cc * 32:288 + cc * 32], st[:, 3 * (ROUNDS_A + 2 * g + cc) + 2, :], d_b[:, g, :], start=g == 0, stop=g == BG - 1)
            last.then_inc(S["s_slf"], 1)

        def sample_values(pe, s):
            pe.wait_ge(S[f"s_kp{s % 2}"], 64 * (DEC // 2 + s // 2 + 1))
            pe.wait_ge(S[f"s_bk{s % 2}"], 48 * (DEC // 2 + s // 2 + 1))
            pe.wait_ge(s_used, USE_LF + 5)
            for cc in range(AW // P):
                for p in range(PAGES):
                    nc.tensor.matmul(sc[0][:, cc * 64 + s * AH:cc * 64 + (s + 1) * AH], kv_a[s % 2][:, p, cc * P:(cc + 1) * P],
                                     pTa[:, p, s, :], start=p == 0, stop=p == PAGES - 1)
            for cc in range(BO // P):
                for g in range(BG):
                    n = SLOTS[g]
                    last = nc.tensor.matmul(sc[1][:, cc * 32 + s * BH:cc * 32 + (s + 1) * BH], kv_b[s % 2][0:n, g, cc * P:(cc + 1) * P],
                                            pTb[0:n, g, s, :], start=g == 0, stop=g == BG - 1)
            last.then_inc(S["s_samp"], 1)

        @block.tensor
        def _(pe):
            use = Tally(s_use)

            def turn(outs):
                b = tr[use.n % 2]
                if use.n >= 2:
                    pe.wait_ge(s_used, use.n - 1)
                for rows, c0, src in outs:
                    k = src.shape[0]
                    w = 1
                    for x in src.shape[1:]:
                        w *= x
                    last = nc.tensor.transpose(b[0:rows, c0:c0 + k], src, ident[0:k, 0:k])
                use.up(last)

            def product(out, w_slot, k0, x_hi, x_lo, c_x, cols, first, last):
                lo, hi = cols
                pairs = ((w_hi[w_slot], x_hi), (w_hi[w_slot], x_lo), (w_lo[w_slot], x_hi))
                for i, (w, x) in enumerate(pairs):
                    ins = nc.tensor.matmul(out, w[:, k0, :], x[:, c_x, lo:hi], start=first and i == 0, stop=last and i == 2)
                return ins

            def project(n, k, x_hi=h_hi, x_lo=h_lo, each=None, kc=DC):
                half, part = divmod(k, 2)
                if k == 0:
                    pe.wait_ge(s_lo, n + 1)
                if part == 0 and n > 0:
                    pe.wait_ge(s_free[half], n)
                for c in range(part * kc // 2, (part + 1) * kc // 2):
                    if each is not None and half == 0:
                        pe.wait_ge(S[each], c + 1)
                    ins = product(pj[half][:, 0:HALF], n % RING, c, x_hi, x_lo, c, HALVES[half], c == 0, c == kc - 1)
                if part == 1:
                    ins.then_inc(s_half[half], 1)

            pe.wait_ge(s_const, 16 * 8)
            pe.wait_ge(s_x, 64)
            for c in range(DC):
                turn([(P, b * P, x_in[:, b, c * P:(c + 1) * P]) for b in range(NB)])
            pe.wait_ge(s_xs, 16)
            for c in range(DC):
                last = nc.tensor.transpose(pv[0][:, c * DEC:(c + 1) * DEC], xs_in[:, c * P:(c + 1) * P], ident[0:DEC, 0:DEC])
            last.then_inc(S["s_xst"], 1)
            pe.wait_ge(S["s_relb"], 4)
            for g in range(BG):
                b = (sc[0], sc[1], pv[1])[g]
                c0, c1 = TABLE_COLS[f"toep{g}"]
                nc.tensor.matmul(b[0:BH, 0:PITCH[g]], relb[:, g * BH:(g + 1) * BH], tables[:, c0:c1], start=True, stop=True).then_inc(S["s_gent"], 1)
            at = 0
            for g in range(BG):
                c0, c1 = TABLE_COLS[f"slots{g}"]
                last = nc.tensor.matmul(pj[0][0:DEC * BH, at:at + c1 - c0], relb_rows[:, g, :, :], tables[:, c0:c1], start=True, stop=True)
                at += c1 - c0
            last.then_inc(S["s_biasm"], 1)
            pe.wait_ge(S["s_accp"], DC)
            pe.wait_ge(S["s_accs"], 1)
            pe.wait_ge(S["s_bias"], 1)
            for half, (lo, hi) in enumerate(HALVES):
                last = nc.tensor.matmul(pj[half][:, 0:HALF], ones, acc[:, lo:hi], start=True, stop=True)
            last.then_inc(S["s_ssum"], 1)
            pe.wait_ge(S["s_wflo"], 1)
            pe.wait_ge(S["s_xsv"], 1)
            pe.wait_ge(S["s_gen"], BG)
            for half, (lo, hi) in enumerate(HALVES):
                for c in range(DC):
                    if half == 0:
                        pe.wait_ge(S["s_hlo"], c + 1)
                    for i, (w, x) in enumerate(((wf_hi, h_hi), (wf_hi, h_lo), (wf_lo, h_hi))):
                        last = nc.tensor.matmul(pv[half][0:AH, 0:HALF], w[:, c, :], x[:, c, lo:hi], start=c == 0 and i == 0, stop=c == DC - 1 and i == 2)
            last.then_inc(S["s_fm"], 1)
            pe.wait_ge(S["s_nv"], 2)

            def scores(r, i):
                hd, qb = units(r)[i]
                u = unit0[r] + i
                s = (r - 1) % 2
                b = sc[u % 2]
                if i == 0:
                    pe.wait_ge(s_free[0], 3 * r)
                    pe.wait_ge(s_free[1], 3 * r)
                    if is_a(r):
                        pe.wait_ge(s_crow[s], 32 * ((r - 1) // 2 + 1))
                if u >= 2:
                    if u - 2 < unit_a:
                        pe.wait_ge(s_ex, u - 1)
                    else:
                        pe.wait_ge(s_mx, u - 1)
                if is_a(r):
                    n = (qb + 1) * P
                    nc.tensor.matmul(b[:, 0:n], q_aug[s][:, hd, qb * P:n], k_aug[s][:, hd, 0:n], start=True, stop=False)
                    last = nc.tensor.matmul(b[:, qb * P:n], identb[:, :], causalb[:, :], start=False, stop=True)
                elif qb is not None:
                    k0 = max(qb - 1, 0) * P
                    n = (qb + 1) * P - k0
                    last = nc.tensor.matmul(b[:, 0:n], q_aug[s][0:HD, hd, qb * P:(qb + 1) * P], k_aug[s][0:HD, hd, k0:k0 + n], start=True, stop=True)
                else:
                    for c in range(CLS):
                        last = nc.tensor.matmul(b[:, c * P:(c + 1) * P], q_aug[s][0:HD, hd, c:SEQ:CLS], k_aug[s][0:HD, hd, c:SEQ:CLS], start=True, stop=True)
                last.then_inc(s_sc, 1)

            def blocks(r, qb):
                return qb + 1 if is_a(r) else CLS if qb is None else min(qb, 1) + 1

            def probs_t(r, i):
                u = unit0[r] + i
                pe.wait_ge(s_ex, u + 1)
                turn([(P, j * P, prob[u % 2][:, j * P:(j + 1) * P]) for j in range(blocks(r, units(r)[i][1]))])

            def values(r, i):
                hd, qb = units(r)[i]
                u = unit0[r] + i
                pe.wait_ge(s_used, pt_use[u] + 1)
                if u >= 2:
                    pe.wait_ge(s_pve, u - 1)
                n = blocks(r, qb)
                first = 0 if is_a(r) or qb is None else max(qb - 1, 0)
                for j in range(n):
                    v = v_tok[:, first + j, hd * HD:(hd + 1) * HD]
                    p = probT[u % 2][:, j * P:(j + 1) * P]
                    if qb is None:
                        last = nc.tensor.matmul(pv[u % 2][:, j * HD:(j + 1) * HD], p, v, start=True, stop=True)
                    else:
                        last = nc.tensor.matmul(pv[u % 2][:, 0:HD], p, v, start=j == 0, stop=j == n - 1)
                last.then_inc(s_pv, 1)

            for r in range(ROUNDS + 1):
                nu = len(units(r))
                for i in range(12):
                    if r and i == 0:
                        pe.wait_ge(s_free[0], 3 * r)
                        pe.wait_ge(s_free[1], 3 * r)
                        turn([(P, b * P, kT[:, b * P:(b + 1) * P]) for b in range(NB)])
                        if r - 1 < ROUNDS_A + 2:
                            turn([(P, b * P, vT[:, b * P:(b + 1) * P]) for b in range(NB)])
                        else:
                            turn([(P, c * P, vT[:, c:SEQ:CLS]) for c in range(CLS)])
                    if i < nu:
                        scores(r, i)
                    project(3 * r + i // 4, i % 4)
                    if r == 0 and i == 5:
                        pe.wait_ge(S["s_logf"], 1)
                        b = tr[use.n % 2]
                        pe.wait_ge(s_used, use.n - 1)
                        for k in range(NB):
                            nc.tensor.transpose(b[:, k * AH:(k + 1) * AH], logf[:, k * P:(k + 1) * P], ident[0:AH, 0:AH])
                        use.up(nc.tensor.transpose(b[0:DEC, NB * AH:(NB + 1) * AH], logf[:, SEQ:T], ident[0:AH, 0:AH]))
                    if 1 <= i <= nu:
                        probs_t(r, i - 1)
                    if 2 <= i <= nu + 1:
                        values(r, i - 2)
                    if i == 10 and r and is_a(r):
                        pe.wait_ge(s_pve, unit0[r] + 8)
                        turn([(P, b * P, o_tok[:, b, :]) for b in range(NB)])

            for n in range(TILE_G + 3, TILE_BR):
                for k in range(4):
                    project(n, k)
                t = n - TILE_G - 3
                if t == 0:
                    assert use.n == USE_COMBINE
                    pe.wait_ge(S["s_comb"], 1)
                    for cc in range(2):
                        turn([(P, c * P, obuf[:, 0, c, cc * P:(cc + 1) * P]) for c in range(CLS)])
                if t == 1:
                    for k in range(8):
                        turn([(DEC, (q - 4 * k) * P, samp[:, q, :]) for q in range(4 * k, min(4 * k + 4, 3 * ROUNDS))])
                if t == 12:
                    sample_rows_t(pe, turn)
                if t == 14:
                    sample_probs_t(pe, turn)
                if t >= 15:
                    for s in range(2 * (t - 15), 2 * (t - 15) + 2):
                        sample_values(pe, s)

            for m in range(DC):
                n = TILE_BR + m
                pe.wait_ge(s_lo, n + 1)
                for half, cols in enumerate(HALVES):
                    pe.wait_ge(s_free[half], n)
                    for c in range(6):
                        if m == 0 and half == 0:
                            pe.wait_ge(S["s_ogl"], c + 1)
                        out = (pj if c < 4 else sc)[half][:, 0:HALF]
                        ins = product(out, n % RING, c, og_hi, og_lo, c, cols, c in (0, 4), c in (3, 5))
                    ins.then_inc(s_half[half], 1)
            pe.wait_ge(S["s_pin"], 32)
            pe.wait_ge(S["s_ov"], 1)
            for c in range(2):
                for b in range(NB):
                    last = nc.tensor.transpose(pv[c][:, b * P:(b + 1) * P], p_in[:, b, c * P:(c + 1) * P], ident)
                last.then_inc(S["s_ptr"], 1)
            turn([(P, c * DEC, ps_in[:, c * P:(c + 1) * P]) for c in range(2)])
            for n in range(TILE_PLE, TILE_OUT):
                for k in range(4):
                    project(n, k, pT_hi, pT_lo, "s_ptl" if n == TILE_PLE else None, 2)
            for n in range(TILE_OUT, TILE_GATE):
                for k in range(4):
                    project(n, k, h_hi, h_lo, "s_ml" if n == TILE_OUT else None)
                if n == TILE_OUT + 1:
                    pe.wait_ge(S["s_ace"], DC)
                    pe.wait_ge(S["s_ov"], 1)
                    pe.wait_ge(S["s_pte"], 2)
                    for half, (lo, hi) in enumerate(HALVES):
                        last = nc.tensor.matmul(pv[half][:, 0:HALF], ones, acc_e[:, lo:hi], start=True, stop=True)
                    last.then_inc(S["s_sse"], 1)
            pe.wait_ge(S["s_acy"], DC)
            pe.wait_ge(S["s_nve"], 2)
            for half, (lo, hi) in enumerate(HALVES):
                last = nc.tensor.matmul(pv[half][:, 0:HALF], ones, acc_y[:, lo:hi], start=True, stop=True)
            last.then_inc(S["s_ssy"], 1)
            def result(m):
                pe.wait_ge(S["s_fin"], m + 1)
                if m >= 2:
                    pe.wait_ge(S["s_tte"], m - 1)
                for b in range(NB):
                    last = nc.tensor.transpose(sc[m % 2][:, b * P:(b + 1) * P], fin[m % 2][:, b * P:(b + 1) * P], ident)
                last.then_inc(S["s_tt"], 1)
                nc.tensor.transpose(pv[m // 4][0:DEC, m % 4 * P:m % 4 * P + P], fin[m % 2][:, SEQ:T], ident).then_inc(S["s_tts"], 1)

            pe.wait_ge(S["s_nvy"], 2)
            for m in range(DC):
                for k in range(4):
                    project(TILE_GATE + m, k, h_hi, h_lo, "s_x2l" if m == 0 else None)
                if m:
                    result(m - 1)
            result(DC - 1)

        @block.scalar
        def _(act):
            own = Tally(s_a)

            def hi_part(n):
                act.wait_ge(s_w[n % RING], landed_at[n])
                if n >= RING:
                    act.wait_ge(s_half[1], n - RING + 1)
                k = chunks(n)
                nc.scalar.activation(w_hi[n % RING][:, 0:k, :], w_raw[n % RING][:, 0:k, :], ACT.Copy).then_inc(s_hi, 1)

            for c in range(DC):
                act.wait_ge(s_used, c + 1)
                if c >= 2:
                    act.wait_ge(S["s_accp"], c - 1)
                nc.scalar.activation(sq[c % 2][:, 0:SEQ], xT[:, c, 0:SEQ], ACT.Square).then_inc(S["s_sq"], 1)
            act.wait_ge(S["s_xsv"], 1)
            nc.scalar.activation(sq_s[:, :, :], xT[:, :, SEQ:T], ACT.Square).then_inc(S["s_sqs"], 1)
            act.wait_ge(s_wf, 16)
            nc.scalar.activation(wf_hi[:, :, :], wf_raw[:, :, :], ACT.Copy).then_inc(S["s_wfhi"], 1)
            hi_part(0)
            act.wait_ge(S["s_nv"], 2)
            own.up(nc.scalar.activation(nt[:, :], nv[:, :], ACT.Ln))
            act.wait_ge(s_a, own.n)
            nc.scalar.activation(rs[:, :], nt[:, :], ACT.Exp, scale=-0.5).then_inc(S["s_y0"], 1)
            for c in range(DC):
                act.wait_ge(S["s_hraw"], c + 1)
                nc.scalar.activation(h_hi[:, c, :], h_raw[c % 2][:, :], ACT.Copy).then_inc(S["s_hhi"], 1)
            hi_part(1)
            hi_part(2)
            act.wait_ge(S["s_fx"], 2)
            own.up(nc.scalar.activation(fa[:, :], fx[:, :], ACT.Abs))
            act.wait_ge(s_a, own.n)
            nc.scalar.activation(fe[:, :], fa[:, :], ACT.Exp, scale=-1.0).then_inc(S["s_fe"], 1)
            act.wait_ge(S["s_fu"], 1)
            nc.scalar.activation(fa[:, :], fu[:, :], ACT.Ln).then_inc(S["s_fl"], 1)

            def evac0(n):
                act.wait_ge(s_half[0], n + 1)
                ps = pj[0]
                if n == 0:
                    act.wait_ge(S["s_clear"], 1)
                if n < TILE_G:
                    r, j = divmod(n, 3)
                    s = r % 2
                    if j == 0:
                        nc.scalar.activation(q_aug[s][0:HD, 0, 0:HALF], ps[0:HD, 0:HALF], ACT.Copy, scale=SCALE)
                        last = nc.scalar.activation(q_aug[s][0:HD, 1, 0:HALF], ps[HD:P, 0:HALF], ACT.Copy, scale=SCALE)
                    elif j == 1:
                        nc.scalar.activation(k_aug[s][0:HD, 0, 0:HALF], ps[0:HD, 0:HALF], ACT.Copy)
                        nc.scalar.activation(k_aug[s][0:HD, 1, 0:HALF], ps[HD:P, 0:HALF], ACT.Copy)
                        last = nc.scalar.activation(kT[:, 0:HALF], ps[:, 0:HALF], ACT.Copy)
                    else:
                        last = nc.scalar.activation(vT[:, 0:HALF], ps[:, 0:HALF], ACT.Copy)
                    last.then_inc(s_free[0], 1)
                elif n < TILE_Z:
                    last = nc.scalar.activation(gsig[:, n - TILE_G, 0:HALF], ps[:, 0:HALF], ACT.Exp, scale=-1.0)
                    last.then_inc(s_free[0], 1)
                else:
                    nc.scalar.activation(zsil[:, n - TILE_Z, 0:HALF], ps[:, 0:HALF], ACT.Exp, scale=-1.0).then_inc(S["s_ge"], 1)

            def evac1(n):
                if n < TILE_G:
                    return
                act.wait_ge(s_half[1], n + 1)
                if n < TILE_Z:
                    nc.scalar.activation(gsig[:, n - TILE_G, HALF:T], pj[1][:, 0:HALF], ACT.Exp, scale=-1.0).then_inc(s_free[1], 1)
                else:
                    nc.scalar.activation(zsil[:, n - TILE_Z, HALF:T], pj[1][:, 0:HALF], ACT.Exp, scale=-1.0).then_inc(S["s_ge"], 1)

            def exps(r, i):
                hd, qb = units(r)[i]
                u = unit0[r] + i
                act.wait_ge(s_mx, u + 1)
                if u >= 2:
                    act.wait_ge(s_use, pt_use[u - 2] + 1)
                if is_a(r):
                    n = (qb + 1) * P
                    if u >= 8:
                        act.wait_ge(s_rc, u - 7)
                    last = nc.scalar.activation(prob[u % 2][:, 0:n], sc[u % 2][:, 0:n], ACT.Exp, bias=nm_a[:, u % 8:u % 8 + 1], accum_out=l_a[:, u % 8:u % 8 + 1])
                else:
                    g, hp = divmod(r - 1 - ROUNDS_A, 2)
                    h = 2 * hp + hd
                    if qb is not None:
                        n = (min(qb, 1) + 1) * P
                        last = nc.scalar.activation(prob[u % 2][:, 0:n], biased[u % 2][:, 0:n], ACT.Exp, bias=nm_b[:, 4 * (u % 2):4 * (u % 2) + 1],
                                                    accum_out=lbuf[:, g, qb, h:h + 1])
                    else:
                        for c in range(CLS):
                            last = nc.scalar.activation(prob[u % 2][:, c * P:(c + 1) * P], biased[u % 2][:, c * P:(c + 1) * P], ACT.Exp,
                                                        bias=nm_b[:, 4 * (u % 2) + c:4 * (u % 2) + c + 1], accum_out=lbuf[:, g, c, h:h + 1])
                last.then_inc(s_ex, 1)

            def values_out(r, i):
                hd, qb = units(r)[i]
                u = unit0[r] + i
                act.wait_ge(s_pv, u + 1)
                if is_a(r):
                    act.wait_ge(s_rc, u + 1)
                    if i == 0 and r > 1:
                        act.wait_ge(s_use, use0[r])
                    last = nc.scalar.activation(o_tok[:, qb, hd * HD:(hd + 1) * HD], pv[u % 2][:, 0:HD], ACT.Copy, scale=r_a[:, u % 8:u % 8 + 1])
                else:
                    g, hp = divmod(r - 1 - ROUNDS_A, 2)
                    h = 2 * hp + hd
                    if qb is not None:
                        last = nc.scalar.activation(obuf[:, g, qb, h * HD:(h + 1) * HD], pv[u % 2][:, 0:HD], ACT.Copy)
                    else:
                        last = nc.scalar.activation(obuf[:, g, :, h * HD:(h + 1) * HD], pv[u % 2][:, 0:CLS * HD].rearrange("p (c d) -> p c d", d=HD), ACT.Copy)
                last.then_inc(s_pve, 1)

            for r in range(ROUNDS + 1):
                nu = len(units(r))
                for i in range(12):
                    n = 3 * r + i // 4
                    if i < nu:
                        exps(r, i)
                    if i % 4 == 1:
                        evac0(n)
                    if 2 <= i <= nu + 1:
                        values_out(r, i - 2)
                    if i % 4 == 3:
                        evac1(n)
                        hi_part(n + RING)

            for n in range(TILE_G + 3, TILE_BR):
                t = n - TILE_G - 3
                if t == 0:
                    act.wait_ge(S["s_md"], 1)
                    nc.scalar.activation(mbuf[:, :, :, :], mbuf[:, :, :, :], ACT.Exp).then_inc(S["s_wexp"], 1)
                evac0(n)
                evac1(n)
                hi_part(n + RING)
                if t == 12:
                    act.wait_ge(S["s_nma"], 1)
                    nc.scalar.activation(row_a[:, :], row_a[:, :], ACT.Exp, bias=sm[:, 5:6], accum_out=sm[:, 6:7]).then_inc(S["s_exa"], 1)
                    act.wait_ge(S["s_nmb"], 1)
                    nc.scalar.activation(row_b[:, :], row_b[:, :], ACT.Exp, bias=sm[0:32, 8:9], accum_out=sm[0:32, 9:10]).then_inc(S["s_exb"], 1)
            for i in range(6):
                act.wait_ge(S["s_ogr"], i + 1)
                nc.scalar.activation(og_hi[:, i, :], og_raw[i % 2][:, :], ACT.Copy).then_inc(S["s_ogh"], 1)
            for m in range(DC):
                act.wait_ge(s_free[0], TILE_BR + m + 1)
                act.wait_ge(s_free[1], TILE_BR + m + 1)
                nc.scalar.activation(h_hi[:, m, :], gsig[:, m, :], ACT.Copy).then_inc(S["s_mh"], 1)
                hi_part(TILE_BR + m + RING)
            for c in range(2):
                if c == 0:
                    act.wait_ge(S["s_pte"], 2)
                    act.wait_ge(s_used, USE_LF + 6)
                nc.scalar.activation(pT_hi[:, c, :], acc_y[:, :] if c else acc_e[:, :], ACT.Copy).then_inc(S["s_pth"], 1)
            for n in range(TILE_PLE, TILE_GATE):
                y = n >= TILE_OUT
                m = (n - TILE_BR) % DC
                dst = yT if y else eT
                act.wait_ge(s_half[0], n + 1)
                nc.scalar.activation(dst[:, m, 0:HALF], pj[0][:, 0:HALF], ACT.Copy).then_inc(s_free[0], 1)
                act.wait_ge(s_free[0], n + 1)
                act.wait_ge(s_free[1], n + 1)
                if m >= 2:
                    act.wait_ge(S["s_acy" if y else "s_ace"], m - 1)
                elif y:
                    act.wait_ge(S["s_ace"], DC)
                nc.scalar.activation(sq2[m % 2][:, :], dst[:, m, :], ACT.Square).then_inc(S["s_sqy" if y else "s_sqe"], 1)
                hi_part(n + RING)
                if n == TILE_OUT + 2:
                    act.wait_ge(S["s_nve"], 2)
                    own.up(nc.scalar.activation(nt2[:, :], nv2[:, :], ACT.Ln))
                    act.wait_ge(s_a, own.n)
                    nc.scalar.activation(rs_e[:, :], nt2[:, :], ACT.Exp, scale=-0.5).then_inc(S["s_y0e"], 1)
            act.wait_ge(S["s_nvy"], 2)
            own.up(nc.scalar.activation(nt2[:, :], nv2[:, :], ACT.Ln))
            act.wait_ge(s_a, own.n)
            nc.scalar.activation(rs_y[:, :], nt2[:, :], ACT.Exp, scale=-0.5).then_inc(S["s_y0y"], 1)
            for c in range(DC):
                act.wait_ge(S["s_x2"], c + 1)
                nc.scalar.activation(h_hi[:, c, :], xT[:, c, :], ACT.Copy).then_inc(S["s_x2h"], 1)
            for m in range(DC):
                n = TILE_GATE + m
                if m >= 2:
                    act.wait_ge(S["s_fin"], m - 1)
                for half, (lo, hi) in enumerate(HALVES):
                    act.wait_ge(s_half[half], n + 1)
                    nc.scalar.activation(sg[m % 2][:, lo:hi], pj[half][:, 0:HALF], ACT.Exp, scale=-1.0).then_inc(s_free[half], 1)
                if n + RING < TILES:
                    hi_part(n + RING)

        @block.vector
        def _(dve):
            own = Tally(s_v)
            used = Tally(s_used)
            V = nc.vector

            def link(ins):
                own.up(ins)
                dve.wait_ge(s_v, own.n)

            def lo_part(n):
                dve.wait_ge(s_hi, n + 1)
                k = chunks(n)
                V.tensor_tensor(w_lo[n % RING][:, 0:k, :], w_raw[n % RING][:, 0:k, :], w_hi[n % RING][:, 0:k, :].bitcast(F32), ALU.subtract).then_inc(s_lo, 1)

            def out_of_turn(*moves):
                dve.wait_ge(s_use, used.n + 1)
                b = tr[used.n % 2]
                for dst, src in moves:
                    last = V.tensor_copy(dst, src(b))
                used.up(last)

            def rsqrt(y, v, t, done):
                link(V.tensor_tensor(t, y, y, ALU.mult))
                link(V.tensor_tensor(t, t, v, ALU.mult))
                link(V.tensor_scalar(t, t, -0.5, 1.5, ALU.mult, ALU.add))
                V.tensor_tensor(y, y, t, ALU.mult).then_inc(done, 1)

            dve.wait_ge(s_const, 16 * 8)
            V.tensor_copy(identb[:, :], ident).then_inc(S["s_relb"], 1)
            V.tensor_copy(causalb[:, :], cst("causal")).then_inc(S["s_relb"], 1)
            V.memset(relb[32:33, :], NEG).then_inc(S["s_relb"], 1)
            dve.wait_ge(S["s_relb"], 3)
            for g in range(BG):
                last = V.tensor_copy(relb_rows[:, g, :, :], relb[:, g * BH:(g + 1) * BH].unsqueeze(1).to_broadcast([33, DEC, BH]))
            last.then_inc(S["s_relb"], 1)
            for c in range(DC):
                out_of_turn((xT[:, c, 0:SEQ], lambda b: b[:, 0:SEQ]))
            dve.wait_ge(S["s_xst"], 1)
            V.tensor_copy(xT[:, :, SEQ:T], pv[0][:, 0:DC * DEC].rearrange("p (c s) -> p c s", s=DEC)).then_inc(S["s_xsv"], 1)
            dve.wait_ge(S["s_sqs"], 1)
            V.tensor_reduce(acc[:, SEQ:T], sq_s[:, :, :].rearrange("p c s -> p s c"), AX.X, ALU.add).then_inc(S["s_accs"], 1)
            for g in range(BG):
                dve.wait_ge(S["s_gent"], g + 1)
                V.tensor_copy(gen[g][:, :], (sc[0], sc[1], pv[1])[g][0:BH, 0:PITCH[g]]).then_inc(S["s_gen"], 1)
            dve.wait_ge(S["s_biasm"], 1)
            V.tensor_copy(bias_s[:, :], pj[0][0:DEC * BH, 0:sum(SLOTS) + BG]).then_inc(S["s_bias"], 1)
            dve.wait_ge(S["s_wfhi"], 1)
            V.tensor_tensor(wf_lo[:, :, :], wf_raw[:, :, :], wf_hi[:, :, :].bitcast(F32), ALU.subtract).then_inc(S["s_wflo"], 1)
            lo_part(0)
            dve.wait_ge(S["s_ssum"], 1)
            for half, (lo, hi) in enumerate(HALVES):
                V.tensor_scalar(nv[:, lo:hi], pj[half][:, 0:HALF], 1.0 / D, EPS, ALU.mult, ALU.add).then_inc(S["s_nv"], 1)
            dve.wait_ge(S["s_y0"], 1)
            rsqrt(rs[:, :], nv[:, :], nt[:, :], S["s_rs"])
            dve.wait_ge(S["s_rs"], 1)
            for c in range(DC):
                if c >= 2:
                    dve.wait_ge(S["s_hlo"], c - 1)
                V.scalar_tensor_tensor(h_raw[c % 2][:, :], xT[:, c, :], gpre[:, c:c + 1], rs[:, :], ALU.mult, ALU.mult).then_inc(S["s_hraw"], 1)
            lo_part(1)
            lo_part(2)
            dve.wait_ge(S["s_fm"], 1)
            for half, (lo, hi) in enumerate(HALVES):
                V.tensor_scalar(fx[:, lo:hi], pv[half][0:AH, 0:HALF], bf[:, 0:1], None, ALU.add).then_inc(S["s_fx"], 1)
            dve.wait_ge(S["s_fe"], 1)
            V.tensor_scalar(fu[:, :], fe[:, :], 1.0, None, ALU.add).then_inc(S["s_fu"], 1)
            dve.wait_ge(S["s_fu"], 1)
            link(V.tensor_scalar(fd[:, :], fu[:, :], -1.0, None, ALU.add))
            link(V.tensor_tensor(fd[:, :], fe[:, :], fd[:, :], ALU.subtract))
            link(V.reciprocal(fr[:, :], fu[:, :]))
            link(V.tensor_tensor(fd[:, :], fd[:, :], fr[:, :], ALU.mult))
            dve.wait_ge(S["s_fl"], 1)
            link(V.tensor_tensor(fd[:, :], fa[:, :], fd[:, :], ALU.add))
            V.scalar_tensor_tensor(logf[:, :], fx[:, :], 0.0, fd[:, :], ALU.min, ALU.subtract).then_inc(S["s_logf"], 1)
            dve.wait_ge(S["s_logf"], 1)
            V.tensor_tensor_scan(cum[:, :], ones[0:AH, 0:1].to_broadcast([AH, SEQ]), logf[:, 0:SEQ], 0.0, ALU.mult, ALU.add).then_inc(S["s_cum"], 1)
            dve.wait_ge(S["s_cum"], 1)
            V.tensor_scalar(ncum[:, :], cum[:, :], -1.0, None, ALU.mult).then_inc(S["s_cum"], 1)
            dve.wait_ge(S["s_hlo"], DC)
            dve.wait_ge(S["s_gend"], 16 * BG * BH)
            for buf in (*q_aug, *k_aug):
                last = V.memset(buf[HD:HD + 2, :, :], 1.0)
            last.then_inc(S["s_clear"], 1)

            def evac1(n):
                dve.wait_ge(s_half[1], n + 1)
                r, j = divmod(n, 3)
                s = r % 2
                ps = pj[1]
                V.tensor_scalar(samp[:, n, :], ps[:, HALF - DEC:HALF], SCALE if j == 0 else 1.0, None, ALU.mult)
                if j == 0:
                    for hd in range(2):
                        last = V.tensor_scalar(q_aug[s][0:HD, hd, HALF:T], ps[hd * HD:(hd + 1) * HD, 0:HALF], SCALE, None, ALU.mult)
                elif j == 1:
                    for hd in range(2):
                        V.tensor_copy(k_aug[s][0:HD, hd, HALF:T], ps[hd * HD:(hd + 1) * HD, 0:HALF])
                    last = V.tensor_copy(kT[:, HALF:T], ps[:, 0:HALF])
                else:
                    last = V.tensor_copy(vT[:, HALF:T], ps[:, 0:HALF])
                last.then_inc(s_free[1], 1)

            n_ge = [0]

            def sigmoid(n):
                g = n < TILE_Z
                buf = gsig[:, n - TILE_G, :] if g else zsil[:, n - TILE_Z, :]
                if g:
                    dve.wait_ge(s_free[0], n + 1)
                    dve.wait_ge(s_free[1], n + 1)
                else:
                    dve.wait_ge(S["s_ge"], 2 * (n - TILE_Z) + 2)
                link(V.tensor_scalar(buf, buf, 1.0, None, ALU.add))
                if g:
                    V.reciprocal(buf, buf).then_inc(S["s_gs"], 1)
                else:
                    link(V.reciprocal(buf, buf))
                    for half, (lo, hi) in enumerate(HALVES):
                        V.tensor_tensor(buf[:, lo:hi], buf[:, lo:hi], pj[half][:, 0:HALF], ALU.mult).then_inc(s_free[half], 1)

            def maxima(r, i):
                hd, qb = units(r)[i]
                u = unit0[r] + i
                dve.wait_ge(s_sc, u + 1)
                if is_a(r):
                    if u >= 8:
                        dve.wait_ge(s_ex, u - 7)
                    V.tensor_reduce(nm_a[:, u % 8:u % 8 + 1], sc[u % 2][:, 0:(qb + 1) * P], AX.X, ALU.max, negate=True).then_inc(s_mx, 1)
                    return
                g, hp = divmod(r - 1 - ROUNDS_A, 2)
                h = 2 * hp + hd
                dve.wait_ge(s_ex, u - 1)
                if u == unit_a:
                    dve.wait_ge(s_use, use0[r])
                    dve.wait_ge(S["s_toep"], 16 * BG * BH)
                if qb is not None:
                    n = (min(qb, 1) + 1) * P
                    link(V.tensor_tensor_reduce(out=biased[u % 2][:, 0:n], in0=sc[u % 2][:, 0:n], in1=toep[0][:, h, 2 * P - n:2 * P], scale=1.0, scalar=-3e38,
                                                op0=ALU.add, op1=ALU.max, accum_out=mbuf[:, g, qb, h:h + 1]))
                    V.tensor_scalar(nm_b[:, 4 * (u % 2):4 * (u % 2) + 1], mbuf[:, g, qb, h:h + 1], -1.0, None, ALU.mult).then_inc(s_mx, 1)
                else:
                    for c in range(CLS):
                        cols = slice(c * P, (c + 1) * P)
                        ins = V.tensor_tensor_reduce(out=biased[u % 2][:, cols], in0=sc[u % 2][:, cols], in1=toep[g][:, h, :], scale=1.0, scalar=-3e38,
                                                     op0=ALU.add, op1=ALU.max, accum_out=mbuf[:, g, c, h:h + 1])
                    link(ins)
                    V.tensor_scalar(nm_b[:, 4 * (u % 2):4 * (u % 2) + 4], mbuf[:, g, :, h], -1.0, None, ALU.mult).then_inc(s_mx, 1)

            def probs_out(r, i):
                u = unit0[r] + i
                qb = units(r)[i][1]
                n = (qb + 1 if is_a(r) else CLS if qb is None else min(qb, 1) + 1) * P
                if u >= 2:
                    dve.wait_ge(s_pv, u - 1)
                out_of_turn((probT[u % 2][:, 0:n], lambda b: b[:, 0:n]))

            for r in range(ROUNDS + 1):
                nu = len(units(r))
                t = r - 1
                for i in range(12):
                    n = 3 * r + i // 4
                    if r and i == 0:
                        if r >= 2:
                            dve.wait_ge(s_kst, 16 * (r - 1))
                        out_of_turn((k_tok[:, :, :].rearrange("p b c -> p (b c)"), lambda b: b[:, :]))
                        if r >= 2:
                            dve.wait_ge(s_vst, 16 * (r - 1))
                            dve.wait_ge(s_pv, unit0[r])
                        out_of_turn((v_tok[:, :, :].rearrange("p b c -> p (b c)"), lambda b: b[:, :]))
                    if i < nu:
                        maxima(r, i)
                    if is_a(r) and 1 <= i <= nu:
                        u = unit0[r] + i - 1
                        dve.wait_ge(s_ex, u + 1)
                        if u >= 8:
                            dve.wait_ge(s_pve, u - 7)
                        V.reciprocal(r_a[:, u % 8:u % 8 + 1], l_a[:, u % 8:u % 8 + 1]).then_inc(s_rc, 1)
                    if r == 0 and i == 5:
                        dve.wait_ge(s_use, used.n + 1)
                        b = tr[used.n % 2]
                        V.tensor_copy(lf_small[:, 0:NB, :].rearrange("p b h -> p (b h)"), b[:, 0:NB * AH])
                        used.up(V.tensor_copy(lf_small[0:DEC, NB, :], b[0:DEC, NB * AH:(NB + 1) * AH]))
                    if 1 <= i <= nu:
                        probs_out(r, i - 1)
                    if i % 4 == 3:
                        if n < TILE_G:
                            evac1(n)
                        lo_part(n + RING)
                        if n >= TILE_G:
                            sigmoid(n)
                    if i == 10 and r and is_a(r):
                        out_of_turn((oaT[:, t, 0:SEQ], lambda b: b[:, :]))

            def combine():
                dve.wait_ge(S["s_o0r"], 48)
                dve.wait_ge(s_ex, UNITS)
                flat = lambda b, g: b[:, g, :, :].rearrange("p c h -> p (c h)")
                mm, den = top_m, den_m
                link(V.tensor_tensor(mm[:, :], flat(mbuf, 0), flat(mbuf, 1), ALU.max))
                link(V.tensor_tensor(mm[:, :], mm[:, :], flat(mbuf, 2), ALU.max))
                V.tensor_tensor(mbuf[:, :, :, :].rearrange("p g c h -> p g (c h)"), mbuf[:, :, :, :].rearrange("p g c h -> p g (c h)"),
                                mm[:, :].unsqueeze(1).to_broadcast([P, BG, CLS * BH]), ALU.subtract).then_inc(S["s_md"], 1)
                dve.wait_ge(S["s_wexp"], 1)
                allg = lambda b: b[:, :, :, :].rearrange("p g c h -> p (g c h)")
                link(V.tensor_tensor(allg(lbuf), allg(lbuf), allg(mbuf), ALU.mult))
                link(V.tensor_reduce(den[:, :], lbuf[:, :, :, :].rearrange("p g c h -> p (c h) g"), AX.X, ALU.add))
                link(V.reciprocal(den[:, :], den[:, :]))
                link(V.tensor_tensor(mbuf[:, :, :, :].rearrange("p g c h -> p g (c h)"), mbuf[:, :, :, :].rearrange("p g c h -> p g (c h)"),
                                     den[:, :].unsqueeze(1).to_broadcast([P, BG, CLS * BH]), ALU.mult))
                dve.wait_ge(s_pve, UNITS)
                for g in range(BG):
                    o = obuf[:, g, :, :].rearrange("p c (h d) -> p (c h) d", d=HD)
                    link(V.tensor_tensor(o, o, flat(mbuf, g).unsqueeze(2).to_broadcast([P, CLS * BH, HD]), ALU.mult))
                fo = lambda g: obuf[:, g, :, :].rearrange("p c n -> p (c n)")
                link(V.tensor_tensor(fo(0), fo(0), fo(1), ALU.add))
                V.tensor_tensor(fo(0), fo(0), fo(2), ALU.add).then_inc(S["s_comb"], 1)

            red = [0]

            def sample_logits(s):
                for i in range(PAGES + BG):
                    k = red[0]
                    dve.wait_ge(S["s_prod"], k + 1)
                    if i < PAGES:
                        src, dst = prod[k % 2][:, :].rearrange("p (h d) -> p h d", d=HD), lg_a[:, i, s, :]
                    else:
                        n = SLOTS[i - PAGES]
                        src, dst = prod[k % 2][0:n, 0:BO].rearrange("p (h d) -> p h d", d=HD), lg_b[0:n, i - PAGES, s, :]
                    V.tensor_reduce(dst, src, AX.X, ALU.add).then_inc(S["s_red"], 1)
                    red[0] += 1

            def sample_softmax():
                out_of_turn((lfT[:, :, :, :].rearrange("p g s h -> p h s g"), lambda b: b[:, 0:256].rearrange("p (h s g) -> p h s g", h=AH, g=PAGES)))
                dve.wait_ge(S["s_suf"], 1)
                dve.wait_ge(S["s_red"], 7 * DEC)
                la = lg_a[:, :, :, :].rearrange("p g s h -> p (g s h)")
                V.tensor_tensor(la, la, sc[0][:, 0:256], ALU.add).then_inc(S["s_lga"], 1)
                dve.wait_ge(S["s_selfr"], 48)
                dve.wait_ge(s_use, used.n + 1)
                used.up(V.tensor_scalar(row_a[:, 0:PAST], tr[used.n % 2][0:DEC * AH, :], sm[:, 0:1], None, ALU.add))
                dve.wait_ge(s_used, used.n)
                V.tensor_reduce(sm[:, 5:6], row_a[:, :], AX.X, ALU.max, negate=True).then_inc(S["s_nma"], 1)
                dve.wait_ge(s_use, used.n + 1)
                b, at = tr[used.n % 2], 0
                for g in range(BG):
                    to = at + SLOTS[g]
                    V.tensor_tensor(row_b[:, to:to + 1], sm[0:32, 1 + g:2 + g], bias_s[:, to:to + 1], ALU.add)
                    last = V.tensor_tensor(row_b[:, at:to], b[0:32, at:to], bias_s[:, at:to], ALU.add)
                    at = to + 1
                used.up(last)
                dve.wait_ge(s_used, used.n)
                V.tensor_reduce(sm[0:32, 8:9], row_b[:, :], AX.X, ALU.max, negate=True).then_inc(S["s_nmb"], 1)
                dve.wait_ge(S["s_exa"], 1)
                link(V.reciprocal(sm[:, 7:8], sm[:, 6:7]))
                V.tensor_scalar(row_a[:, :], row_a[:, :], sm[:, 7:8], None, ALU.mult).then_inc(S["s_pn"], 1)
                dve.wait_ge(S["s_exb"], 1)
                link(V.reciprocal(sm[0:32, 10:11], sm[0:32, 9:10]))
                V.tensor_scalar(row_b[:, :], row_b[:, :], sm[0:32, 10:11], None, ALU.mult).then_inc(S["s_pn"], 1)
                dve.wait_ge(S["s_pn"], 2)
                V.tensor_scalar(dsel_a[:, :], cst("row_a", 64), row_a[:, PAST:PAST + 1], None, ALU.mult).then_inc(S["s_ds"], 1)
                at = 0
                for g in range(BG):
                    at += SLOTS[g]
                    V.tensor_scalar(dsel_b[:, g, :], cst("row_b", 32), row_b[:, at:at + 1], None, ALU.mult).then_inc(S["s_ds"], 1)
                    at += 1

            def sample_selves():
                out_of_turn((pTa[:, :, :, :].rearrange("p g s h -> p (g s h)"), lambda b: b[:, 0:256]))
                out_of_turn((pTb[:, 0:2, :, :].rearrange("p g s h -> p (g s h)"), lambda b: b[:, 0:64]),
                            (pTb[0:32, 2, :, :].rearrange("p s h -> p (s h)"), lambda b: b[0:32, 64:96]))
                dve.wait_ge(S["s_dm"], 1)
                V.tensor_copy(d_a[:, :], pv[0][0:DEC, 0:64]).then_inc(S["s_dv"], 1)
                V.tensor_copy(d_b[:, :, :].rearrange("s g x -> s (g x)"), pv[0][0:DEC, 64:160]).then_inc(S["s_dv"], 1)
                dve.wait_ge(S["s_slf"], 1)
                V.tensor_copy(os_a[:, :], pv[1][:, 0:256])
                link(V.tensor_copy(os_b[:, :], pv[1][:, 256:320]))

            def result_out(m):
                dve.wait_ge(S["s_tt"], m + 1)
                if m >= 2:
                    dve.wait_ge(S[f"s_yst{m % 2}"], 16 * (m // 2))
                V.tensor_copy(tok_out[m % 2][:, :, :].rearrange("p b c -> p (b c)"), sc[m % 2][:, :]).then_inc(S["s_tte"], 1)

            for n in range(TILE_G + 3, TILE_BR):
                t = n - TILE_G - 3
                if t == 0:
                    combine()
                if n < TILE_Z:
                    dve.wait_ge(s_half[1], n + 1)
                sigmoid(n)
                lo_part(n + RING)
                if t == 0:
                    for cc in range(2):
                        out_of_turn((obT[:, cc, 0:SEQ].rearrange("p (i c) -> p c i", c=CLS), lambda b: b[:, :].rearrange("p (c i) -> p c i", c=CLS)))
                if t == 1:
                    dve.wait_ge(s_kst, 16 * ROUNDS)
                    dve.wait_ge(s_vst, 16 * ROUNDS)
                    for k in range(8):
                        w = min(4, 3 * ROUNDS - 4 * k)
                        out_of_turn((st[:, 4 * k:4 * k + w, :].rearrange("p r c -> p (r c)"), lambda b: b[0:DEC, 0:w * P]))
                    dve.wait_ge(s_used, used.n)
                    stv = st[:, :, :].rearrange("s (r j) c -> s j r c", j=3)
                    link(V.tensor_tensor(self_p[:, :, :], stv[:, 0], stv[:, 1], ALU.mult))
                    heads = self_p[:, :, :].rearrange("s r (h d) -> s (r h) d", d=HD)
                    link(V.tensor_reduce(self_a[:, :], heads[:, 0:AH], AX.X, ALU.add))
                    for g in range(BG):
                        ins = V.tensor_reduce(self_b[:, :, g], heads[:, AH + BH * g:AH + BH * (g + 1)], AX.X, ALU.add)
                    ins.then_inc(S["s_selfp"], 1)
                if 3 <= t < 3 + DEC:
                    sample_logits(t - 3)
                if t == 12:
                    sample_softmax()
                if t == 14:
                    sample_selves()

            dve.wait_ge(S["s_samp"], DEC)
            for cc in range(AW // P):
                for hf in range(2):
                    rows = slice(hf * HD, (hf + 1) * HD)
                    pick = lambda b: b[rows, cc * 64:(cc + 1) * 64].rearrange("p (s h) -> p h s", h=AH)[:, 2 * cc + hf, :]
                    V.tensor_tensor(oaT[rows, cc, SEQ:T], pick(sc[0]), pick(os_a), ALU.add)
            for cc in range(BO // P):
                for hf in range(2):
                    rows = slice(hf * HD, (hf + 1) * HD)
                    pick = lambda b: b[rows, cc * 32:(cc + 1) * 32].rearrange("p (s h) -> p h s", h=BH)[:, 2 * cc + hf, :]
                    last = V.tensor_tensor(obT[rows, cc, SEQ:T], pick(sc[1]), pick(os_b), ALU.add)
            last.then_inc(S["s_ov"], 1)
            dve.wait_ge(S["s_ov"], 1)
            for i in range(6):
                if i >= 2:
                    dve.wait_ge(S["s_ogl"], i - 1)
                dve.wait_ge(s_free[1], TILE_BR)
                src = oaT[:, i, :] if i < 4 else obT[:, i - 4, :]
                ins = V.tensor_tensor(og_raw[i % 2][:, :], src, zsil[:, i, :], ALU.mult)
                ins.then_inc(S["s_ogr"], 1)
            for m in range(DC):
                n = TILE_BR + m
                for half, (lo, hi) in enumerate(HALVES):
                    dve.wait_ge(s_half[half], n + 1)
                    a, b = gsig[:, m, lo:hi], gsig[:, DC + m, lo:hi]
                    V.tensor_tensor(a, a, pj[half][:, 0:HALF], ALU.mult)
                    own.up(V.tensor_tensor(b, b, sc[half][:, 0:HALF], ALU.mult))
                    dve.wait_ge(s_v, own.n)
                    last = V.tensor_tensor(a, a, b, ALU.add)
                    last.then_inc(s_free[half], 1)
                lo_part(n + RING)
            dve.wait_ge(S["s_ptr"], 2)
            dve.wait_ge(s_use, used.n + 1)
            V.tensor_copy(acc_e[:, 0:SEQ], pv[0][:, :]).then_inc(S["s_pte"], 1)
            V.tensor_copy(acc_y[:, 0:SEQ], pv[1][:, :]).then_inc(S["s_pte"], 1)
            b = tr[used.n % 2]
            V.tensor_copy(acc_e[:, SEQ:T], b[:, 0:DEC])
            used.up(V.tensor_copy(acc_y[:, SEQ:T], b[:, DEC:2 * DEC]))
            for c, src in enumerate((acc_e, acc_y)):
                dve.wait_ge(S["s_pth"], c + 1)
                V.tensor_tensor(pT_lo[:, c, :], src[:, :], pT_hi[:, c, :].bitcast(F32), ALU.subtract).then_inc(S["s_ptl"], 1)
            for n in range(TILE_PLE, TILE_GATE):
                y = n >= TILE_OUT
                m = (n - TILE_BR) % DC
                dve.wait_ge(s_half[1], n + 1)
                V.tensor_copy((yT if y else eT)[:, m, HALF:T], pj[1][:, 0:HALF]).then_inc(s_free[1], 1)
                lo_part(n + RING)
                if n == TILE_OUT + 2:
                    dve.wait_ge(S["s_sse"], 1)
                    for half, (lo, hi) in enumerate(HALVES):
                        V.tensor_scalar(nv2[:, lo:hi], pv[half][:, 0:HALF], 1.0 / D, EPS, ALU.mult, ALU.add).then_inc(S["s_nve"], 1)
                    dve.wait_ge(S["s_y0e"], 1)
                    rsqrt(rs_e[:, :], nv2[:, :], nt2[:, :], S["s_rse"])
                    dve.wait_ge(S["s_rse"], 1)
                if n >= TILE_OUT + 3 and n < TILE_OUT + 7:
                    for c in range(2 * (n - TILE_OUT - 3), 2 * (n - TILE_OUT - 3) + 2):
                        V.scalar_tensor_tensor(eT[:, c, :], eT[:, c, :], gple[:, c:c + 1], rs_e[:, :], ALU.mult, ALU.mult).then_inc(S["s_en"], 1)
            dve.wait_ge(S["s_ssy"], 1)
            for half, (lo, hi) in enumerate(HALVES):
                V.tensor_scalar(nv2[:, lo:hi], pv[half][:, 0:HALF], 1.0 / D, EPS, ALU.mult, ALU.add).then_inc(S["s_nvy"], 1)
            dve.wait_ge(S["s_y0y"], 1)
            rsqrt(rs_y[:, :], nv2[:, :], nt2[:, :], S["s_rsy"])
            dve.wait_ge(S["s_rsy"], 1)
            for c in range(DC):
                link(V.scalar_tensor_tensor(yT[:, c, :], yT[:, c, :], gpost[:, c:c + 1], rs_y[:, :], ALU.mult, ALU.mult))
                V.tensor_tensor(xT[:, c, :], xT[:, c, :], yT[:, c, :], ALU.add).then_inc(S["s_x2"], 1)
            for m in range(DC):
                n = TILE_GATE + m
                dve.wait_ge(s_free[0], n + 1)
                dve.wait_ge(s_free[1], n + 1)
                buf = sg[m % 2][:, :]
                link(V.tensor_scalar(buf, buf, 1.0, None, ALU.add))
                link(V.reciprocal(buf, buf))
                dve.wait_ge(S["s_en"], m + 1)
                link(V.tensor_tensor(buf, buf, eT[:, m, :], ALU.mult))
                if m >= 2:
                    dve.wait_ge(S["s_tts"], m - 1)
                    dve.wait_ge(S["s_tt"], m - 1)
                V.tensor_tensor(fin[m % 2][:, :], xT[:, m, :], buf, ALU.add).then_inc(S["s_fin"], 1)
                if n + RING < TILES:
                    lo_part(n + RING)
                if m:
                    result_out(m - 1)
            result_out(DC - 1)
            dve.wait_ge(S["s_tts"], DC)
            for i in range(2):
                V.tensor_copy(toks_out[:, 512 * i:512 * (i + 1)], pv[i][0:DEC, :]).then_inc(S["s_ttse"], 1)


_INS = ["x_prompt", "x_sample", "cache_a_kv", "cache_a_logf", "cache_b0_kv", "cache_b1_kv", "cache_b2_kv", "page_table",
        "p_prompt", "p_sample", "rel_bias", "g_pre", "w_in", "b_f", "w_br_a", "w_br_b", "w_out", "g_post", "w_ple", "g_ple", "w_ple_gate"]
_OUTS = [(1, SEQ, D), (DEC, 1, D), (1, 1, SEQ, 2, AH, HD), (1, 1, SEQ, AH),
         (1, 1, 128, 2, BH, HD), (1, 1, SEQ, 2, BH, HD), (1, 1, SEQ, 2, BH, HD),
         (1, DEC, 1, 2, AH, HD), (1, DEC, 1, AH),
         (1, DEC, 128, 2, BH, HD), (1, DEC, PAST, 2, BH, HD), (1, DEC, PAST, 2, BH, HD)]


def kernel(**inputs):
    import concourse.bacc as _bacc
    from concourse.bass_utils import run_bass_kernel_spmd as _run

    nc = _bacc.Bacc("TRN2", target_bir_lowering=False, num_devices=1)
    arrays, args = {}, {}
    for name in _INS:
        a = np.ascontiguousarray(inputs[name])
        arrays[f"in_{name}_dram"] = a
        args[name] = nc.dram_tensor(f"in_{name}_dram", a.shape, mybir.dt.from_np(a.dtype), kind="ExternalInput").ap()
    consts = []
    for name, a in (("const", CONST), ("tables", TABLES)):
        arrays[f"in_{name}_dram"] = a
        consts.append(nc.dram_tensor(f"in_{name}_dram", a.shape, F32, kind="ExternalInput").ap())
    outs = [nc.dram_tensor(f"out_{i}_dram", shape, F32, kind="ExternalOutput").ap() for i, shape in enumerate(_OUTS)]
    build(nc, args, outs, consts)
    r = _run(nc, [arrays], core_ids=[0])
    return tuple(r.results[0][f"out_{i}_dram"] for i in range(len(_OUTS)))
```

```python
from contextlib import ExitStack

import numpy as np

import concourse.bass as bass
from concourse import mybir

F32 = mybir.dt.float32
F32R = mybir.dt.float32r
BF16 = mybir.dt.bfloat16
I32 = mybir.dt.int32
ALU = mybir.AluOpType
ACT = mybir.ActivationFunctionType
AX = mybir.AxisListType

P = 128
D = 1024
DC = D // P
SEQ = 512
NB = SEQ // P
DEC = 8
T = SEQ + DEC
HALF = T // 2
HALVES = ((0, HALF), (HALF, T))
HD = 64
AH = 8
AW = AH * HD
BG, BH = 3, 4
DIL = (1, 4, 16)
WIN = (128, 512, 2048)
BQ = BG * BH * HD
BO = BH * HD
PLE = 256
PAGES, PAGE = 4, 128
PAST = PAGES * PAGE
POOL_PAGES = 40
CLS = 4
SCALE = HD ** -0.5
EPS = 1e-6
NEG = -1e30

COL_QA, COL_KA, COL_VA = 0, AW, 2 * AW
COL_F = 3 * AW
COL_ZA = COL_F + AH
COL_QB = COL_ZA + AW
COL_KB, COL_VB = COL_QB + BQ, COL_QB + 2 * BQ
COL_ZB = COL_QB + 3 * BQ
COL_GA = COL_ZB + BO
IN_W = COL_GA + 2 * D

RING = 3
ROUNDS_A, ROUNDS_B = AH // 2, BG * BH // 2
ROUNDS = ROUNDS_A + ROUNDS_B
N_G, N_Z = 16, 6
TILE_G = 3 * ROUNDS
TILE_Z = TILE_G + N_G
TILE_BR = TILE_Z + N_Z
TILE_OUT = TILE_BR + DC
TILE_PLE = TILE_OUT + DC
TILE_GATE = TILE_PLE + DC
TILES = TILE_GATE + DC

TOEP = (256, 128, 128)
PITCH = (384, 256, 256)
SLOTS = (128, 128, 32)


def bucket(dist):
    d = np.maximum(dist, 1).astype(np.float32)
    large = 16 + (np.log(d / np.float32(16)) / np.float32(np.log(2048 / 16)) * np.float32(16)).astype(np.int32)
    return np.where(dist < 16, dist, np.minimum(large, 31))


CONST_COLS = {}
TABLE_COLS = {}
EARLY_COLS = {}


def constants():
    parts, tables, early = [], [], []

    def add(name, m, to=parts, cols=CONST_COLS):
        full = np.zeros((33 if to is tables else P, m.shape[1]), np.float32)
        full[:m.shape[0]] = m
        at = sum(x.shape[1] for x in to)
        cols[name] = (at, at + m.shape[1])
        to.append(full)

    i = np.arange(P)
    add("ident", np.eye(P))
    add("ones", np.ones((P, P)))
    add("later", (i[:, None] > i[None, :]) * 1.0, early, EARLY_COLS)
    add("causal", np.where(i[None, :] <= i[:, None], 0.0, NEG), early, EARLY_COLS)
    add("row_a", (np.arange(64)[:, None] // AH == np.arange(DEC)) * 1.0)
    add("row_b", (np.arange(32)[:, None] // BH == np.arange(DEC)) * 1.0)
    add("head_a", (np.arange(64)[:, None] % AH == np.arange(AH)) * 1.0)
    add("head_b", (np.arange(32)[:, None] % BH == np.arange(BH)) * 1.0)
    for g in range(BG):
        y = np.arange(PITCH[g])
        dist = 255 - y if g == 0 else (127 - y) * CLS
        seen = (dist >= 0) & (dist <= WIN[g]) & (dist % DIL[g] == 0)
        hot = np.zeros((33, PITCH[g]))
        hot[np.where(seen, bucket(np.maximum(dist, 0)), 32), y] = 1
        add(f"toep{g}", hot, tables, TABLE_COLS)
    for g in range(BG):
        n = SLOTS[g]
        dist = np.concatenate([(n - np.arange(n)) * DIL[g], [0]])
        hot = np.zeros((33, n + 1))
        hot[bucket(dist), np.arange(n + 1)] = 1
        add(f"slots{g}", hot, tables, TABLE_COLS)
    return tuple(np.concatenate(x, axis=1) for x in (parts, tables, early))


CONST, TABLES, EARLY = constants()


class Tally:

    def __init__(self, sem):
        self.sem, self.n = sem, 0

    def up(self, ins):
        ins.then_inc(self.sem, 1)
        self.n = self.n + 1
        return ins


def build(nc, A, O, const_in):
    with ExitStack() as ctx:
        cursor = [nc.sbuf_base + 31 & ~31]
        top = [cursor[0]]

        def sb(name, shape, dt=F32, at=None):
            size = int(np.prod(shape[1:])) * (2 if dt == BF16 else 4)
            size = size + 31 & ~31
            if at is not None:
                cursor[0] = at
            t = nc.alloc_sbuf_tensor_at(name, shape, dt, offset=cursor[0])
            cursor[0] += size
            top[0] = max(top[0], cursor[0])
            return t

        def bank(name):
            return ctx.enter_context(nc.psum_tensor(name, [P, 512], F32))

        def sem(name):
            return ctx.enter_context(nc.semaphore(name))

        def sems(name, n):
            return [sem(f"{name}{i}") for i in range(n)]

        pj = [bank("pj0"), bank("pj1")]
        sc = [bank("sc0"), bank("sc1")]
        tr = [bank("tr0"), bank("tr1")]
        pv = [bank("pv0"), bank("pv1")]

        const = sb("const", [P, CONST.shape[1]])
        cst = lambda name, rows=P: const[0:rows, CONST_COLS[name][0]:CONST_COLS[name][1]]
        ident, ones = cst("ident"), cst("ones")
        identb = sb("identb", [P, P], BF16)
        causalb = sb("causalb", [P, P], BF16)
        g_all = sb("g_all", [P, 3 * DC])
        gpre, gpost, gple = (g_all[:, i * DC:(i + 1) * DC] for i in range(3))
        xT = sb("xT", [P, DC, T])
        h_hi, h_lo = sb("h_hi", [P, DC, T], F32R), sb("h_lo", [P, DC, T], F32R)
        w_raw = [sb(f"w_raw{i}", [P, DC, P]) for i in range(RING)]
        w_hi = [sb(f"w_hi{i}", [P, DC, P], F32R) for i in range(RING)]
        w_lo = [sb(f"w_lo{i}", [P, DC, P], F32R) for i in range(RING)]
        samp = sb("samp", [P, 3 * ROUNDS, DEC])
        lg_a = sb("lg_a", [P, PAGES, DEC, AH])
        lg_b = sb("lg_b", [P, BG, DEC, BH])
        later = sb("later_sums", [P, PAGES * DEC * AH])
        lf_small = sb("lf_small", [P, NB + 1, AH])
        oaT, obT = sb("oaT", [P, AW // P, T]), sb("obT", [P, BO // P, T])
        zsil = sb("zsil", [P, N_Z, T])
        at_g = cursor[0]
        gsig = sb("gsig", [P, N_G, T])
        after_g = cursor[0]
        yT, eT = (sb("yT", [P, DC, T], at=at_g), sb("eT", [P, DC, T], at=at_g + DC * T * 4))
        x_in = sb("x_in", [P, NB, D], at=at_g)
        xs_in = sb("xs_in", [DEC, D])
        early = sb("early", [P, EARLY.shape[1]])
        lf_rows = sb("lf_rows", [DEC * PAGES, PAGE * AH])
        lfT = sb("lfT", [P, PAGES, DEC, AH])
        assert cursor[0] <= after_g
        cursor[0] = after_g
        at_2 = cursor[0]
        mbuf, lbuf = sb("mbuf", [P, BG, CLS, BH]), sb("lbuf", [P, BG, CLS, BH])
        obuf = sb("obuf", [P, BG, CLS, BO])
        toep = [sb(f"toep{g}", [P, BH, TOEP[g]]) for g in range(BG)]
        at_3 = cursor[0]
        q_aug = [sb(f"q_aug{i}", [HD + 2, 2, T]) for i in range(2)]
        k_aug = [sb(f"k_aug{i}", [HD + 2, 2, T]) for i in range(2)]
        kT, vT = sb("kT", [P, T]), sb("vT", [P, T])
        k_tok, v_tok = sb("k_tok", [P, NB, P]), sb("v_tok", [P, NB, P])
        prob = [sb(f"prob{i}", [P, 512]) for i in range(2)]
        probT = [sb(f"probT{i}", [P, 512]) for i in range(2)]
        at_4 = cursor[0]
        biased = [sb(f"biased{i}", [P, 512]) for i in range(2)]
        o_tok = sb("o_tok", [P, NB, P], at=at_4)
        top_m, den_m = sb("top_m", [P, CLS * BH], at=at_4), sb("den_m", [P, CLS * BH])
        cursor[0] = at_4 + 4096
        l_a, r_a, nm_a = sb("l_a", [P, 8]), sb("r_a", [P, 8]), sb("nm_a", [P, 8])
        nm_b = sb("nm_b", [P, 8])
        wf_raw, wf_hi, wf_lo = sb("wf_raw", [P, DC, AH]), sb("wf_hi", [P, DC, AH], F32R), sb("wf_lo", [P, DC, AH], F32R)
        bf = sb("bf", [AH, 1])
        xn, xsn = sb("xn", [P, NB, D], at=at_3), sb("xsn", [DEC, D])
        ss, rs, nv, nt = (sb(x, [P, NB + 1]) for x in ("ss", "rs", "nv", "nt"))
        hs_raw = sb("hs_raw", [P, DC, DEC])
        g_rows = sb("g_rows", [3 * DC, P])
        tables = sb("tables", [33, TABLES.shape[1]])
        relb = sb("relb", [33, 12])
        relb_rows = sb("relb_rows", [33, BG, DEC, BH])
        assert cursor[0] <= at_4
        fx = sb("fx", [AH, T], at=at_2)
        fa, fe, fu, fd, fr = (sb(n, [AH, T]) for n in ("fa", "fe", "fu", "fd", "fr"))
        assert cursor[0] <= at_2 + 384 + CLS * BG * BO * 4
        gen = [sb(f"gen{g}", [BH, PITCH[g]], at=at_2 + 384 + CLS * BG * BO * 4 if g == 0 else None) for g in range(BG)]
        assert cursor[0] <= at_3
        st = sb("st", [DEC, 3 * ROUNDS, P], at=at_3)
        kv_a = [sb(f"kv_a{i}", [P, PAGES, AW]) for i in range(2)]
        kv_b = [sb(f"kv_b{i}", [P, BG, BO]) for i in range(2)]
        self_p = sb("self_p", [DEC, ROUNDS, P], at=at_3 + 3 * ROUNDS * P * 4 + PAGES * AW * 4)
        qbc = [sb(f"qbc{i}", [P, AW + BQ], at=at_2 + i * 4 * (AW + BQ)) for i in range(2)]
        prod = [sb(f"prod{i}", [P, AW]) for i in range(2)]
        assert cursor[0] <= at_3
        cursor[0] = top[0]
        bias_s = sb("bias_s", [DEC * BH, sum(SLOTS) + BG])
        logf = sb("logf", [AH, T])
        cum, ncum = sb("cum", [AH, SEQ], at=at_4), sb("ncum", [AH, SEQ], at=at_4 + 2048)
        cursor[0] = top[0]
        pt = sb("pt", [1, DEC * PAGES], I32)
        sm = sb("sm", [DEC * AH, 16])
        self_a, self_b = sb("self_a", [DEC, AH]), sb("self_b", [DEC, BH, BG])
        row_a = sb("row_a", [DEC * AH, PAST + 1], at=at_2)
        row_b = sb("row_b", [DEC * BH, sum(SLOTS) + BG])
        pTa = sb("pTa", [P, PAGES, DEC, DEC, AH])
        pTb = sb("pTb", [P, BG, DEC, DEC, BH])
        dsel_a, dsel_b = sb("dsel_a", [64, DEC]), sb("dsel_b", [32, BG, DEC])
        d_a, d_b = sb("d_a", [DEC, 64]), sb("d_b", [DEC, BG, 32])
        os_a, os_b = sb("os_a", [DEC * AH, AW]), sb("os_b", [DEC * BH, BO])
        assert cursor[0] <= at_3
        og_hi, og_lo = sb("og_hi", [P, 6, T], F32R, at=at_2), sb("og_lo", [P, 6, T], F32R)
        og_raw = [sb(f"og_raw{i}", [P, T]) for i in range(2)]
        pT_hi, pT_lo = sb("pT_hi", [P, 2, T], F32R), sb("pT_lo", [P, 2, T], F32R)
        p_in, ps_in = sb("p_in", [P, NB, PLE]), sb("ps_in", [DEC, PLE])
        assert cursor[0] <= top[0], (cursor[0], top[0])
        sq2 = [sb("sq2_0", [P, T]), sb("sq2_1", [P, T])]
        acc_y, acc_e, rs_y, rs_e, nv2, nt2 = (sb(n, [P, T]) for n in ("acc_y", "acc_e", "rs_y", "rs_e", "nv2", "nt2"))
        assert cursor[0] <= top[0]
        sg = [sb("sg0", [P, T], at=at_2), sb("sg1", [P, T])]
        fin = [sb(f"fin{i}", [P, T]) for i in range(2)]
        tok_out = [sb(f"tok_out{i}", [P, NB, P]) for i in range(2)]
        toks_out = sb("toks_out", [DEC, D])
        assert cursor[0] <= top[0], (cursor[0], top[0])

        c_dram = nc.dram_tensor("c_dram", [2, AH, SEQ], F32).ap()
        toep_dram = [nc.dram_tensor(f"toep_dram{g}", [BH, P * PITCH[g]], F32).ap() for g in range(BG)]
        o0_dram = nc.dram_tensor("o0_dram", [SEQ, BO], F32).ap()
        m0_dram, l0_dram = (nc.dram_tensor(n, [SEQ, BH], F32).ap() for n in ("m0_dram", "l0_dram"))
        q_dram = nc.dram_tensor("q_dram", [DEC, ROUNDS * P], F32).ap()
        selfa_dram = nc.dram_tensor("selfa_dram", [DEC, AH], F32).ap()
        selfb_dram = nc.dram_tensor("selfb_dram", [DEC, BH * BG], F32).ap()
        lfn_dram = nc.dram_tensor("lfn_dram", [DEC, AH], F32).ap()

        (yp, ys, akv_p, alf_p, b0_p, b1_p, b2_p, akv_s, alf_s, b0_s, b1_s, b2_s) = O
        b_p, b_s = (b0_p, b1_p, b2_p), (b0_s, b1_s, b2_s)
        caches = (A["cache_b0_kv"], A["cache_b1_kv"], A["cache_b2_kv"])
        w_in = A["w_in"][0].rearrange("(c p) n -> p c n", p=P)
        w_br_a = A["w_br_a"][0].rearrange("(c p) n -> p c n", p=P)
        w_br_b = A["w_br_b"][0].rearrange("(c p) n -> p c n", p=P)
        w_out = A["w_out"][0].rearrange("(c p) n -> p c n", p=P)
        w_ple = A["w_ple"][0].rearrange("(c p) n -> p c n", p=P)
        w_gate = A["w_ple_gate"][0].rearrange("(c p) n -> p c n", p=P)

        def weight_parts(n):
            if n < TILE_G:
                r, j = n // 3, n % 3
                if r < ROUNDS_A:
                    col = (COL_QA, COL_KA, COL_VA)[j] + r * P
                else:
                    col = (COL_QB, COL_KB, COL_VB)[j] + (r - ROUNDS_A) * P
                return [(w_in[:, :, col:col + P], 0, DC)]
            if n < TILE_Z:
                col = COL_GA + (n - TILE_G) * P
                return [(w_in[:, :, col:col + P], 0, DC)]
            if n < TILE_BR:
                z = n - TILE_Z
                col = COL_ZA + z * P if z < AW // P else COL_ZB + (z - AW // P) * P
                return [(w_in[:, :, col:col + P], 0, DC)]
            m = (n - TILE_BR) % DC
            cols = slice(m * P, (m + 1) * P)
            if n < TILE_OUT:
                return [(w_br_a[:, :, cols], 0, 4), (w_br_b[:, :, cols], 4, 2)]
            if TILE_PLE <= n < TILE_GATE:
                return [(w_ple[:, :, cols], 0, 2)]
            return [((w_out if n < TILE_GATE else w_gate)[:, :, cols], 0, DC)]

        def chunks(n):
            return sum(k for _, _, k in weight_parts(n))

        landed_at, total = {}, [0] * RING
        for n in range(TILES):
            total[n % RING] += 16 * len(weight_parts(n))
            landed_at[n] = total[n % RING]

        def units(r):
            if r == 0:
                return []
            return [(hd, qb) for qb in range(NB) for hd in range(2)] if r <= ROUNDS_A + 2 else [(0, None), (1, None)]

        USE_LOGF, USE_LF = 2 * DC, 2 * DC + 1
        unit0, use0, u, k = {}, {}, 0, 2 * DC + 2
        for r in range(1, ROUNDS + 1):
            unit0[r], use0[r] = u, k
            u += len(units(r))
            k += 2 + len(units(r)) + (r <= ROUNDS_A)
        UNITS, USE_COMBINE = u, k
        USE_SAMP = USE_COMBINE + 2
        USE_ROW = USE_SAMP + 8
        pt_use = {unit0[r] + i: use0[r] + 2 + i for r in unit0 for i in range(len(units(r)))}
        is_a = lambda r: r <= ROUNDS_A
        unit_a = 8 * ROUNDS_A

        s_const, s_small, s_pt, s_g, s_xs, s_wf, s_cd = (sem(n) for n in ("s_const", "s_small", "s_pt", "s_g", "s_xs", "s_wf", "s_cd"))
        s_x = sems("s_x", NB)
        s_w = sems("s_w", RING)
        s_crow = sems("s_crow", 2)
        s_hi, s_lo = sem("s_hi"), sem("s_lo")
        s_half, s_free = sems("s_half", 2), sems("s_free", 2)
        s_use, s_used = sem("s_use"), sem("s_used")
        s_sc, s_mx, s_ex, s_rc, s_pv, s_pve = (sem(n) for n in ("s_sc", "s_mx", "s_ex", "s_rc", "s_pv", "s_pve"))
        s_kst, s_vst = sem("s_kst"), sem("s_vst")
        s_v = sem("s_v")
        s_a = sem("s_a")
        s_p = sem("s_p")
        names = ("s_relb s_gt s_gv s_ssz s_sqx s_nv s_y0 s_rs s_xn s_hh s_hsr s_hsh s_hl s_wfhi s_wflo s_gen s_gent s_gend s_toep "
                 "s_biasm s_bias s_fm s_fx s_fe s_fu s_fl s_logf s_cum s_clear s_xst s_xsv s_copy s_ge s_g3 "
                 "s_o0 s_o0r s_md s_wexp s_comb s_selfp s_sst s_qd s_qb0 s_qb1 s_kp0 s_kp1 s_bk0 s_bk1 s_prod s_red s_pz "
                 "s_lfr s_suf s_lsum s_lga s_selfr s_nma s_nmb s_exa s_exb s_pn s_dm s_dv s_ds s_samp s_os s_osm s_ot s_ov s_slfd "
                 "s_ogr s_ogh s_ogl s_mh s_ml s_pin s_ptr s_pte s_pth s_ptl s_sqe s_ace s_sqy s_acy "
                 "s_sse s_nve s_y0e s_rse s_ssy s_nvy s_y0y s_rsy s_xsum s_x2h s_x2l s_fin s_tt s_tte s_tts s_ttse s_yst0 s_yst1 s_ysst s_lfst").split()
        S = {n: sem(n) for n in names}

        N_CONST = 10
        block = ctx.enter_context(nc.Block())

        @block.sync
        def _(sp):
            def load(n):
                if n >= RING:
                    sp.wait_ge(s_lo, n - RING + 1)
                for src, c0, nk in weight_parts(n):
                    sp.dma_start(w_raw[n % RING][:, c0:c0 + nk, :], src).then_inc(s_w[n % RING], 16)

            for b in range(NB):
                sp.dma_start(x_in[:, b, :], A["x_prompt"][0, b * P:(b + 1) * P, :]).then_inc(s_x[b], 16)
            sp.dma_start(xs_in[:, :], A["x_sample"].rearrange("s o d -> (s o) d")).then_inc(s_xs, 16)
            sp.dma_start(wf_raw[:, :, :], w_in[:, :, COL_F:COL_F + AH]).then_inc(s_wf, 16)
            for n in range(RING):
                load(n)
            sp.wait_ge(s_pt, 16)
            for i in range(DEC * PAGES):
                page = sp.value_load(pt[0:1, i:i + 1], min_val=0, max_val=POOL_PAGES - 1)
                sp.dma_start(lf_rows[i:i + 1, :], A["cache_a_logf"][0, bass.ds(page, 1), :, :].rearrange("o t h -> o (t h)")).then_inc(S["s_lfr"], 16)
            sp.wait_ge(S["s_cum"], 2)
            sp.dma_start(c_dram[0], cum[:, :]).then_inc(s_cd, 16)
            sp.dma_start(c_dram[1], ncum[:, :]).then_inc(s_cd, 16)
            sp.wait_ge(s_cd, 32)
            sp.wait_ge(S["s_clear"], 1)
            for r in range(ROUNDS_A):
                for n in range(3 * r + 3, 3 * r + 5):
                    load(n)
                if r >= 2:
                    sp.wait_ge(s_sc, 8 * (r - 1))
                s = r % 2
                sp.dma_start(q_aug[s][HD + 1:HD + 2, :, 0:SEQ], c_dram[0:1, 2 * r:2 * r + 2, :]).then_inc(s_crow[s], 16)
                sp.dma_start(k_aug[s][HD:HD + 1, :, 0:SEQ], c_dram[1:2, 2 * r:2 * r + 2, :]).then_inc(s_crow[s], 16)
                load(3 * r + 5)
            for n in range(3 * ROUNDS_A + 3, TILE_G + 9):
                load(n)

            def sample_queries(s):
                if s >= 2:
                    sp.wait_ge(S["s_prod"], 7 * (s - 1))
                sp.dma_start(qbc[s % 2][:, :], q_dram[s:s + 1, :].to_broadcast([P, ROUNDS * P])).then_inc(S[f"s_qb{s % 2}"], 16)

            def sample_rows(s, kv):
                for p in range(PAGES):
                    page = sp.value_load(pt[0:1, PAGES * s + p:PAGES * s + p + 1], min_val=0, max_val=POOL_PAGES - 1)
                    src = A["cache_a_kv"][0, bass.ds(page, 1), :, kv, :, :].rearrange("o t h d -> (o t) (h d)")
                    sp.dma_start(kv_a[s % 2][:, p, :], src).then_inc(S[f"s_kp{s % 2}"], 16)
                for g in range(BG):
                    n, step = SLOTS[g], DIL[g]
                    src = caches[g][0, s, 0:n * step:step, kv, :, :].rearrange("t h d -> t (h d)")
                    sp.dma_start(kv_b[s % 2][0:n, g, :], src).then_inc(S[f"s_bk{s % 2}"], 16)

            sp.wait_ge(S["s_qd"], 16)
            sp.wait_ge(S["s_comb"], 1)
            sp.wait_ge(S["s_selfp"], 1)
            n = TILE_G + 9
            for s in range(DEC):
                sample_queries(s)
                sample_rows(s, 0)
                load(n)
                n += 1
            sp.wait_ge(S["s_red"], 7 * DEC)
            sp.wait_ge(S["s_prod"], 7 * DEC)
            sp.wait_ge(S["s_slfd"], 48)
            sp.dma_start(row_a[:, PAST:PAST + 1], selfa_dram.rearrange("s (h o) -> (s h) o", o=1)).then_inc(S["s_selfr"], 16)
            sp.dma_start(sm[:, 0:1], lfn_dram.rearrange("s (h o) -> (s h) o", o=1)).then_inc(S["s_selfr"], 16)
            sp.dma_start(sm[0:DEC * BH, 1:1 + BG], selfb_dram.rearrange("s (h g) -> (s h) g", g=BG)).then_inc(S["s_selfr"], 16)
            for s in range(2):
                sample_rows(s, 1)
            while n < TILE_BR:
                load(n)
                n += 1
            for s in range(2, DEC):
                sp.wait_ge(S["s_samp"], s - 1)
                sample_rows(s, 1)
                if s >= 5:
                    load(n)
                    n += 1
            sp.wait_ge(S["s_ov"], 1)
            sp.dma_start(p_in[:, :, :], A["p_prompt"][0, 0].rearrange("(b p) d -> p b d", p=P)).then_inc(S["s_pin"], 16)
            sp.dma_start(ps_in[:, :], A["p_sample"][0].rearrange("s o d -> (s o) d")).then_inc(S["s_pin"], 16)
            while n < TILES:
                load(n)
                n += 1

        @block.gpsimd
        def _(pool):
            own = Tally(s_p)
            pool.dma_start(pt[:, :], A["page_table"].rearrange("(o s) p -> o (s p)", o=1)).then_inc(s_pt, 16)
            pool.dma_start(relb[0:32, :], A["rel_bias"]).then_inc(s_small, 16)
            pool.dma_start(tables[:, :], const_in[1]).then_inc(s_small, 16)
            pool.dma_start(bf[:, :], A["b_f"].rearrange("o h -> h o"), allow_slow_non_contiguous=True).then_inc(s_small, 16)
            pool.dma_start(early[:, :], const_in[2]).then_inc(s_small, 16)
            pool.wait_ge(S["s_gen"], BG)
            for g in range(BG):
                for h in range(BH):
                    src = gen[g][h:h + 1, :].unsqueeze(1).to_broadcast([1, P, PITCH[g]])
                    pool.dma_start(toep_dram[g][h:h + 1, :].rearrange("o (i y) -> o i y", i=P), src).then_inc(S["s_gend"], 16)
            pool.wait_ge(S["s_gend"], 16 * BG * BH)
            for g in range(BG):
                for h in range(BH):
                    rows = toep_dram[g][h, P - 1:P - 1 + P * (PITCH[g] - 1)].rearrange("(i y) -> i y", i=P)
                    pool.dma_start(toep[g][:, h, :], rows[:, 0:TOEP[g]]).then_inc(S["s_toep"], 16)
            pool.wait_ge(s_used, USE_LOGF + 1)
            pool.dma_start(alf_p[0, 0].rearrange("(b p) h -> p b h", p=P), lf_small[:, 0:NB, :]).then_inc(S["s_lfst"], 16)
            pool.dma_start(alf_s[0].rearrange("s o h -> (s o) h"), lf_small[0:DEC, NB, :]).then_inc(S["s_lfst"], 16)
            pool.dma_start(lfn_dram, lf_small[0:DEC, NB, :]).then_inc(S["s_slfd"], 16)

            for r in range(1, ROUNDS + 1):
                t = r - 1
                if r <= ROUNDS - 1:
                    for g in range(BG):
                        wb = caches[g].shape[2]
                        if g == 0 and r > 1:
                            continue
                        s0, s1 = (0, DEC) if g == 0 else (r - 1, r)
                        if s1 > DEC:
                            continue
                        a = 16 // (s1 - s0)
                        pool.dma_start(b_s[g][0, s0:s1, 0:wb - 1].rearrange("s t k h d -> s (t k h d)").rearrange("s (a n) -> s a n", a=a),
                                       caches[g][0, s0:s1, 1:wb].rearrange("s t k h d -> s (t k h d)").rearrange("s (a n) -> s a n", a=a)).then_inc(S["s_copy"], 16)
                pool.wait_ge(s_used, use0[r] + 1)
                for kv, (buf, done) in enumerate(((k_tok, s_kst), (v_tok, s_vst))):
                    if kv == 1:
                        pool.wait_ge(s_used, use0[r] + 2)
                    if is_a(r):
                        dst = akv_p[0, 0, :, kv, 2 * t:2 * t + 2, :].rearrange("(b p) h d -> p b (h d)", p=P)
                        pool.dma_start(dst, buf[:, :, :]).then_inc(done, 16)
                    else:
                        g, hp = divmod(t - ROUNDS_A, 2)
                        out = b_p[g][0, 0, :, kv, 2 * hp:2 * hp + 2, :]
                        if g == 0:
                            pool.dma_start(out.rearrange("p h d -> p (h d)"), buf[:, NB - 1, :]).then_inc(done, 16)
                        elif kv == 0:
                            pool.dma_start(out.rearrange("(b p) h d -> p b (h d)", p=P), buf[:, :, :]).then_inc(done, 16)
                        else:
                            pool.dma_start(out.rearrange("(p c) h d -> p c (h d)", c=CLS), buf[:, :, :]).then_inc(done, 16)
                if r == ROUNDS_A + 2:
                    pool.wait_ge(s_pve, unit0[r + 1])
                    pool.wait_ge(s_mx, unit0[r + 1])
                    pool.dma_start(o0_dram.rearrange("(b p) n -> p b n", p=P), obuf[:, 0]).then_inc(S["s_o0"], 16)
                    pool.dma_start(m0_dram.rearrange("(b p) n -> p b n", p=P), mbuf[:, 0]).then_inc(S["s_o0"], 16)
                    pool.dma_start(l0_dram.rearrange("(b p) n -> p b n", p=P), lbuf[:, 0]).then_inc(S["s_o0"], 16)
                    pool.wait_ge(S["s_o0"], 48)
                    pool.dma_start(obuf[:, 0], o0_dram.rearrange("(p c) n -> p c n", c=CLS)).then_inc(S["s_o0r"], 16)
                    pool.dma_start(mbuf[:, 0], m0_dram.rearrange("(p c) n -> p c n", c=CLS)).then_inc(S["s_o0r"], 16)
                    pool.dma_start(lbuf[:, 0], l0_dram.rearrange("(p c) n -> p c n", c=CLS)).then_inc(S["s_o0r"], 16)
            pool.wait_ge(s_used, USE_SAMP + 8)
            stv = st[:, :, :].rearrange("s (r j) c -> s j r c", j=3)
            pool.dma_start(q_dram.rearrange("s (r c) -> s r c", c=P), stv[:, 0]).then_inc(S["s_qd"], 16)
            for kv in range(2):
                pool.dma_start(akv_s[0, :, 0, kv].rearrange("s (r h) d -> s r (h d)", h=2), stv[:, 1 + kv, 0:ROUNDS_A]).then_inc(S["s_sst"], 16)
                for g in range(BG):
                    wb = caches[g].shape[2]
                    r0 = ROUNDS_A + 2 * g
                    pool.dma_start(b_s[g][0, :, wb - 1, kv].rearrange("s (r h) d -> s r (h d)", h=2), stv[:, 1 + kv, r0:r0 + 2]).then_inc(S["s_sst"], 16)
            pool.wait_ge(S["s_selfp"], 1)
            pool.dma_start(selfa_dram, self_a[:, :]).then_inc(S["s_slfd"], 16)
            pool.dma_start(selfb_dram, self_b[:, :, :].rearrange("s h g -> s (h g)")).then_inc(S["s_slfd"], 16)
            k = 0
            for s in range(DEC):
                pool.wait_ge(S[f"s_qb{s % 2}"], 16 * (s // 2 + 1))
                pool.wait_ge(S[f"s_kp{s % 2}"], 64 * (s // 2 + 1))
                pool.wait_ge(S[f"s_bk{s % 2}"], 48 * (s // 2 + 1))
                for i in range(PAGES + BG):
                    if k >= 2:
                        pool.wait_ge(S["s_red"], k - 1)
                    if i < PAGES:
                        nc.gpsimd.tensor_tensor(prod[k % 2][:, :], kv_a[s % 2][:, i, :], qbc[s % 2][:, 0:AW], ALU.mult).then_inc(S["s_prod"], 1)
                    else:
                        g = i - PAGES
                        n = SLOTS[g]
                        nc.gpsimd.tensor_tensor(prod[k % 2][0:n, 0:BO], kv_b[s % 2][0:n, g, :], qbc[s % 2][0:n, AW + g * BO:AW + (g + 1) * BO], ALU.mult).then_inc(S["s_prod"], 1)
                    k += 1
            pool.wait_ge(S["s_red"], 7 * DEC)
            nc.gpsimd.memset(pTa[:, :, :, :, :], 0.0).then_inc(S["s_pz"], 1)
            nc.gpsimd.memset(pTb[:, :, :, :, :], 0.0).then_inc(S["s_pz"], 1)
            for i in range(6):
                pool.wait_ge(S["s_ogh"], i + 1)
                nc.gpsimd.tensor_tensor(og_lo[:, i, :], og_raw[i % 2][:, :], og_hi[:, i, :].bitcast(F32), ALU.subtract).then_inc(S["s_ogl"], 1)
            for m in range(DC):
                pool.wait_ge(S["s_mh"], m + 1)
                nc.gpsimd.tensor_tensor(h_lo[:, m, :], gsig[:, m, :], h_hi[:, m, :].bitcast(F32), ALU.subtract).then_inc(S["s_ml"], 1)
            def square_sum(total_, m, sq_done, done):
                pool.wait_ge(S[sq_done], m + 1)
                if m == 0:
                    nc.gpsimd.tensor_copy(total_[:, :], sq2[0][:, :]).then_inc(S[done], 1)
                else:
                    pool.wait_ge(S[done], m)
                    nc.gpsimd.tensor_tensor(total_[:, :], total_[:, :], sq2[m % 2][:, :], ALU.add).then_inc(S[done], 1)

            pool.wait_ge(S["s_ptl"], 2)
            for m in range(DC):
                square_sum(acc_y, m, "s_sqy", "s_acy")
            for c in range(DC):
                pool.wait_ge(S["s_x2h"], c + 1)
                nc.gpsimd.tensor_tensor(h_lo[:, c, :], xT[:, c, :], h_hi[:, c, :].bitcast(F32), ALU.subtract).then_inc(S["s_x2l"], 1)
            for m in range(DC):
                square_sum(acc_e, m, "s_sqe", "s_ace")
            for m in range(DC):
                pool.wait_ge(S["s_tte"], m + 1)
                pool.dma_start(yp[0, :, m * P:(m + 1) * P].rearrange("(b p) d -> p b d", p=P), tok_out[m % 2][:, :, :]).then_inc(S[f"s_yst{m % 2}"], 16)
            pool.wait_ge(S["s_ttse"], 2)
            pool.dma_start(ys.rearrange("s o d -> (s o) d"), toks_out[:, :]).then_inc(S["s_ysst"], 16)
            pool.wait_ge(S["s_lfst"], 32)
            pool.wait_ge(S["s_copy"], 16 * (1 + 2 * DEC))
            pool.wait_ge(s_kst, 16 * ROUNDS)
            pool.wait_ge(s_vst, 16 * ROUNDS)
            pool.wait_ge(S["s_sst"], 16 * 8)
            pool.wait_ge(S["s_yst0"], 16 * DC // 2)
            pool.wait_ge(S["s_yst1"], 16 * DC // 2)
            pool.wait_ge(S["s_ysst"], 16)

        def later_sums_t(pe, turn):
            pe.wait_ge(S["s_lfr"], 16 * DEC * PAGES)
            turn([(P, h * 32, lf_rows[:, h:PAGE * AH:AH]) for h in range(AH)])
            pe.wait_ge(s_used, USE_LF + 1)
            cols = lfT[:, :, :, :].rearrange("p g s h -> p (g s h)")
            c0, c1 = EARLY_COLS["later"]
            nc.tensor.matmul(pv[0][:, 0:256], early[:, c0:c1], cols, start=True, stop=False)
            for k in range(1, PAGES):
                w = 256 - 64 * k
                last = nc.tensor.matmul(pv[0][:, 0:w], ones, cols[:, 64 * k:256], start=False, stop=k == PAGES - 1)
            last.then_inc(S["s_suf"], 1)

        def sample_rows_t(pe, turn):
            pe.wait_ge(S["s_lga"], 1)
            turn([(DEC * AH, p * P, lg_a[:, p, :, :].rearrange("p s h -> p (s h)")) for p in range(PAGES)])
            at, outs = 0, []
            for g in range(BG):
                outs.append((DEC * BH, at, lg_b[0:SLOTS[g], g, :, :].rearrange("p s h -> p (s h)")))
                at += SLOTS[g] + 1
            turn(outs)

        def sample_probs_t(pe, turn):
            pe.wait_ge(S["s_pn"], 2)
            turn([(P, p * 64, row_a[:, p * P:(p + 1) * P]) for p in range(PAGES)])
            at, outs = 0, []
            for g in range(BG):
                outs.append((SLOTS[g], g * 32, row_b[:, at:at + SLOTS[g]]))
                at += SLOTS[g] + 1
            turn(outs)
            pe.wait_ge(S["s_ds"], 1 + BG)
            nc.tensor.matmul(pv[0][0:DEC, 0:64], dsel_a[:, :], ident[0:64, 0:64], start=True, stop=True)
            for g in range(BG):
                last = nc.tensor.matmul(pv[0][0:DEC, 64 + 32 * g:96 + 32 * g], dsel_b[:, g, :], ident[0:32, 0:32], start=True, stop=True)
            last.then_inc(S["s_dm"], 1)

        def sample_values(pe, s):
            pe.wait_ge(S[f"s_kp{s % 2}"], 64 * (DEC // 2 + s // 2 + 1))
            pe.wait_ge(S[f"s_bk{s % 2}"], 48 * (DEC // 2 + s // 2 + 1))
            pe.wait_ge(s_used, USE_ROW + 4)
            for p in range(PAGES):
                nc.tensor.matmul(sc[0][0:DEC * AH, :], pTa[:, p, s, :, :].rearrange("p s h -> p (s h)"), kv_a[s % 2][:, p, :],
                                 start=s == 0 and p == 0, stop=False)
            for g in range(BG):
                n = SLOTS[g]
                last = nc.tensor.matmul(sc[1][0:DEC * BH, 0:BO], pTb[0:n, g, s, :, :].rearrange("p s h -> p (s h)"), kv_b[s % 2][0:n, g, :],
                                        start=s == 0 and g == 0, stop=False)
            last.then_inc(S["s_samp"], 1)

        def sample_end(pe):
            pe.wait_ge(S["s_dv"], 2)
            stv = st[:, :, :].rearrange("s (r j) c -> s j r c", j=3)[:, 2]
            nc.tensor.matmul(sc[0][0:DEC * AH, :], d_a[:, :], stv[:, 0:ROUNDS_A, :], start=False, stop=True)
            for g in range(BG):
                r0 = ROUNDS_A + 2 * g
                last = nc.tensor.matmul(sc[1][0:DEC * BH, 0:BO], d_b[:, g, :], stv[:, r0:r0 + 2, :], start=False, stop=g == BG - 1)
            last.then_inc(S["s_os"], 1)
            pe.wait_ge(S["s_osm"], 2)
            for cc in range(AW // P):
                nc.tensor.matmul(pv[0][:, cc * DEC:(cc + 1) * DEC], os_a[:, cc * P:(cc + 1) * P], cst("row_a", 64), start=True, stop=True)
            for cc in range(BO // P):
                last = nc.tensor.matmul(pv[0][:, 32 + cc * DEC:32 + (cc + 1) * DEC], os_b[:, cc * P:(cc + 1) * P], cst("row_b", 32), start=True, stop=True)
            last.then_inc(S["s_ot"], 1)

        @block.tensor
        def _(pe):
            use = Tally(s_use)

            def turn(outs):
                b = tr[use.n % 2]
                if use.n >= 2:
                    pe.wait_ge(s_used, use.n - 1)
                for rows, c0, src in outs:
                    k = src.shape[0]
                    w = 1
                    for x in src.shape[1:]:
                        w *= x
                    last = nc.tensor.transpose(b[0:rows, c0:c0 + k], src, ident[0:k, 0:k])
                use.up(last)

            def product(out, w_slot, k0, x_hi, x_lo, c_x, cols, first, last):
                lo, hi = cols
                pairs = ((w_hi[w_slot], x_hi), (w_hi[w_slot], x_lo), (w_lo[w_slot], x_hi))
                for i, (w, x) in enumerate(pairs):
                    ins = nc.tensor.matmul(out, w[:, k0, :], x[:, c_x, lo:hi], start=first and i == 0, stop=last and i == 2)
                return ins

            def project(n, k, x_hi=h_hi, x_lo=h_lo, each=None, kc=DC):
                half, part = divmod(k, 2)
                if k == 0:
                    pe.wait_ge(s_lo, n + 1)
                if part == 0 and n > 0:
                    pe.wait_ge(s_free[half], n)
                for c in range(part * kc // 2, (part + 1) * kc // 2):
                    if each is not None and half == 0:
                        pe.wait_ge(S[each], c + 1)
                    ins = product(pj[half][:, 0:HALF], n % RING, c, x_hi, x_lo, c, HALVES[half], c == 0, c == kc - 1)
                if part == 1:
                    ins.then_inc(s_half[half], 1)

            pe.wait_ge(s_const, 16)
            pe.wait_ge(s_g, 48)
            nc.tensor.transpose(pj[0][:, 0:3 * DC], g_rows[:, :], ident[0:3 * DC, 0:3 * DC]).then_inc(S["s_gt"], 1)
            pe.wait_ge(S["s_xn"], NB + 1)
            for c in range(DC):
                turn([(P, b * P, xn[:, b, c * P:(c + 1) * P]) for b in range(NB)])
            pe.wait_ge(s_xs, 16)
            for k, x in enumerate((xsn, xs_in)):
                for c in range(DC):
                    last = nc.tensor.transpose(pv[0][:, (k * DC + c) * DEC:(k * DC + c + 1) * DEC], x[:, c * P:(c + 1) * P], ident[0:DEC, 0:DEC])
            last.then_inc(S["s_xst"], 1)
            pe.wait_ge(S["s_wflo"], 1)
            pe.wait_ge(S["s_xsv"], 1)
            pe.wait_ge(S["s_hl"], 1)
            for half, (lo, hi) in enumerate(HALVES):
                for c in range(DC):
                    if half == 0:
                        pe.wait_ge(s_used, c + 1)
                    for i, (w, x) in enumerate(((wf_hi, h_hi), (wf_hi, h_lo), (wf_lo, h_hi))):
                        last = nc.tensor.matmul(pv[half][0:AH, 0:HALF], w[:, c, :], x[:, c, lo:hi], start=c == 0 and i == 0, stop=c == DC - 1 and i == 2)
            last.then_inc(S["s_fm"], 1)
            pe.wait_ge(S["s_relb"], 4)
            for g in range(BG):
                b = (sc[0], sc[1], pj[1])[g]
                c0, c1 = TABLE_COLS[f"toep{g}"]
                nc.tensor.matmul(b[0:BH, 0:PITCH[g]], relb[:, g * BH:(g + 1) * BH], tables[:, c0:c1], start=True, stop=True).then_inc(S["s_gent"], 1)
            at = 3 * DC
            for g in range(BG):
                c0, c1 = TABLE_COLS[f"slots{g}"]
                last = nc.tensor.matmul(pj[0][0:DEC * BH, at:at + c1 - c0], relb_rows[:, g, :, :], tables[:, c0:c1], start=True, stop=True)
                at += c1 - c0
            last.then_inc(S["s_biasm"], 1)
            pe.wait_ge(S["s_gen"], BG)
            pe.wait_ge(S["s_bias"], 1)

            def scores(r, i):
                hd, qb = units(r)[i]
                u = unit0[r] + i
                s = (r - 1) % 2
                b = sc[u % 2]
                if i == 0:
                    pe.wait_ge(s_free[0], 3 * r)
                    pe.wait_ge(s_free[1], 3 * r)
                    if is_a(r):
                        pe.wait_ge(s_crow[s], 32 * ((r - 1) // 2 + 1))
                if u >= 2:
                    if u - 2 < unit_a:
                        pe.wait_ge(s_ex, u - 1)
                    else:
                        pe.wait_ge(s_mx, u - 1)
                if is_a(r):
                    n = (qb + 1) * P
                    nc.tensor.matmul(b[:, 0:n], q_aug[s][:, hd, qb * P:n], k_aug[s][:, hd, 0:n], start=True, stop=False)
                    last = nc.tensor.matmul(b[:, qb * P:n], identb[:, :], causalb[:, :], start=False, stop=True)
                elif qb is not None:
                    k0 = max(qb - 1, 0) * P
                    n = (qb + 1) * P - k0
                    last = nc.tensor.matmul(b[:, 0:n], q_aug[s][0:HD, hd, qb * P:(qb + 1) * P], k_aug[s][0:HD, hd, k0:k0 + n], start=True, stop=True)
                else:
                    for c in range(CLS):
                        last = nc.tensor.matmul(b[:, c * P:(c + 1) * P], q_aug[s][0:HD, hd, c:SEQ:CLS], k_aug[s][0:HD, hd, c:SEQ:CLS], start=True, stop=True)
                last.then_inc(s_sc, 1)

            def blocks(r, qb):
                return qb + 1 if is_a(r) else CLS if qb is None else min(qb, 1) + 1

            def probs_t(r, i):
                u = unit0[r] + i
                pe.wait_ge(s_ex, u + 1)
                turn([(P, j * P, prob[u % 2][:, j * P:(j + 1) * P]) for j in range(blocks(r, units(r)[i][1]))])

            def values(r, i):
                hd, qb = units(r)[i]
                u = unit0[r] + i
                pe.wait_ge(s_used, pt_use[u] + 1)
                if u >= 2:
                    pe.wait_ge(s_pve, u - 1)
                n = blocks(r, qb)
                first = 0 if is_a(r) or qb is None else max(qb - 1, 0)
                for j in range(n):
                    v = v_tok[:, first + j, hd * HD:(hd + 1) * HD]
                    p = probT[u % 2][:, j * P:(j + 1) * P]
                    if qb is None:
                        last = nc.tensor.matmul(pv[u % 2][:, j * HD:(j + 1) * HD], p, v, start=True, stop=True)
                    else:
                        last = nc.tensor.matmul(pv[u % 2][:, 0:HD], p, v, start=j == 0, stop=j == n - 1)
                last.then_inc(s_pv, 1)

            for r in range(ROUNDS + 1):
                nu = len(units(r))
                for i in range(12):
                    if r and i == 0:
                        pe.wait_ge(s_free[0], 3 * r)
                        pe.wait_ge(s_free[1], 3 * r)
                        turn([(P, b * P, kT[:, b * P:(b + 1) * P]) for b in range(NB)])
                        if r - 1 < ROUNDS_A + 2:
                            turn([(P, b * P, vT[:, b * P:(b + 1) * P]) for b in range(NB)])
                        else:
                            turn([(P, c * P, vT[:, c:SEQ:CLS]) for c in range(CLS)])
                    if i < nu:
                        scores(r, i)
                    project(3 * r + i // 4, i % 4)
                    if r == 0 and 1 <= i <= DC:
                        turn([(P, b * P, x_in[:, b, (i - 1) * P:i * P]) for b in range(NB)])
                    if r == 0 and i == 9:
                        pe.wait_ge(S["s_logf"], 1)
                        b = tr[use.n % 2]
                        pe.wait_ge(s_used, use.n - 1)
                        for k in range(NB):
                            nc.tensor.transpose(b[:, k * AH:(k + 1) * AH], logf[:, k * P:(k + 1) * P], ident[0:AH, 0:AH])
                        use.up(nc.tensor.transpose(b[0:DEC, NB * AH:(NB + 1) * AH], logf[:, SEQ:T], ident[0:AH, 0:AH]))
                    if r == 0 and i == 10:
                        later_sums_t(pe, turn)
                    if 1 <= i <= nu:
                        probs_t(r, i - 1)
                    if 2 <= i <= nu + 1:
                        if r == 1 and i == 2:
                            pe.wait_ge(S["s_lsum"], 1)
                        values(r, i - 2)
                    if i == 10 and r and is_a(r):
                        pe.wait_ge(s_pve, unit0[r] + 8)
                        turn([(P, b * P, o_tok[:, b, :]) for b in range(NB)])

            for n in range(TILE_G + 3, TILE_BR):
                for k in range(4):
                    project(n, k)
                t = n - TILE_G - 3
                if t == 1:
                    assert use.n == USE_COMBINE
                    pe.wait_ge(S["s_comb"], 1)
                    for cc in range(2):
                        turn([(P, c * P, obuf[:, 0, c, cc * P:(cc + 1) * P]) for c in range(CLS)])
                    for k in range(8):
                        turn([(DEC, (q - 4 * k) * P, samp[:, q, :]) for q in range(4 * k, min(4 * k + 4, 3 * ROUNDS))])
                if t == 12:
                    sample_rows_t(pe, turn)
                if t == 13:
                    sample_probs_t(pe, turn)
                if 14 <= t:
                    for s in range(2 * (t - 14), min(2 * (t - 14) + 2, DEC)):
                        sample_values(pe, s)
            sample_end(pe)

            for m in range(DC):
                n = TILE_BR + m
                pe.wait_ge(s_lo, n + 1)
                for half, cols in enumerate(HALVES):
                    pe.wait_ge(s_free[half], n)
                    for c in range(6):
                        if m == 0 and half == 0:
                            pe.wait_ge(S["s_ogl"], c + 1)
                        out = (pj if c < 4 else sc)[half][:, 0:HALF]
                        ins = product(out, n % RING, c, og_hi, og_lo, c, cols, c in (0, 4), c in (3, 5))
                    ins.then_inc(s_half[half], 1)
            pe.wait_ge(S["s_pin"], 32)
            pe.wait_ge(S["s_ov"], 1)
            for c in range(2):
                for b in range(NB):
                    last = nc.tensor.transpose(pv[c][:, b * P:(b + 1) * P], p_in[:, b, c * P:(c + 1) * P], ident)
                last.then_inc(S["s_ptr"], 1)
            turn([(P, c * DEC, ps_in[:, c * P:(c + 1) * P]) for c in range(2)])
            def mean_square(total_, ready, done):
                pe.wait_ge(S[ready], DC)
                for half, (lo, hi) in enumerate(HALVES):
                    last = nc.tensor.matmul(pv[half][:, 0:HALF], ones, total_[:, lo:hi], start=True, stop=True)
                last.then_inc(S[done], 1)

            pe.wait_ge(S["s_pte"], 2)
            for n in range(TILE_OUT, TILE_PLE):
                for k in range(4):
                    project(n, k, h_hi, h_lo, "s_ml" if n == TILE_OUT else None)
            for n in range(TILE_PLE, TILE_GATE):
                for k in range(4):
                    project(n, k, pT_hi, pT_lo, "s_ptl" if n == TILE_PLE else None, 2)
                if n == TILE_PLE + 1:
                    mean_square(acc_y, "s_acy", "s_ssy")
            def result(m):
                pe.wait_ge(S["s_fin"], m + 1)
                if m >= 2:
                    pe.wait_ge(S["s_tte"], m - 1)
                for b in range(NB):
                    last = nc.tensor.transpose(sc[m % 2][:, b * P:(b + 1) * P], fin[m % 2][:, b * P:(b + 1) * P], ident)
                last.then_inc(S["s_tt"], 1)
                nc.tensor.transpose(pv[m // 4][0:DEC, m % 4 * P:m % 4 * P + P], fin[m % 2][:, SEQ:T], ident).then_inc(S["s_tts"], 1)

            for m in range(DC):
                if m == 2:
                    pe.wait_ge(S["s_nvy"], 2)
                    mean_square(acc_e, "s_ace", "s_sse")
                    pe.wait_ge(S["s_nve"], 2)
                for k in range(4):
                    project(TILE_GATE + m, k, h_hi, h_lo, "s_x2l" if m == 0 else None)
                if m >= 2:
                    result(m - 2)
            for m in range(DC - 2, DC):
                result(m)

        @block.scalar
        def _(act):
            own = Tally(s_a)

            def hi_part(n):
                act.wait_ge(s_w[n % RING], landed_at[n])
                if n >= RING:
                    act.wait_ge(s_half[1], n - RING + 1)
                k = chunks(n)
                nc.scalar.activation(w_hi[n % RING][:, 0:k, :], w_raw[n % RING][:, 0:k, :], ACT.Copy).then_inc(s_hi, 1)

            act.dma_start(const[:, :], const_in[0]).then_inc(s_const, 16)
            for i, name in enumerate(("g_pre", "g_post", "g_ple")):
                act.dma_start(g_rows[i * DC:(i + 1) * DC, :], A[name][0].rearrange("(c p) -> c p", p=P)).then_inc(s_g, 16)
            act.wait_ge(S["s_ssz"], 1)
            for b in range(NB):
                act.wait_ge(s_x[b], 16)
                nc.scalar.activation(xn[:, b, :], x_in[:, b, :], ACT.Square, accum_out=ss[:, b:b + 1]).then_inc(S["s_sqx"], 1)
            act.wait_ge(s_xs, 16)
            nc.scalar.activation(xsn[:, :], xs_in[:, :], ACT.Square, accum_out=ss[0:DEC, NB:NB + 1]).then_inc(S["s_sqx"], 1)
            act.wait_ge(s_wf, 16)
            nc.scalar.activation(wf_hi[:, :, :], wf_raw[:, :, :], ACT.Copy).then_inc(S["s_wfhi"], 1)
            act.wait_ge(S["s_nv"], 1)
            own.up(nc.scalar.activation(nt[:, :], nv[:, :], ACT.Ln))
            act.wait_ge(s_a, own.n)
            nc.scalar.activation(rs[:, :], nt[:, :], ACT.Exp, scale=-0.5).then_inc(S["s_y0"], 1)
            hi_part(0)
            act.wait_ge(S["s_gv"], 1)
            for c in range(DC):
                act.wait_ge(s_use, c + 1)
                nc.scalar.activation(h_hi[:, c, 0:SEQ], tr[c % 2][:, :], ACT.Copy, scale=gpre[:, c:c + 1]).then_inc(S["s_hh"], 1)
            act.wait_ge(S["s_hsr"], 1)
            nc.scalar.activation(h_hi[:, :, SEQ:T], hs_raw[:, :, :], ACT.Copy).then_inc(S["s_hsh"], 1)
            hi_part(1)
            hi_part(2)
            act.wait_ge(S["s_fx"], 2)
            own.up(nc.scalar.activation(fa[:, :], fx[:, :], ACT.Abs))
            act.wait_ge(s_a, own.n)
            nc.scalar.activation(fe[:, :], fa[:, :], ACT.Exp, scale=-1.0).then_inc(S["s_fe"], 1)
            act.wait_ge(S["s_fu"], 1)
            nc.scalar.activation(fa[:, :], fu[:, :], ACT.Ln).then_inc(S["s_fl"], 1)

            def evac0(n):
                act.wait_ge(s_half[0], n + 1)
                ps = pj[0]
                if n == 0:
                    act.wait_ge(S["s_clear"], 1)
                if n < TILE_G:
                    r, j = divmod(n, 3)
                    s = r % 2
                    if j == 0:
                        nc.scalar.activation(q_aug[s][0:HD, 0, 0:HALF], ps[0:HD, 0:HALF], ACT.Copy, scale=SCALE)
                        last = nc.scalar.activation(q_aug[s][0:HD, 1, 0:HALF], ps[HD:P, 0:HALF], ACT.Copy, scale=SCALE)
                    elif j == 1:
                        nc.scalar.activation(k_aug[s][0:HD, 0, 0:HALF], ps[0:HD, 0:HALF], ACT.Copy)
                        nc.scalar.activation(k_aug[s][0:HD, 1, 0:HALF], ps[HD:P, 0:HALF], ACT.Copy)
                        last = nc.scalar.activation(kT[:, 0:HALF], ps[:, 0:HALF], ACT.Copy)
                    else:
                        last = nc.scalar.activation(vT[:, 0:HALF], ps[:, 0:HALF], ACT.Copy)
                    last.then_inc(s_free[0], 1)
                else:
                    gate(n, 0)

            def gate(n, half):
                lo, hi = HALVES[half]
                if n < TILE_Z:
                    dst = gsig[:, n - TILE_G, lo:hi]
                    nc.scalar.activation(dst, pj[half][:, 0:HALF], ACT.Copy if n < TILE_G + 3 else ACT.Sigmoid).then_inc(s_free[half], 1)
                else:
                    nc.scalar.activation(zsil[:, n - TILE_Z, lo:hi], pj[half][:, 0:HALF], ACT.Sigmoid).then_inc(S["s_ge"], 1)

            def evac1(n):
                if n < TILE_G:
                    return
                act.wait_ge(s_half[1], n + 1)
                gate(n, 1)

            def exps(r, i):
                hd, qb = units(r)[i]
                u = unit0[r] + i
                act.wait_ge(s_mx, u + 1)
                if u >= 2:
                    act.wait_ge(s_use, pt_use[u - 2] + 1)
                if is_a(r):
                    n = (qb + 1) * P
                    if u >= 8:
                        act.wait_ge(s_rc, u - 7)
                    last = nc.scalar.activation(prob[u % 2][:, 0:n], sc[u % 2][:, 0:n], ACT.Exp, bias=nm_a[:, u % 8:u % 8 + 1], accum_out=l_a[:, u % 8:u % 8 + 1])
                else:
                    g, hp = divmod(r - 1 - ROUNDS_A, 2)
                    h = 2 * hp + hd
                    if qb is not None:
                        n = (min(qb, 1) + 1) * P
                        last = nc.scalar.activation(prob[u % 2][:, 0:n], biased[u % 2][:, 0:n], ACT.Exp, bias=nm_b[:, 4 * (u % 2):4 * (u % 2) + 1],
                                                    accum_out=lbuf[:, g, qb, h:h + 1])
                    else:
                        for c in range(CLS):
                            last = nc.scalar.activation(prob[u % 2][:, c * P:(c + 1) * P], biased[u % 2][:, c * P:(c + 1) * P], ACT.Exp,
                                                        bias=nm_b[:, 4 * (u % 2) + c:4 * (u % 2) + c + 1], accum_out=lbuf[:, g, c, h:h + 1])
                last.then_inc(s_ex, 1)

            def values_out(r, i):
                hd, qb = units(r)[i]
                u = unit0[r] + i
                act.wait_ge(s_pv, u + 1)
                if is_a(r):
                    act.wait_ge(s_rc, u + 1)
                    if i == 0 and r > 1:
                        act.wait_ge(s_use, use0[r])
                    last = nc.scalar.activation(o_tok[:, qb, hd * HD:(hd + 1) * HD], pv[u % 2][:, 0:HD], ACT.Copy, scale=r_a[:, u % 8:u % 8 + 1])
                else:
                    g, hp = divmod(r - 1 - ROUNDS_A, 2)
                    h = 2 * hp + hd
                    if qb is not None:
                        last = nc.scalar.activation(obuf[:, g, qb, h * HD:(h + 1) * HD], pv[u % 2][:, 0:HD], ACT.Copy)
                    else:
                        last = nc.scalar.activation(obuf[:, g, :, h * HD:(h + 1) * HD], pv[u % 2][:, 0:CLS * HD].rearrange("p (c d) -> p c d", d=HD), ACT.Copy)
                last.then_inc(s_pve, 1)

            for r in range(ROUNDS + 1):
                nu = len(units(r))
                for i in range(12):
                    n = 3 * r + i // 4
                    if i < nu:
                        exps(r, i)
                    if i % 4 == 1:
                        evac0(n)
                    if 2 <= i <= nu + 1:
                        values_out(r, i - 2)
                    if i % 4 == 3:
                        evac1(n)
                        hi_part(n + RING)

            for n in range(TILE_G + 3, TILE_BR):
                t = n - TILE_G - 3
                evac0(n)
                evac1(n)
                hi_part(n + RING)
                if t == 0:
                    act.wait_ge(S["s_md"], 1)
                    nc.scalar.activation(mbuf[:, :, :, :], mbuf[:, :, :, :], ACT.Exp).then_inc(S["s_wexp"], 1)
                    nc.scalar.activation(gsig[:, 0:3, :], gsig[:, 0:3, :], ACT.Sigmoid).then_inc(S["s_g3"], 1)
                if t == 12:
                    act.wait_ge(S["s_nma"], 1)
                    nc.scalar.activation(row_a[:, :], row_a[:, :], ACT.Exp, bias=sm[:, 5:6], accum_out=sm[:, 6:7]).then_inc(S["s_exa"], 1)
                    act.wait_ge(S["s_nmb"], 1)
                    nc.scalar.activation(row_b[:, :], row_b[:, :], ACT.Exp, bias=sm[0:32, 8:9], accum_out=sm[0:32, 9:10]).then_inc(S["s_exb"], 1)
            for i in range(6):
                act.wait_ge(S["s_ogr"], i + 1)
                nc.scalar.activation(og_hi[:, i, :], og_raw[i % 2][:, :], ACT.Copy).then_inc(S["s_ogh"], 1)
            for m in range(DC):
                act.wait_ge(s_free[0], TILE_BR + m + 1)
                act.wait_ge(s_free[1], TILE_BR + m + 1)
                nc.scalar.activation(h_hi[:, m, :], gsig[:, m, :], ACT.Copy).then_inc(S["s_mh"], 1)
                hi_part(TILE_BR + m + RING)
            for c in range(2):
                if c == 0:
                    act.wait_ge(S["s_pte"], 2)
                    act.wait_ge(s_used, USE_ROW + 5)
                nc.scalar.activation(pT_hi[:, c, :], acc_y[:, :] if c else acc_e[:, :], ACT.Copy).then_inc(S["s_pth"], 1)
            for m in range(DC):
                n = TILE_OUT + m
                act.wait_ge(s_half[0], n + 1)
                nc.scalar.activation(yT[:, m, 0:HALF], pj[0][:, 0:HALF], ACT.Copy).then_inc(s_free[0], 1)
                act.wait_ge(s_free[0], n + 1)
                act.wait_ge(s_free[1], n + 1)
                if m >= 2:
                    act.wait_ge(S["s_acy"], m - 1)
                nc.scalar.activation(sq2[m % 2][:, :], yT[:, m, :], ACT.Square).then_inc(S["s_sqy"], 1)
                hi_part(n + RING)
            for m in range(DC):
                n = TILE_PLE + m
                act.wait_ge(s_half[0], n + 1)
                nc.scalar.activation(eT[:, m, 0:HALF], pj[0][:, 0:HALF], ACT.Copy).then_inc(s_free[0], 1)
                hi_part(n + RING)
                if m == 2:
                    act.wait_ge(S["s_nvy"], 2)
                    own.up(nc.scalar.activation(nt2[:, :], nv2[:, :], ACT.Ln))
                    act.wait_ge(s_a, own.n)
                    nc.scalar.activation(rs_y[:, :], nt2[:, :], ACT.Exp, scale=-0.5).then_inc(S["s_y0y"], 1)
                if 3 <= m <= 6:
                    for c in range(2 * (m - 3), 2 * (m - 3) + 2):
                        act.wait_ge(S["s_xsum"], c + 1)
                        nc.scalar.activation(h_hi[:, c, :], xT[:, c, :], ACT.Copy).then_inc(S["s_x2h"], 1)
            for m in range(DC):
                act.wait_ge(s_free[0], TILE_PLE + m + 1)
                act.wait_ge(s_free[1], TILE_PLE + m + 1)
                if m >= 2:
                    act.wait_ge(S["s_ace"], m - 1)
                else:
                    act.wait_ge(S["s_acy"], DC)
                nc.scalar.activation(sq2[m % 2][:, :], eT[:, m, :], ACT.Square).then_inc(S["s_sqe"], 1)
            for m in range(DC):
                n = TILE_GATE + m
                if m == 2:
                    act.wait_ge(S["s_nve"], 2)
                    own.up(nc.scalar.activation(nt2[:, :], nv2[:, :], ACT.Ln))
                    act.wait_ge(s_a, own.n)
                    nc.scalar.activation(rs_e[:, :], nt2[:, :], ACT.Exp, scale=-0.5).then_inc(S["s_y0e"], 1)
                if m >= 2:
                    act.wait_ge(S["s_fin"], m - 1)
                for half, (lo, hi) in enumerate(HALVES):
                    act.wait_ge(s_half[half], n + 1)
                    nc.scalar.activation(sg[m % 2][:, lo:hi], pj[half][:, 0:HALF], ACT.Sigmoid).then_inc(s_free[half], 1)
                if n + RING < TILES:
                    hi_part(n + RING)

        @block.vector
        def _(dve):
            own = Tally(s_v)
            used = Tally(s_used)
            V = nc.vector

            def link(ins):
                own.up(ins)
                dve.wait_ge(s_v, own.n)

            def lo_part(n):
                dve.wait_ge(s_hi, n + 1)
                k = chunks(n)
                V.tensor_tensor(w_lo[n % RING][:, 0:k, :], w_raw[n % RING][:, 0:k, :], w_hi[n % RING][:, 0:k, :].bitcast(F32), ALU.subtract).then_inc(s_lo, 1)

            def out_of_turn(*moves):
                dve.wait_ge(s_use, used.n + 1)
                b = tr[used.n % 2]
                for dst, src in moves:
                    last = V.tensor_copy(dst, src(b))
                used.up(last)

            def rsqrt(y, v, t, done):
                link(V.tensor_tensor(t, y, y, ALU.mult))
                link(V.tensor_tensor(t, t, v, ALU.mult))
                link(V.tensor_scalar(t, t, -0.5, 1.5, ALU.mult, ALU.add))
                V.tensor_tensor(y, y, t, ALU.mult).then_inc(done, 1)

            V.memset(ss[:, :], 1.0).then_inc(S["s_ssz"], 1)
            dve.wait_ge(S["s_wfhi"], 1)
            V.tensor_tensor(wf_lo[:, :, :], wf_raw[:, :, :], wf_hi[:, :, :].bitcast(F32), ALU.subtract).then_inc(S["s_wflo"], 1)
            dve.wait_ge(S["s_gt"], 1)
            V.tensor_copy(g_all[:, :], pj[0][:, 0:3 * DC]).then_inc(S["s_gv"], 1)
            dve.wait_ge(S["s_sqx"], NB + 1)
            V.tensor_scalar(nv[:, :], ss[:, :], 1.0 / D, EPS, ALU.mult, ALU.add).then_inc(S["s_nv"], 1)
            dve.wait_ge(S["s_y0"], 1)
            rsqrt(rs[:, :], nv[:, :], nt[:, :], S["s_rs"])
            dve.wait_ge(S["s_rs"], 1)
            for b in range(NB):
                V.tensor_scalar(xn[:, b, :], x_in[:, b, :], rs[:, b:b + 1], None, ALU.mult).then_inc(S["s_xn"], 1)
            V.tensor_scalar(xsn[:, :], xs_in[:, :], rs[0:DEC, NB:NB + 1], None, ALU.mult).then_inc(S["s_xn"], 1)
            lo_part(0)
            dve.wait_ge(S["s_gv"], 1)
            for c in range(DC):
                dve.wait_ge(S["s_hh"], c + 1)
                used.up(V.scalar_tensor_tensor(h_lo[:, c, 0:SEQ], tr[c % 2][:, :], gpre[:, c:c + 1], h_hi[:, c, 0:SEQ].bitcast(F32), ALU.mult, ALU.subtract))
            dve.wait_ge(S["s_xst"], 1)
            cols = lambda k: pv[0][:, k * DC * DEC:(k + 1) * DC * DEC].rearrange("p (c s) -> p c s", s=DEC)
            V.tensor_tensor(hs_raw[:, :, :], cols(0), gpre.unsqueeze(2).to_broadcast([P, DC, DEC]), ALU.mult).then_inc(S["s_hsr"], 1)
            V.tensor_copy(xT[:, :, SEQ:T], cols(1)).then_inc(S["s_xsv"], 1)
            dve.wait_ge(S["s_hsh"], 1)
            V.tensor_tensor(h_lo[:, :, SEQ:T], hs_raw[:, :, :], h_hi[:, :, SEQ:T].bitcast(F32), ALU.subtract).then_inc(S["s_hl"], 1)
            dve.wait_ge(s_const, 16)
            dve.wait_ge(s_small, 16 * 4)
            V.tensor_copy(identb[:, :], ident).then_inc(S["s_relb"], 1)
            c0, c1 = EARLY_COLS["causal"]
            V.tensor_copy(causalb[:, :], early[:, c0:c1]).then_inc(S["s_relb"], 1)
            V.memset(relb[32:33, :], NEG).then_inc(S["s_relb"], 1)
            dve.wait_ge(S["s_relb"], 3)
            for g in range(BG):
                last = V.tensor_copy(relb_rows[:, g, :, :], relb[:, g * BH:(g + 1) * BH].unsqueeze(1).to_broadcast([33, DEC, BH]))
            last.then_inc(S["s_relb"], 1)
            lo_part(1)
            for g in range(BG):
                dve.wait_ge(S["s_gent"], g + 1)
                V.tensor_copy(gen[g][:, :], (sc[0], sc[1], pj[1])[g][0:BH, 0:PITCH[g]]).then_inc(S["s_gen"], 1)
            dve.wait_ge(S["s_biasm"], 1)
            V.tensor_copy(bias_s[:, :], pj[0][0:DEC * BH, 3 * DC:3 * DC + sum(SLOTS) + BG]).then_inc(S["s_bias"], 1)
            lo_part(2)
            dve.wait_ge(S["s_fm"], 1)
            for half, (lo, hi) in enumerate(HALVES):
                V.tensor_scalar(fx[:, lo:hi], pv[half][0:AH, 0:HALF], bf[:, 0:1], None, ALU.add).then_inc(S["s_fx"], 1)
            dve.wait_ge(S["s_fe"], 1)
            V.tensor_scalar(fu[:, :], fe[:, :], 1.0, None, ALU.add).then_inc(S["s_fu"], 1)
            dve.wait_ge(S["s_fu"], 1)
            link(V.tensor_scalar(fd[:, :], fu[:, :], -1.0, None, ALU.add))
            link(V.tensor_tensor(fd[:, :], fe[:, :], fd[:, :], ALU.subtract))
            link(V.reciprocal(fr[:, :], fu[:, :]))
            link(V.tensor_tensor(fd[:, :], fd[:, :], fr[:, :], ALU.mult))
            dve.wait_ge(S["s_fl"], 1)
            link(V.tensor_tensor(fd[:, :], fa[:, :], fd[:, :], ALU.add))
            V.scalar_tensor_tensor(logf[:, :], fx[:, :], 0.0, fd[:, :], ALU.min, ALU.subtract).then_inc(S["s_logf"], 1)
            dve.wait_ge(S["s_logf"], 1)
            V.tensor_tensor_scan(cum[:, :], ones[0:AH, 0:1].to_broadcast([AH, SEQ]), logf[:, 0:SEQ], 0.0, ALU.mult, ALU.add).then_inc(S["s_cum"], 1)
            dve.wait_ge(S["s_cum"], 1)
            V.tensor_scalar(ncum[:, :], cum[:, :], -1.0, None, ALU.mult).then_inc(S["s_cum"], 1)
            for buf in (*q_aug, *k_aug):
                last = V.memset(buf[HD:HD + 2, :, :], 1.0)
            last.then_inc(S["s_clear"], 1)

            def evac1(n):
                dve.wait_ge(s_half[1], n + 1)
                r, j = divmod(n, 3)
                s = r % 2
                ps = pj[1]
                V.tensor_scalar(samp[:, n, :], ps[:, HALF - DEC:HALF], SCALE if j == 0 else 1.0, None, ALU.mult)
                if j == 0:
                    for hd in range(2):
                        last = V.tensor_scalar(q_aug[s][0:HD, hd, HALF:T], ps[hd * HD:(hd + 1) * HD, 0:HALF], SCALE, None, ALU.mult)
                elif j == 1:
                    for hd in range(2):
                        V.tensor_copy(k_aug[s][0:HD, hd, HALF:T], ps[hd * HD:(hd + 1) * HD, 0:HALF])
                    last = V.tensor_copy(kT[:, HALF:T], ps[:, 0:HALF])
                else:
                    last = V.tensor_copy(vT[:, HALF:T], ps[:, 0:HALF])
                last.then_inc(s_free[1], 1)

            def silu(n):
                dve.wait_ge(S["s_ge"], 2 * (n - TILE_Z) + 2)
                for half, (lo, hi) in enumerate(HALVES):
                    buf = zsil[:, n - TILE_Z, lo:hi]
                    V.tensor_tensor(buf, buf, pj[half][:, 0:HALF], ALU.mult).then_inc(s_free[half], 1)

            def maxima(r, i):
                hd, qb = units(r)[i]
                u = unit0[r] + i
                dve.wait_ge(s_sc, u + 1)
                if is_a(r):
                    if u >= 8:
                        dve.wait_ge(s_ex, u - 7)
                    V.tensor_reduce(nm_a[:, u % 8:u % 8 + 1], sc[u % 2][:, 0:(qb + 1) * P], AX.X, ALU.max, negate=True).then_inc(s_mx, 1)
                    return
                g, hp = divmod(r - 1 - ROUNDS_A, 2)
                h = 2 * hp + hd
                dve.wait_ge(s_ex, u - 1)
                if u == unit_a:
                    dve.wait_ge(s_use, use0[r])
                    dve.wait_ge(S["s_toep"], 16 * BG * BH)
                if qb is not None:
                    n = (min(qb, 1) + 1) * P
                    link(V.tensor_tensor_reduce(out=biased[u % 2][:, 0:n], in0=sc[u % 2][:, 0:n], in1=toep[0][:, h, 2 * P - n:2 * P], scale=1.0, scalar=-3e38,
                                                op0=ALU.add, op1=ALU.max, accum_out=mbuf[:, g, qb, h:h + 1]))
                    V.tensor_scalar(nm_b[:, 4 * (u % 2):4 * (u % 2) + 1], mbuf[:, g, qb, h:h + 1], -1.0, None, ALU.mult).then_inc(s_mx, 1)
                else:
                    for c in range(CLS):
                        cols = slice(c * P, (c + 1) * P)
                        ins = V.tensor_tensor_reduce(out=biased[u % 2][:, cols], in0=sc[u % 2][:, cols], in1=toep[g][:, h, :], scale=1.0, scalar=-3e38,
                                                     op0=ALU.add, op1=ALU.max, accum_out=mbuf[:, g, c, h:h + 1])
                    link(ins)
                    V.tensor_scalar(nm_b[:, 4 * (u % 2):4 * (u % 2) + 4], mbuf[:, g, :, h], -1.0, None, ALU.mult).then_inc(s_mx, 1)

            def probs_out(r, i):
                u = unit0[r] + i
                qb = units(r)[i][1]
                n = (qb + 1 if is_a(r) else CLS if qb is None else min(qb, 1) + 1) * P
                if u >= 2:
                    dve.wait_ge(s_pv, u - 1)
                out_of_turn((probT[u % 2][:, 0:n], lambda b: b[:, 0:n]))

            for r in range(ROUNDS + 1):
                nu = len(units(r))
                t = r - 1
                for i in range(12):
                    n = 3 * r + i // 4
                    if r and i == 0:
                        if r >= 2:
                            dve.wait_ge(s_kst, 16 * (r - 1))
                        out_of_turn((k_tok[:, :, :].rearrange("p b c -> p (b c)"), lambda b: b[:, :]))
                        if r >= 2:
                            dve.wait_ge(s_vst, 16 * (r - 1))
                            dve.wait_ge(s_pv, unit0[r])
                        out_of_turn((v_tok[:, :, :].rearrange("p b c -> p (b c)"), lambda b: b[:, :]))
                    if i < nu:
                        maxima(r, i)
                    if is_a(r) and 1 <= i <= nu:
                        u = unit0[r] + i - 1
                        dve.wait_ge(s_ex, u + 1)
                        if u >= 8:
                            dve.wait_ge(s_pve, u - 7)
                        V.reciprocal(r_a[:, u % 8:u % 8 + 1], l_a[:, u % 8:u % 8 + 1]).then_inc(s_rc, 1)
                    if r == 0 and 1 <= i <= DC:
                        out_of_turn((xT[:, i - 1, 0:SEQ], lambda b: b[:, :]))
                    if r == 0 and i == 9:
                        dve.wait_ge(s_use, used.n + 1)
                        b = tr[used.n % 2]
                        V.tensor_copy(lf_small[:, 0:NB, :].rearrange("p b h -> p (b h)"), b[:, 0:NB * AH])
                        used.up(V.tensor_copy(lf_small[0:DEC, NB, :], b[0:DEC, NB * AH:(NB + 1) * AH]))
                    if r == 0 and i == 10:
                        out_of_turn((lfT[:, :, :, :].rearrange("p g s h -> p h s g"), lambda b: b[:, 0:256].rearrange("p (h s g) -> p h s g", h=AH, g=PAGES)))
                        dve.wait_ge(S["s_suf"], 1)
                        V.tensor_copy(later[:, :], pv[0][:, 0:PAGES * DEC * AH]).then_inc(S["s_lsum"], 1)
                    if 1 <= i <= nu:
                        probs_out(r, i - 1)
                    if i % 4 == 3:
                        if n < TILE_G:
                            evac1(n)
                        lo_part(n + RING)
                    if i == 10 and r and is_a(r):
                        out_of_turn((oaT[:, t, 0:SEQ], lambda b: b[:, :]))

            def combine():
                dve.wait_ge(S["s_o0r"], 48)
                dve.wait_ge(s_ex, UNITS)
                flat = lambda b, g: b[:, g, :, :].rearrange("p c h -> p (c h)")
                mm, den = top_m, den_m
                link(V.tensor_tensor(mm[:, :], flat(mbuf, 0), flat(mbuf, 1), ALU.max))
                link(V.tensor_tensor(mm[:, :], mm[:, :], flat(mbuf, 2), ALU.max))
                V.tensor_tensor(mbuf[:, :, :, :].rearrange("p g c h -> p g (c h)"), mbuf[:, :, :, :].rearrange("p g c h -> p g (c h)"),
                                mm[:, :].unsqueeze(1).to_broadcast([P, BG, CLS * BH]), ALU.subtract).then_inc(S["s_md"], 1)
                dve.wait_ge(S["s_wexp"], 1)
                allg = lambda b: b[:, :, :, :].rearrange("p g c h -> p (g c h)")
                link(V.tensor_tensor(allg(lbuf), allg(lbuf), allg(mbuf), ALU.mult))
                link(V.tensor_reduce(den[:, :], lbuf[:, :, :, :].rearrange("p g c h -> p (c h) g"), AX.X, ALU.add))
                link(V.reciprocal(den[:, :], den[:, :]))
                link(V.tensor_tensor(mbuf[:, :, :, :].rearrange("p g c h -> p g (c h)"), mbuf[:, :, :, :].rearrange("p g c h -> p g (c h)"),
                                     den[:, :].unsqueeze(1).to_broadcast([P, BG, CLS * BH]), ALU.mult))
                dve.wait_ge(s_pve, UNITS)
                for g in range(BG):
                    o = obuf[:, g, :, :].rearrange("p c (h d) -> p (c h) d", d=HD)
                    link(V.tensor_tensor(o, o, flat(mbuf, g).unsqueeze(2).to_broadcast([P, CLS * BH, HD]), ALU.mult))
                fo = lambda g: obuf[:, g, :, :].rearrange("p c n -> p (c n)")
                link(V.tensor_tensor(fo(0), fo(0), fo(1), ALU.add))
                V.tensor_tensor(fo(0), fo(0), fo(2), ALU.add).then_inc(S["s_comb"], 1)

            red = [0]

            def sample_logits(s):
                for i in range(PAGES + BG):
                    k = red[0]
                    dve.wait_ge(S["s_prod"], k + 1)
                    if i < PAGES:
                        src, dst = prod[k % 2][:, :].rearrange("p (h d) -> p h d", d=HD), lg_a[:, i, s, :]
                    else:
                        n = SLOTS[i - PAGES]
                        src, dst = prod[k % 2][0:n, 0:BO].rearrange("p (h d) -> p h d", d=HD), lg_b[0:n, i - PAGES, s, :]
                    V.tensor_reduce(dst, src, AX.X, ALU.add).then_inc(S["s_red"], 1)
                    red[0] += 1

            def sample_softmax():
                dve.wait_ge(S["s_selfr"], 48)
                dve.wait_ge(s_use, used.n + 1)
                used.up(V.tensor_scalar(row_a[:, 0:PAST], tr[used.n % 2][0:DEC * AH, :], sm[:, 0:1], None, ALU.add))
                dve.wait_ge(s_used, used.n)
                V.tensor_reduce(sm[:, 5:6], row_a[:, :], AX.X, ALU.max, negate=True).then_inc(S["s_nma"], 1)
                dve.wait_ge(s_use, used.n + 1)
                b, at = tr[used.n % 2], 0
                for g in range(BG):
                    to = at + SLOTS[g]
                    V.tensor_tensor(row_b[:, to:to + 1], sm[0:32, 1 + g:2 + g], bias_s[:, to:to + 1], ALU.add)
                    last = V.tensor_tensor(row_b[:, at:to], b[0:32, at:to], bias_s[:, at:to], ALU.add)
                    at = to + 1
                used.up(last)
                dve.wait_ge(s_used, used.n)
                V.tensor_reduce(sm[0:32, 8:9], row_b[:, :], AX.X, ALU.max, negate=True).then_inc(S["s_nmb"], 1)
                dve.wait_ge(S["s_exa"], 1)
                link(V.reciprocal(sm[:, 7:8], sm[:, 6:7]))
                V.tensor_scalar(row_a[:, :], row_a[:, :], sm[:, 7:8], None, ALU.mult).then_inc(S["s_pn"], 1)
                dve.wait_ge(S["s_exb"], 1)
                link(V.reciprocal(sm[0:32, 10:11], sm[0:32, 9:10]))
                V.tensor_scalar(row_b[:, :], row_b[:, :], sm[0:32, 10:11], None, ALU.mult).then_inc(S["s_pn"], 1)
                dve.wait_ge(S["s_pn"], 2)
                V.tensor_scalar(dsel_a[:, :], cst("row_a", 64), row_a[:, PAST:PAST + 1], None, ALU.mult).then_inc(S["s_ds"], 1)
                at = 0
                for g in range(BG):
                    at += SLOTS[g]
                    V.tensor_scalar(dsel_b[:, g, :], cst("row_b", 32), row_b[:, at:at + 1], None, ALU.mult).then_inc(S["s_ds"], 1)
                    at += 1

            def sample_selves():
                dve.wait_ge(S["s_pz"], 2)
                rows = lambda b, g0, g1, n, h: b[0:n, g0 * DEC * h:g1 * DEC * h].rearrange("p (g s h) -> p g s h", s=DEC, h=h)
                out_of_turn(*[(pTa[:, :, s, s, :], lambda b, s=s: rows(b, 0, PAGES, P, AH)[:, :, s, :]) for s in range(DEC)])
                out_of_turn(*[(pTb[:, 0:2, s, s, :], lambda b, s=s: rows(b, 0, 2, P, BH)[:, :, s, :]) for s in range(DEC)],
                            *[(pTb[0:SLOTS[2], 2:3, s, s, :], lambda b, s=s: rows(b, 2, 3, SLOTS[2], BH)[:, :, s, :]) for s in range(DEC)])
                dve.wait_ge(S["s_dm"], 1)
                V.tensor_copy(d_a[:, :], pv[0][0:DEC, 0:64]).then_inc(S["s_dv"], 1)
                V.tensor_copy(d_b[:, :, :].rearrange("s g x -> s (g x)"), pv[0][0:DEC, 64:160]).then_inc(S["s_dv"], 1)

            def result_out(m):
                dve.wait_ge(S["s_tt"], m + 1)
                if m >= 2:
                    dve.wait_ge(S[f"s_yst{m % 2}"], 16 * (m // 2))
                V.tensor_copy(tok_out[m % 2][:, :, :].rearrange("p b c -> p (b c)"), sc[m % 2][:, :]).then_inc(S["s_tte"], 1)

            for n in range(TILE_G + 3, TILE_BR):
                t = n - TILE_G - 3
                if n >= TILE_Z:
                    silu(n)
                lo_part(n + RING)
                if t == 0:
                    combine()
                if t == 1:
                    for cc in range(2):
                        out_of_turn((obT[:, cc, 0:SEQ].rearrange("p (i c) -> p c i", c=CLS), lambda b: b[:, :].rearrange("p (c i) -> p c i", c=CLS)))
                    dve.wait_ge(s_kst, 16 * ROUNDS)
                    dve.wait_ge(s_vst, 16 * ROUNDS)
                    for k in range(8):
                        w = min(4, 3 * ROUNDS - 4 * k)
                        out_of_turn((st[:, 4 * k:4 * k + w, :].rearrange("p r c -> p (r c)"), lambda b: b[0:DEC, 0:w * P]))
                    dve.wait_ge(s_used, used.n)
                    stv = st[:, :, :].rearrange("s (r j) c -> s j r c", j=3)
                    link(V.tensor_tensor(self_p[:, :, :], stv[:, 0], stv[:, 1], ALU.mult))
                    heads = self_p[:, :, :].rearrange("s r (h d) -> s (r h) d", d=HD)
                    link(V.tensor_reduce(self_a[:, :], heads[:, 0:AH], AX.X, ALU.add))
                    for g in range(BG):
                        ins = V.tensor_reduce(self_b[:, :, g], heads[:, AH + BH * g:AH + BH * (g + 1)], AX.X, ALU.add)
                    ins.then_inc(S["s_selfp"], 1)
                if 3 <= t < 3 + DEC:
                    sample_logits(t - 3)
                if t == 11:
                    dve.wait_ge(S["s_red"], 7 * DEC)
                    la = lg_a[:, :, :, :].rearrange("p g s h -> p (g s h)")
                    V.tensor_tensor(la, la, later[:, :], ALU.add).then_inc(S["s_lga"], 1)
                if t == 12:
                    sample_softmax()
                if t == 13:
                    sample_selves()

            dve.wait_ge(S["s_os"], 1)
            heads = lambda b, n: b.rearrange("r (h d) -> r h d", h=n)
            V.tensor_tensor(heads(os_a[:, :], AH), heads(sc[0][0:DEC * AH, :], AH), cst("head_a", 64).unsqueeze(2).to_broadcast([64, AH, HD]), ALU.mult).then_inc(S["s_osm"], 1)
            V.tensor_tensor(heads(os_b[:, :], BH), heads(sc[1][0:DEC * BH, 0:BO], BH), cst("head_b", 32).unsqueeze(2).to_broadcast([32, BH, HD]), ALU.mult).then_inc(S["s_osm"], 1)
            dve.wait_ge(S["s_ot"], 1)
            V.tensor_copy(oaT[:, :, SEQ:T], pv[0][:, 0:32].rearrange("p (c s) -> p c s", s=DEC))
            V.tensor_copy(obT[:, :, SEQ:T], pv[0][:, 32:48].rearrange("p (c s) -> p c s", s=DEC)).then_inc(S["s_ov"], 1)
            dve.wait_ge(S["s_ov"], 1)
            for i in range(6):
                if i >= 2:
                    dve.wait_ge(S["s_ogl"], i - 1)
                dve.wait_ge(s_free[1], TILE_BR)
                src = oaT[:, i, :] if i < 4 else obT[:, i - 4, :]
                ins = V.tensor_tensor(og_raw[i % 2][:, :], src, zsil[:, i, :], ALU.mult)
                ins.then_inc(S["s_ogr"], 1)
            for m in range(DC):
                n = TILE_BR + m
                for half, (lo, hi) in enumerate(HALVES):
                    dve.wait_ge(s_half[half], n + 1)
                    a, b = gsig[:, m, lo:hi], gsig[:, DC + m, lo:hi]
                    V.tensor_tensor(a, a, pj[half][:, 0:HALF], ALU.mult)
                    own.up(V.tensor_tensor(b, b, sc[half][:, 0:HALF], ALU.mult))
                    dve.wait_ge(s_v, own.n)
                    last = V.tensor_tensor(a, a, b, ALU.add)
                    last.then_inc(s_free[half], 1)
                lo_part(n + RING)
            dve.wait_ge(S["s_ptr"], 2)
            dve.wait_ge(s_use, used.n + 1)
            V.tensor_copy(acc_e[:, 0:SEQ], pv[0][:, :]).then_inc(S["s_pte"], 1)
            V.tensor_copy(acc_y[:, 0:SEQ], pv[1][:, :]).then_inc(S["s_pte"], 1)
            b = tr[used.n % 2]
            V.tensor_copy(acc_e[:, SEQ:T], b[:, 0:DEC])
            used.up(V.tensor_copy(acc_y[:, SEQ:T], b[:, DEC:2 * DEC]))
            for c, src in enumerate((acc_e, acc_y)):
                dve.wait_ge(S["s_pth"], c + 1)
                V.tensor_tensor(pT_lo[:, c, :], src[:, :], pT_hi[:, c, :].bitcast(F32), ALU.subtract).then_inc(S["s_ptl"], 1)
            for m in range(DC):
                n = TILE_OUT + m
                dve.wait_ge(s_half[1], n + 1)
                V.tensor_copy(yT[:, m, HALF:T], pj[1][:, 0:HALF]).then_inc(s_free[1], 1)
                lo_part(n + RING)

            def norm(rs_, nv_done, y0, done, ready):
                dve.wait_ge(S[ready], 1)
                for half, (lo, hi) in enumerate(HALVES):
                    V.tensor_scalar(nv2[:, lo:hi], pv[half][:, 0:HALF], 1.0 / D, EPS, ALU.mult, ALU.add).then_inc(S[nv_done], 1)
                dve.wait_ge(S[y0], 1)
                rsqrt(rs_[:, :], nv2[:, :], nt2[:, :], S[done])
                dve.wait_ge(S[done], 1)

            for m in range(DC):
                n = TILE_PLE + m
                dve.wait_ge(s_half[1], n + 1)
                V.tensor_copy(eT[:, m, HALF:T], pj[1][:, 0:HALF]).then_inc(s_free[1], 1)
                lo_part(n + RING)
                if m == 2:
                    norm(rs_y, "s_nvy", "s_y0y", "s_rsy", "s_ssy")
                if 3 <= m <= 6:
                    for c in range(2 * (m - 3), 2 * (m - 3) + 2):
                        link(V.scalar_tensor_tensor(yT[:, c, :], yT[:, c, :], gpost[:, c:c + 1], rs_y[:, :], ALU.mult, ALU.mult))
                        V.tensor_tensor(xT[:, c, :], xT[:, c, :], yT[:, c, :], ALU.add).then_inc(S["s_xsum"], 1)

            def final(m):
                n = TILE_GATE + m
                link(V.scalar_tensor_tensor(eT[:, m, :], eT[:, m, :], gple[:, m:m + 1], rs_e[:, :], ALU.mult, ALU.mult))
                dve.wait_ge(s_free[0], n + 1)
                dve.wait_ge(s_free[1], n + 1)
                link(V.tensor_tensor(eT[:, m, :], sg[m % 2][:, :], eT[:, m, :], ALU.mult))
                if m >= 2:
                    dve.wait_ge(S["s_tts"], m - 1)
                V.tensor_tensor(fin[m % 2][:, :], xT[:, m, :], eT[:, m, :], ALU.add).then_inc(S["s_fin"], 1)

            for m in range(DC):
                n = TILE_GATE + m
                if m == 2:
                    norm(rs_e, "s_nve", "s_y0e", "s_rse", "s_sse")
                    final(0)
                    final(1)
                if n + RING < TILES:
                    lo_part(n + RING)
                if m >= 2:
                    final(m)
                    result_out(m - 2)
            result_out(DC - 2)
            result_out(DC - 1)
            dve.wait_ge(S["s_tts"], DC)
            for i in range(2):
                V.tensor_copy(toks_out[:, 512 * i:512 * (i + 1)], pv[i][0:DEC, :]).then_inc(S["s_ttse"], 1)


_INS = ["x_prompt", "x_sample", "cache_a_kv", "cache_a_logf", "cache_b0_kv", "cache_b1_kv", "cache_b2_kv", "page_table",
        "p_prompt", "p_sample", "rel_bias", "g_pre", "w_in", "b_f", "w_br_a", "w_br_b", "w_out", "g_post", "w_ple", "g_ple", "w_ple_gate"]
_OUTS = [(1, SEQ, D), (DEC, 1, D), (1, 1, SEQ, 2, AH, HD), (1, 1, SEQ, AH),
         (1, 1, 128, 2, BH, HD), (1, 1, SEQ, 2, BH, HD), (1, 1, SEQ, 2, BH, HD),
         (1, DEC, 1, 2, AH, HD), (1, DEC, 1, AH),
         (1, DEC, 128, 2, BH, HD), (1, DEC, PAST, 2, BH, HD), (1, DEC, PAST, 2, BH, HD)]


def kernel(**inputs):
    import concourse.bacc as _bacc
    from concourse.bass_utils import run_bass_kernel_spmd as _run

    nc = _bacc.Bacc("TRN2", target_bir_lowering=False, num_devices=1)
    arrays, args = {}, {}
    for name in _INS:
        a = np.ascontiguousarray(inputs[name])
        arrays[f"in_{name}_dram"] = a
        args[name] = nc.dram_tensor(f"in_{name}_dram", a.shape, mybir.dt.from_np(a.dtype), kind="ExternalInput").ap()
    consts = []
    for name, a in (("const", CONST), ("tables", TABLES), ("early", EARLY)):
        arrays[f"in_{name}_dram"] = a
        consts.append(nc.dram_tensor(f"in_{name}_dram", a.shape, F32, kind="ExternalInput").ap())
    outs = [nc.dram_tensor(f"out_{i}_dram", shape, F32, kind="ExternalOutput").ap() for i, shape in enumerate(_OUTS)]
    build(nc, args, outs, consts)
    r = _run(nc, [arrays], core_ids=[0])
    return tuple(r.results[0][f"out_{i}_dram"] for i in range(len(_OUTS)))
```

```python
from contextlib import ExitStack

import numpy as np

import concourse.bass as bass
from concourse import mybir

F32 = mybir.dt.float32
F32R = mybir.dt.float32r
BF16 = mybir.dt.bfloat16
I32 = mybir.dt.int32
ALU = mybir.AluOpType
ACT = mybir.ActivationFunctionType
AX = mybir.AxisListType

P = 128
D = 1024
DC = D // P
SEQ = 512
NB = SEQ // P
DEC = 8
T = SEQ + DEC
HALF = T // 2
HALVES = ((0, HALF), (HALF, T))
HD = 64
AH = 8
AW = AH * HD
BG, BH = 3, 4
DIL = (1, 4, 16)
WIN = (128, 512, 2048)
BQ = BG * BH * HD
BO = BH * HD
PLE = 256
PAGES, PAGE = 4, 128
PAST = PAGES * PAGE
POOL_PAGES = 40
CLS = 4
SCALE = HD ** -0.5
EPS = 1e-6
NEG = -1e30

COL_QA, COL_KA, COL_VA = 0, AW, 2 * AW
COL_F = 3 * AW
COL_ZA = COL_F + AH
COL_QB = COL_ZA + AW
COL_KB, COL_VB = COL_QB + BQ, COL_QB + 2 * BQ
COL_ZB = COL_QB + 3 * BQ
COL_GA = COL_ZB + BO
IN_W = COL_GA + 2 * D

RING = 3
PRODS = 4
ROUNDS_A, ROUNDS_B = AH // 2, BG * BH // 2
ROUNDS = ROUNDS_A + ROUNDS_B
N_G, N_Z = 16, 6
TILE_G = 3 * ROUNDS
TILE_Z = TILE_G + N_G
TILE_BR = TILE_Z + N_Z
TILE_OUT = TILE_BR + DC
TILE_PLE = TILE_OUT + DC
TILE_GATE = TILE_PLE + DC
TILES = TILE_GATE + DC

TOEP = (256, 128, 128)
PITCH = (384, 256, 256)
SLOTS = (128, 128, 32)


def bucket(dist):
    d = np.maximum(dist, 1).astype(np.float32)
    large = 16 + (np.log(d / np.float32(16)) / np.float32(np.log(2048 / 16)) * np.float32(16)).astype(np.int32)
    return np.where(dist < 16, dist, np.minimum(large, 31))


CONST_COLS = {}
TABLE_COLS = {}
EARLY_COLS = {}


def constants():
    parts, tables, early = [], [], []

    def add(name, m, to=parts, cols=CONST_COLS):
        full = np.zeros((33 if to is tables else P, m.shape[1]), np.float32)
        full[:m.shape[0]] = m
        at = sum(x.shape[1] for x in to)
        cols[name] = (at, at + m.shape[1])
        to.append(full)

    i = np.arange(P)
    add("ident", np.eye(P))
    add("ones", np.ones((P, P)))
    add("later", (i[:, None] > i[None, :]) * 1.0, early, EARLY_COLS)
    add("causal", np.where(i[None, :] <= i[:, None], 0.0, NEG), early, EARLY_COLS)
    add("row_a", (np.arange(64)[:, None] // AH == np.arange(DEC)) * 1.0)
    add("row_b", (np.arange(32)[:, None] // BH == np.arange(DEC)) * 1.0)
    add("head_a", (np.arange(64)[:, None] % AH == np.arange(AH)) * 1.0)
    add("head_b", (np.arange(32)[:, None] % BH == np.arange(BH)) * 1.0)
    for g in range(BG):
        y = np.arange(PITCH[g])
        dist = 255 - y if g == 0 else (127 - y) * CLS
        seen = (dist >= 0) & (dist <= WIN[g]) & (dist % DIL[g] == 0)
        hot = np.zeros((33, PITCH[g]))
        hot[np.where(seen, bucket(np.maximum(dist, 0)), 32), y] = 1
        add(f"toep{g}", hot, tables, TABLE_COLS)
    for g in range(BG):
        n = SLOTS[g]
        dist = np.concatenate([(n - np.arange(n)) * DIL[g], [0]])
        hot = np.zeros((33, n + 1))
        hot[bucket(dist), np.arange(n + 1)] = 1
        add(f"slots{g}", hot, tables, TABLE_COLS)
    return tuple(np.concatenate(x, axis=1) for x in (parts, tables, early))


CONST, TABLES, EARLY = constants()


class Tally:

    def __init__(self, sem):
        self.sem, self.n = sem, 0

    def up(self, ins):
        ins.then_inc(self.sem, 1)
        self.n = self.n + 1
        return ins


def build(nc, A, O, const_in):
    with ExitStack() as ctx:
        cursor = [nc.sbuf_base + 31 & ~31]
        top = [cursor[0]]

        def sb(name, shape, dt=F32, at=None):
            size = int(np.prod(shape[1:])) * (2 if dt == BF16 else 4)
            size = size + 31 & ~31
            if at is not None:
                cursor[0] = at
            t = nc.alloc_sbuf_tensor_at(name, shape, dt, offset=cursor[0])
            cursor[0] += size
            top[0] = max(top[0], cursor[0])
            return t

        def bank(name):
            return ctx.enter_context(nc.psum_tensor(name, [P, 512], F32))

        def sem(name):
            return ctx.enter_context(nc.semaphore(name))

        def sems(name, n):
            return [sem(f"{name}{i}") for i in range(n)]

        pj = [bank("pj0"), bank("pj1")]
        sc = [bank("sc0"), bank("sc1")]
        tr = [bank("tr0"), bank("tr1")]
        pv = [bank("pv0"), bank("pv1")]

        const = sb("const", [P, CONST.shape[1]])
        cst = lambda name, rows=P: const[0:rows, CONST_COLS[name][0]:CONST_COLS[name][1]]
        ident, ones = cst("ident"), cst("ones")
        identb = sb("identb", [P, P], BF16)
        causalb = sb("causalb", [P, P], BF16)
        g_all = sb("g_all", [P, 3 * DC])
        gpre, gpost, gple = (g_all[:, i * DC:(i + 1) * DC] for i in range(3))
        xT = sb("xT", [P, DC, T])
        h_hi, h_lo = sb("h_hi", [P, DC, T], F32R), sb("h_lo", [P, DC, T], F32R)
        w_raw = [sb(f"w_raw{i}", [P, DC, P]) for i in range(RING)]
        w_hi = [sb(f"w_hi{i}", [P, DC, P], F32R) for i in range(RING)]
        w_lo = [sb(f"w_lo{i}", [P, DC, P], F32R) for i in range(RING)]
        samp = sb("samp", [P, 3 * ROUNDS, DEC])
        at_lg = cursor[0]
        lg_a = sb("lg_a", [P, PAGES, DEC, AH])
        lg_b = sb("lg_b", [P, BG, DEC, BH])
        later = sb("later_sums", [P, PAGES * DEC * AH])
        lf_small = sb("lf_small", [P, NB + 1, AH])
        at_o = cursor[0]
        oaT, obT = sb("oaT", [P, AW // P, T]), sb("obT", [P, BO // P, T])
        at_z = cursor[0]
        zsil = sb("zsil", [P, N_Z, T])
        og_hi, og_lo = sb("og_hi", [P, 6, T], F32R, at=at_o), sb("og_lo", [P, 6, T], F32R, at=at_z)
        at_g = cursor[0]
        gsig = sb("gsig", [P, N_G, T])
        after_g = cursor[0]
        yT, eT = (sb("yT", [P, DC, T], at=at_g), sb("eT", [P, DC, T], at=at_g + DC * T * 4))
        x_in = sb("x_in", [P, NB, D], at=at_g)
        xs_in = sb("xs_in", [DEC, D])
        early = sb("early", [P, EARLY.shape[1]])
        lf_rows = sb("lf_rows", [DEC * PAGES, PAGE * AH])
        lfT = sb("lfT", [P, PAGES, DEC, AH])
        assert cursor[0] <= after_g
        cursor[0] = after_g
        at_2 = cursor[0]
        mbuf, lbuf = sb("mbuf", [P, BG, CLS, BH]), sb("lbuf", [P, BG, CLS, BH])
        obuf = sb("obuf", [P, BG, CLS, BO])
        toep = [sb(f"toep{g}", [P, BH, TOEP[g]]) for g in range(BG)]
        at_3 = cursor[0]
        q_aug = [sb(f"q_aug{i}", [HD + 2, 2, T]) for i in range(2)]
        k_aug = [sb(f"k_aug{i}", [HD + 2, 2, T]) for i in range(2)]
        kT, vT = sb("kT", [P, T]), sb("vT", [P, T])
        k_tok, v_tok = sb("k_tok", [P, NB, P]), sb("v_tok", [P, NB, P])
        prob = [sb(f"prob{i}", [P, 512]) for i in range(2)]
        probT = [sb(f"probT{i}", [P, 512]) for i in range(2)]
        at_4 = cursor[0]
        biased = [sb(f"biased{i}", [P, 512]) for i in range(2)]
        o_tok = sb("o_tok", [P, NB, P], at=at_4)
        top_m, den_m = sb("top_m", [P, CLS * BH], at=at_4), sb("den_m", [P, CLS * BH])
        cursor[0] = at_4 + 4096
        l_a, r_a, nm_a = sb("l_a", [P, 8]), sb("r_a", [P, 8]), sb("nm_a", [P, 8])
        nm_b = sb("nm_b", [P, 8])
        wf_raw, wf_hi, wf_lo = sb("wf_raw", [P, DC, AH]), sb("wf_hi", [P, DC, AH], F32R), sb("wf_lo", [P, DC, AH], F32R)
        bf = sb("bf", [AH, 1])
        h_raw = sb("h_raw", [P, DC, T], at=at_3)
        sq_junk = sb("sq_junk", [DEC, D])
        ss, rs, nv, nt = (sb(x, [P, NB + 1]) for x in ("ss", "rs", "nv", "nt"))
        g_rows = sb("g_rows", [3 * DC, P])
        tables = sb("tables", [33, TABLES.shape[1]])
        relb = sb("relb", [33, 12])
        relb_rows = sb("relb_rows", [33, BG, DEC, BH])
        assert cursor[0] <= at_4
        fx = sb("fx", [AH, T], at=at_2)
        fa, fe, fu, fd, fr = (sb(n, [AH, T]) for n in ("fa", "fe", "fu", "fd", "fr"))
        assert cursor[0] <= at_2 + 384 + CLS * BG * BO * 4
        gen = [sb(f"gen{g}", [BH, PITCH[g]], at=at_2 + 384 + CLS * BG * BO * 4 if g == 0 else None) for g in range(BG)]
        assert cursor[0] <= at_3
        st = sb("st", [DEC, 3 * ROUNDS, P], at=at_3)
        kv_a = [sb(f"kv_a{i}", [P, PAGES, AW]) for i in range(2)]
        kv_b = [sb(f"kv_b{i}", [P, BG, BO]) for i in range(2)]
        self_p = sb("self_p", [DEC, ROUNDS, P], at=at_3 + 3 * ROUNDS * P * 4 + PAGES * AW * 4)
        qbc = [sb(f"qbc{i}", [P, AW + BQ], at=at_2 + i * 4 * (AW + BQ)) for i in range(2)]
        prod = [sb(f"prod{i}", [P, AW]) for i in range(PRODS)]
        prod_v = sb("prod_v", [P, AW])
        assert cursor[0] <= at_3
        cursor[0] = top[0]
        bias_s = sb("bias_s", [DEC * BH, sum(SLOTS) + BG])
        logf = sb("logf", [AH, T])
        cum, ncum = sb("cum", [AH, SEQ], at=at_4), sb("ncum", [AH, SEQ], at=at_4 + 2048)
        cursor[0] = top[0]
        pt = sb("pt", [1, DEC * PAGES], I32)
        sm = sb("sm", [DEC * AH, 16])
        self_a, self_b = sb("self_a", [DEC, AH]), sb("self_b", [DEC, BH, BG])
        row_a = sb("row_a", [DEC * AH, PAST + 1], at=at_2)
        row_b = sb("row_b", [DEC * BH, sum(SLOTS) + BG])
        pTa = sb("pTa", [P, PAGES, DEC, DEC, AH])
        pTb = sb("pTb", [P, BG, DEC, DEC, BH])
        dsel_a, dsel_b = sb("dsel_a", [64, DEC]), sb("dsel_b", [32, BG, DEC])
        d_a, d_b = sb("d_a", [DEC, 64]), sb("d_b", [DEC, BG, 32])
        os_a, os_b = sb("os_a", [DEC * AH, AW]), sb("os_b", [DEC * BH, BO])
        og_s = sb("og_s", [P, 6, DEC])
        og_raw = [sb("og_raw0", [P, SEQ]), None]
        assert cursor[0] <= at_3
        og_raw[1] = sb("og_raw1", [P, SEQ], at=at_lg)
        assert cursor[0] <= at_lg + 4 * (PAGES * DEC * AH + BG * DEC * BH + PAGES * DEC * AH)
        pT_hi, pT_lo = sb("pT_hi", [P, 2, T], F32R, at=at_3), sb("pT_lo", [P, 2, T], F32R)
        p_in, ps_in = sb("p_in", [P, NB, PLE]), sb("ps_in", [DEC, PLE])
        assert cursor[0] <= top[0], (cursor[0], top[0])
        sq2 = [sb("sq2_0", [P, T]), sb("sq2_1", [P, T])]
        acc_y, acc_e, rs_y, rs_e, nv2, nt2 = (sb(n, [P, T]) for n in ("acc_y", "acc_e", "rs_y", "rs_e", "nv2", "nt2"))
        assert cursor[0] <= top[0]
        sg = [sb("sg0", [P, T], at=at_2), sb("sg1", [P, T])]
        fin = [sb(f"fin{i}", [P, T]) for i in range(2)]
        tok_out = [sb(f"tok_out{i}", [P, NB, P]) for i in range(2)]
        toks_out = sb("toks_out", [DEC, D])
        assert cursor[0] <= top[0], (cursor[0], top[0])

        c_dram = nc.dram_tensor("c_dram", [2, AH, SEQ], F32).ap()
        toep_dram = [nc.dram_tensor(f"toep_dram{g}", [BH, P * PITCH[g]], F32).ap() for g in range(BG)]
        o0_dram = nc.dram_tensor("o0_dram", [SEQ, BO], F32).ap()
        m0_dram, l0_dram = (nc.dram_tensor(n, [SEQ, BH], F32).ap() for n in ("m0_dram", "l0_dram"))
        q_dram = nc.dram_tensor("q_dram", [DEC, ROUNDS * P], F32).ap()
        selfa_dram = nc.dram_tensor("selfa_dram", [DEC, AH], F32).ap()
        selfb_dram = nc.dram_tensor("selfb_dram", [DEC, BH * BG], F32).ap()
        lfn_dram = nc.dram_tensor("lfn_dram", [DEC, AH], F32).ap()

        (yp, ys, akv_p, alf_p, b0_p, b1_p, b2_p, akv_s, alf_s, b0_s, b1_s, b2_s) = O
        b_p, b_s = (b0_p, b1_p, b2_p), (b0_s, b1_s, b2_s)
        caches = (A["cache_b0_kv"], A["cache_b1_kv"], A["cache_b2_kv"])
        w_in = A["w_in"][0].rearrange("(c p) n -> p c n", p=P)
        w_br_a = A["w_br_a"][0].rearrange("(c p) n -> p c n", p=P)
        w_br_b = A["w_br_b"][0].rearrange("(c p) n -> p c n", p=P)
        w_out = A["w_out"][0].rearrange("(c p) n -> p c n", p=P)
        w_ple = A["w_ple"][0].rearrange("(c p) n -> p c n", p=P)
        w_gate = A["w_ple_gate"][0].rearrange("(c p) n -> p c n", p=P)

        def weight_parts(n):
            if n < TILE_G:
                r, j = n // 3, n % 3
                if r < ROUNDS_A:
                    col = (COL_QA, COL_KA, COL_VA)[j] + r * P
                else:
                    col = (COL_QB, COL_KB, COL_VB)[j] + (r - ROUNDS_A) * P
                return [(w_in[:, :, col:col + P], 0, DC)]
            if n < TILE_Z:
                col = COL_GA + (n - TILE_G) * P
                return [(w_in[:, :, col:col + P], 0, DC)]
            if n < TILE_BR:
                z = n - TILE_Z
                col = COL_ZA + z * P if z < AW // P else COL_ZB + (z - AW // P) * P
                return [(w_in[:, :, col:col + P], 0, DC)]
            m = (n - TILE_BR) % DC
            cols = slice(m * P, (m + 1) * P)
            if n < TILE_OUT:
                return [(w_br_a[:, :, cols], 0, 4), (w_br_b[:, :, cols], 4, 2)]
            if TILE_PLE <= n < TILE_GATE:
                return [(w_ple[:, :, cols], 0, 2)]
            return [((w_out if n < TILE_GATE else w_gate)[:, :, cols], 0, DC)]

        def chunks(n):
            return sum(k for _, _, k in weight_parts(n))

        landed_at, total = {}, [0] * RING
        for n in range(TILES):
            total[n % RING] += 16 * len(weight_parts(n))
            landed_at[n] = total[n % RING]

        def units(r):
            if r == 0:
                return []
            return [(hd, qb) for qb in range(NB) for hd in range(2)] if r <= ROUNDS_A + 2 else [(0, None), (1, None)]

        USE_LOGF, USE_LF = DC, DC + 1
        unit0, use0, u, k = {}, {}, 0, DC + 2
        for r in range(1, ROUNDS + 1):
            unit0[r], use0[r] = u, k
            u += len(units(r))
            k += 2 + len(units(r)) + (r <= ROUNDS_A)
        UNITS, USE_SAMP, USE_COMBINE = u, k, k + 8
        USE_ROW = USE_COMBINE + 2
        pt_use = {unit0[r] + i: use0[r] + 2 + i for r in unit0 for i in range(len(units(r)))}
        is_a = lambda r: r <= ROUNDS_A
        unit_a = 8 * ROUNDS_A

        s_const, s_small, s_pt, s_g, s_xs, s_wf, s_cd = (sem(n) for n in ("s_const", "s_small", "s_pt", "s_g", "s_xs", "s_wf", "s_cd"))
        s_x = sems("s_x", NB)
        s_w = sems("s_w", RING)
        s_crow = sems("s_crow", 2)
        s_hi, s_lo = sem("s_hi"), sem("s_lo")
        s_half, s_free = sems("s_half", 2), sems("s_free", 2)
        s_use, s_used = sem("s_use"), sem("s_used")
        s_sc, s_mx, s_ex, s_rc, s_pv, s_pve = (sem(n) for n in ("s_sc", "s_mx", "s_ex", "s_rc", "s_pv", "s_pve"))
        s_kst, s_vst = sem("s_kst"), sem("s_vst")
        s_v = sem("s_v")
        s_a = sem("s_a")
        s_p = sem("s_p")
        names = ("s_relb s_gt s_gv s_ssz s_sqx s_nv s_y0 s_rs s_rsb s_hraw s_hh s_hl s_wfhi s_wflo s_gen s_gent s_gend s_toep "
                 "s_biasm s_bias s_fm s_fx s_fe s_fu s_fl s_logf s_cum s_clear s_xst s_xsv s_copy s_ge s_g3 "
                 "s_o0 s_o0r s_md s_wexp s_cw s_comb s_selfp s_sst s_qd s_qb0 s_qb1 s_kp0 s_kp1 s_bk0 s_bk1 s_prod s_prodv s_red s_pz "
                 "s_lfr s_suf s_lsum s_lga s_selfr s_nma s_nmb s_exa s_exb s_pn s_dm s_dv s_ds s_samp s_os s_osm s_ot s_ov s_slfd "
                 "s_ogr s_ogh s_ogl s_ogsr s_ogsh s_ogsl s_mh s_ml s_pin s_ptr s_pte s_pth s_ptl s_sqe s_ace s_sqy s_acy "
                 "s_sse s_nve s_y0e s_rse s_ssy s_nvy s_y0y s_rsy s_xsum s_x2h s_x2l s_lop s_fin s_tt s_tte s_tts s_ttse s_yst0 s_yst1 s_ysst s_lfst").split()
        S = {n: sem(n) for n in names}

        def wait_parts(e, n):
            if TILE_PLE <= n < TILE_GATE:
                e.wait_ge(S["s_lop"], n - TILE_PLE + 1)
            else:
                e.wait_ge(s_lo, n + 1 - (DC if n >= TILE_GATE else 0))

        block = ctx.enter_context(nc.Block())

        @block.sync
        def _(sp):
            def load(n):
                if n >= RING:
                    wait_parts(sp, n - RING)
                for src, c0, nk in weight_parts(n):
                    sp.dma_start(w_raw[n % RING][:, c0:c0 + nk, :], src).then_inc(s_w[n % RING], 16)

            sp.dma_start(const[:, :], const_in[0]).then_inc(s_const, 16)
            sp.dma_start(xs_in[:, :], A["x_sample"].rearrange("s o d -> (s o) d")).then_inc(s_xs, 16)
            for b in range(NB):
                sp.dma_start(x_in[:, b, :], A["x_prompt"][0, b * P:(b + 1) * P, :]).then_inc(s_x[b], 16)
            sp.dma_start(wf_raw[:, :, :], w_in[:, :, COL_F:COL_F + AH]).then_inc(s_wf, 16)
            for n in range(RING):
                load(n)
            sp.wait_ge(s_pt, 16)
            for i in range(DEC * PAGES):
                page = sp.value_load(pt[0:1, i:i + 1], min_val=0, max_val=POOL_PAGES - 1)
                sp.dma_start(lf_rows[i:i + 1, :], A["cache_a_logf"][0, bass.ds(page, 1), :, :].rearrange("o t h -> o (t h)")).then_inc(S["s_lfr"], 16)
            for n in range(RING, 2 * RING):
                load(n)
            sp.wait_ge(S["s_cum"], 2)
            sp.dma_start(c_dram[0], cum[:, :]).then_inc(s_cd, 16)
            sp.dma_start(c_dram[1], ncum[:, :]).then_inc(s_cd, 16)
            sp.wait_ge(s_cd, 32)
            sp.wait_ge(S["s_clear"], 1)
            for r in range(ROUNDS_A):
                for n in range(3 * r + 3, 3 * r + 5):
                    if r:
                        load(n)
                if r >= 2:
                    sp.wait_ge(s_sc, 8 * (r - 1))
                s = r % 2
                sp.dma_start(q_aug[s][HD + 1:HD + 2, :, 0:SEQ], c_dram[0:1, 2 * r:2 * r + 2, :]).then_inc(s_crow[s], 16)
                sp.dma_start(k_aug[s][HD:HD + 1, :, 0:SEQ], c_dram[1:2, 2 * r:2 * r + 2, :]).then_inc(s_crow[s], 16)
                if r:
                    load(3 * r + 5)
            for n in range(3 * ROUNDS_A + 3, TILE_G + 7):
                load(n)

            def sample_queries(s):
                if s >= 2:
                    sp.wait_ge(S["s_prod"], 6 * (s - 1))
                    sp.wait_ge(S["s_prodv"], s - 1)
                if s == 0:
                    sp.wait_ge(s_used, USE_COMBINE + 2)
                sp.dma_start(qbc[s % 2][:, :], q_dram[s:s + 1, :].to_broadcast([P, ROUNDS * P])).then_inc(S[f"s_qb{s % 2}"], 16)

            def sample_rows(s, kv):
                for p in range(PAGES):
                    page = sp.value_load(pt[0:1, PAGES * s + p:PAGES * s + p + 1], min_val=0, max_val=POOL_PAGES - 1)
                    src = A["cache_a_kv"][0, bass.ds(page, 1), :, kv, :, :].rearrange("o t h d -> (o t) (h d)")
                    sp.dma_start(kv_a[s % 2][:, p, :], src).then_inc(S[f"s_kp{s % 2}"], 16)
                for g in range(BG):
                    n, step = SLOTS[g], DIL[g]
                    src = caches[g][0, s, 0:n * step:step, kv, :, :].rearrange("t h d -> t (h d)")
                    sp.dma_start(kv_b[s % 2][0:n, g, :], src).then_inc(S[f"s_bk{s % 2}"], 16)

            sp.wait_ge(s_kst, 16 * ROUNDS)
            sp.wait_ge(s_vst, 16 * ROUNDS)
            sp.wait_ge(S["s_comb"], 1)
            sample_rows(0, 0)
            sp.wait_ge(S["s_qd"], 16)
            sp.wait_ge(S["s_selfp"], 1)
            n = TILE_G + 7
            for s in range(DEC):
                sample_queries(s)
                if s:
                    sample_rows(s, 0)
                load(n)
                n += 1
            for k in range(3):
                load(n + k)
            sp.wait_ge(S["s_prod"], 6 * DEC)
            sp.wait_ge(S["s_prodv"], DEC)
            sp.wait_ge(S["s_slfd"], 48)
            sp.dma_start(row_a[:, PAST:PAST + 1], selfa_dram.rearrange("s (h o) -> (s h) o", o=1)).then_inc(S["s_selfr"], 16)
            sp.dma_start(sm[:, 0:1], lfn_dram.rearrange("s (h o) -> (s h) o", o=1)).then_inc(S["s_selfr"], 16)
            sp.dma_start(sm[0:DEC * BH, 1:1 + BG], selfb_dram.rearrange("s (h g) -> (s h) g", g=BG)).then_inc(S["s_selfr"], 16)
            sample_rows(0, 1)
            load(n + 3)
            sample_rows(1, 1)
            load(n + 4)
            load(n + 5)
            n += 6
            for s in range(2, DEC):
                sp.wait_ge(S["s_samp"], s - 1)
                sample_rows(s, 1)
                load(n)
                n += 1
            sp.wait_ge(S["s_os"], 1)
            sp.wait_ge(S["s_sst"], 16 * 8)
            sp.dma_start(p_in[:, :, :], A["p_prompt"][0, 0].rearrange("(b p) d -> p b d", p=P)).then_inc(S["s_pin"], 16)
            sp.dma_start(ps_in[:, :], A["p_sample"][0].rearrange("s o d -> (s o) d")).then_inc(S["s_pin"], 16)
            while n < TILES:
                load(n)
                n += 1

        @block.gpsimd
        def _(pool):
            own = Tally(s_p)
            pool.dma_start(pt[:, :], A["page_table"].rearrange("(o s) p -> o (s p)", o=1)).then_inc(s_pt, 16)
            pool.dma_start(relb[0:32, :], A["rel_bias"]).then_inc(s_small, 16)
            pool.dma_start(tables[:, :], const_in[1]).then_inc(s_small, 16)
            pool.dma_start(bf[:, :], A["b_f"].rearrange("o h -> h o"), allow_slow_non_contiguous=True).then_inc(s_small, 16)
            pool.dma_start(early[:, :], const_in[2]).then_inc(s_small, 16)
            pool.wait_ge(s_const, 16)
            pool.wait_ge(s_small, 16 * 4)
            nc.gpsimd.tensor_copy(identb[:, :], ident).then_inc(S["s_relb"], 1)
            c0, c1 = EARLY_COLS["causal"]
            nc.gpsimd.tensor_copy(causalb[:, :], early[:, c0:c1]).then_inc(S["s_relb"], 1)
            pool.wait_ge(S["s_relb"], 2)
            nc.gpsimd.memset(relb[32:33, :], NEG).then_inc(S["s_relb"], 1)
            pool.wait_ge(S["s_relb"], 3)
            for g in range(BG):
                last = nc.gpsimd.tensor_copy(relb_rows[:, g, :, :], relb[:, g * BH:(g + 1) * BH].unsqueeze(1).to_broadcast([33, DEC, BH]))
            last.then_inc(S["s_relb"], 1)
            pool.wait_ge(S["s_relb"], 4)
            for c in range(DC):
                pool.wait_ge(S["s_hh"], c + 1)
                nc.gpsimd.tensor_tensor(h_lo[:, c, :], h_raw[:, c, :], h_hi[:, c, :].bitcast(F32), ALU.subtract).then_inc(S["s_hl"], 1)
            pool.wait_ge(S["s_hl"], DC)
            for buf in (*q_aug, *k_aug):
                last = nc.gpsimd.memset(buf[HD:HD + 2, :, :], 1.0)
            last.then_inc(S["s_clear"], 1)
            pool.wait_ge(S["s_gen"], BG)
            for g in range(BG):
                for h in range(BH):
                    src = gen[g][h:h + 1, :].unsqueeze(1).to_broadcast([1, P, PITCH[g]])
                    pool.dma_start(toep_dram[g][h:h + 1, :].rearrange("o (i y) -> o i y", i=P), src).then_inc(S["s_gend"], 16)
            pool.wait_ge(S["s_gend"], 16 * BG * BH)
            for g in range(BG):
                for h in range(BH):
                    rows = toep_dram[g][h, P - 1:P - 1 + P * (PITCH[g] - 1)].rearrange("(i y) -> i y", i=P)
                    pool.dma_start(toep[g][:, h, :], rows[:, 0:TOEP[g]]).then_inc(S["s_toep"], 16)
            pool.wait_ge(s_used, USE_LOGF + 1)
            pool.dma_start(alf_p[0, 0].rearrange("(b p) h -> p b h", p=P), lf_small[:, 0:NB, :]).then_inc(S["s_lfst"], 16)
            pool.dma_start(alf_s[0].rearrange("s o h -> (s o) h"), lf_small[0:DEC, NB, :]).then_inc(S["s_lfst"], 16)
            pool.dma_start(lfn_dram, lf_small[0:DEC, NB, :]).then_inc(S["s_slfd"], 16)

            for r in range(1, ROUNDS + 1):
                t = r - 1
                if r <= ROUNDS - 1:
                    for g in range(BG):
                        wb = caches[g].shape[2]
                        if g == 0 and r > 1:
                            continue
                        s0, s1 = (0, DEC) if g == 0 else (r - 1, r)
                        if s1 > DEC:
                            continue
                        a = 16 // (s1 - s0)
                        pool.dma_start(b_s[g][0, s0:s1, 0:wb - 1].rearrange("s t k h d -> s (t k h d)").rearrange("s (a n) -> s a n", a=a),
                                       caches[g][0, s0:s1, 1:wb].rearrange("s t k h d -> s (t k h d)").rearrange("s (a n) -> s a n", a=a)).then_inc(S["s_copy"], 16)
                pool.wait_ge(s_used, use0[r] + 1)
                for kv, (buf, done) in enumerate(((k_tok, s_kst), (v_tok, s_vst))):
                    if kv == 1:
                        pool.wait_ge(s_used, use0[r] + 2)
                    if is_a(r):
                        dst = akv_p[0, 0, :, kv, 2 * t:2 * t + 2, :].rearrange("(b p) h d -> p b (h d)", p=P)
                        pool.dma_start(dst, buf[:, :, :]).then_inc(done, 16)
                    else:
                        g, hp = divmod(t - ROUNDS_A, 2)
                        out = b_p[g][0, 0, :, kv, 2 * hp:2 * hp + 2, :]
                        if g == 0:
                            pool.dma_start(out.rearrange("p h d -> p (h d)"), buf[:, NB - 1, :]).then_inc(done, 16)
                        elif kv == 0:
                            pool.dma_start(out.rearrange("(b p) h d -> p b (h d)", p=P), buf[:, :, :]).then_inc(done, 16)
                        else:
                            pool.dma_start(out.rearrange("(p c) h d -> p c (h d)", c=CLS), buf[:, :, :]).then_inc(done, 16)
                if r == ROUNDS_A + 2:
                    pool.wait_ge(s_pve, unit0[r + 1])
                    pool.wait_ge(s_mx, unit0[r + 1])
                    pool.dma_start(o0_dram.rearrange("(b p) n -> p b n", p=P), obuf[:, 0]).then_inc(S["s_o0"], 16)
                    pool.dma_start(m0_dram.rearrange("(b p) n -> p b n", p=P), mbuf[:, 0]).then_inc(S["s_o0"], 16)
                    pool.dma_start(l0_dram.rearrange("(b p) n -> p b n", p=P), lbuf[:, 0]).then_inc(S["s_o0"], 16)
                    pool.wait_ge(S["s_o0"], 48)
                    pool.dma_start(obuf[:, 0], o0_dram.rearrange("(p c) n -> p c n", c=CLS)).then_inc(S["s_o0r"], 16)
                    pool.dma_start(mbuf[:, 0], m0_dram.rearrange("(p c) n -> p c n", c=CLS)).then_inc(S["s_o0r"], 16)
                    pool.dma_start(lbuf[:, 0], l0_dram.rearrange("(p c) n -> p c n", c=CLS)).then_inc(S["s_o0r"], 16)
            pool.wait_ge(S["s_o0r"], 48)
            pool.wait_ge(s_pve, UNITS)
            pool.wait_ge(S["s_cw"], 1)
            for g in range(2):
                o = obuf[:, g, :, :].rearrange("p c (h d) -> p (c h) d", d=HD)
                own.up(nc.gpsimd.tensor_tensor(o, o, mbuf[:, g, :, :].rearrange("p c h -> p (c h)").unsqueeze(2).to_broadcast([P, CLS * BH, HD]), ALU.mult))
            fo = lambda g: obuf[:, g, :, :].rearrange("p c n -> p (c n)")
            pool.wait_ge(s_p, own.n)
            own.up(nc.gpsimd.tensor_tensor(fo(0), fo(0), fo(1), ALU.add))
            pool.wait_ge(s_p, own.n)
            pool.wait_ge(S["s_cw"], 2)
            nc.gpsimd.tensor_tensor(fo(0), fo(0), fo(2), ALU.add).then_inc(S["s_comb"], 1)
            pool.wait_ge(s_used, USE_SAMP + 8)
            stv = st[:, :, :].rearrange("s (r j) c -> s j r c", j=3)
            pool.dma_start(q_dram.rearrange("s (r c) -> s r c", c=P), stv[:, 0]).then_inc(S["s_qd"], 16)
            pool.wait_ge(S["s_selfp"], 1)
            pool.dma_start(selfa_dram, self_a[:, :]).then_inc(S["s_slfd"], 16)
            pool.dma_start(selfb_dram, self_b[:, :, :].rearrange("s h g -> s (h g)")).then_inc(S["s_slfd"], 16)
            k = 0
            for s in range(DEC):
                pool.wait_ge(S[f"s_qb{s % 2}"], 16 * (s // 2 + 1))
                pool.wait_ge(S[f"s_kp{s % 2}"], 64 * (s // 2 + 1))
                pool.wait_ge(S[f"s_bk{s % 2}"], 48 * (s // 2 + 1))
                for i in range(PAGES + BG):
                    if i == PAGES - 1:
                        continue
                    if k >= PRODS:
                        pool.wait_ge(S["s_red"], k - PRODS + 1)
                    if i < PAGES:
                        nc.gpsimd.tensor_tensor(prod[k % PRODS][:, :], kv_a[s % 2][:, i, :], qbc[s % 2][:, 0:AW], ALU.mult).then_inc(S["s_prod"], 1)
                    else:
                        g = i - PAGES
                        n = SLOTS[g]
                        nc.gpsimd.tensor_tensor(prod[k % PRODS][0:n, 0:BO], kv_b[s % 2][0:n, g, :], qbc[s % 2][0:n, AW + g * BO:AW + (g + 1) * BO], ALU.mult).then_inc(S["s_prod"], 1)
                    k += 1
            for kv in range(2):
                pool.dma_start(akv_s[0, :, 0, kv].rearrange("s (r h) d -> s r (h d)", h=2), stv[:, 1 + kv, 0:ROUNDS_A]).then_inc(S["s_sst"], 16)
                for g in range(BG):
                    wb = caches[g].shape[2]
                    r0 = ROUNDS_A + 2 * g
                    pool.dma_start(b_s[g][0, :, wb - 1, kv].rearrange("s (r h) d -> s r (h d)", h=2), stv[:, 1 + kv, r0:r0 + 2]).then_inc(S["s_sst"], 16)
            pool.wait_ge(S["s_red"], 6 * DEC)
            nc.gpsimd.memset(pTa[:, :, :, :, :], 0.0).then_inc(S["s_pz"], 1)
            nc.gpsimd.memset(pTb[:, :, :, :, :], 0.0).then_inc(S["s_pz"], 1)
            for i in range(6):
                pool.wait_ge(S["s_ogh"], i + 1)
                nc.gpsimd.tensor_tensor(og_lo[:, i, 0:SEQ], og_raw[i % 2][:, :], og_hi[:, i, 0:SEQ].bitcast(F32), ALU.subtract).then_inc(S["s_ogl"], 1)
            for m in range(DC):
                pool.wait_ge(S["s_mh"], m + 1)
                nc.gpsimd.tensor_tensor(h_lo[:, m, :], gsig[:, m, :], h_hi[:, m, :].bitcast(F32), ALU.subtract).then_inc(S["s_ml"], 1)
            def square_sum(total_, m, sq_done, done):
                pool.wait_ge(S[sq_done], m + 1)
                if m == 1:
                    nc.gpsimd.tensor_tensor(total_[:, :], sq2[0][:, :], sq2[1][:, :], ALU.add).then_inc(S[done], 2)
                if m >= 2:
                    pool.wait_ge(S[done], m)
                    nc.gpsimd.tensor_tensor(total_[:, :], total_[:, :], sq2[m % 2][:, :], ALU.add).then_inc(S[done], 1)

            pool.wait_ge(S["s_ptl"], 2)
            def ple_rest(m):
                n = TILE_PLE + m
                pool.wait_ge(s_hi, n + 1)
                k = chunks(n)
                nc.gpsimd.tensor_tensor(w_lo[n % RING][:, 0:k, :], w_raw[n % RING][:, 0:k, :], w_hi[n % RING][:, 0:k, :].bitcast(F32), ALU.subtract).then_inc(S["s_lop"], 1)

            for m in range(DC):
                square_sum(acc_y, m, "s_sqy", "s_acy")
                if m >= DC - RING:
                    ple_rest(m - (DC - RING))
            for m in range(RING, DC):
                ple_rest(m)
            for c in range(DC):
                pool.wait_ge(S["s_x2h"], c + 1)
                nc.gpsimd.tensor_tensor(h_lo[:, c, :], xT[:, c, :], h_hi[:, c, :].bitcast(F32), ALU.subtract).then_inc(S["s_x2l"], 1)
            for m in range(DC):
                square_sum(acc_e, m, "s_sqe", "s_ace")
            for m in range(DC):
                pool.wait_ge(S["s_tte"], m + 1)
                pool.dma_start(yp[0, :, m * P:(m + 1) * P].rearrange("(b p) d -> p b d", p=P), tok_out[m % 2][:, :, :]).then_inc(S[f"s_yst{m % 2}"], 16)
            pool.wait_ge(S["s_ttse"], 2)
            pool.dma_start(ys.rearrange("s o d -> (s o) d"), toks_out[:, :]).then_inc(S["s_ysst"], 16)
            pool.wait_ge(S["s_lfst"], 32)
            pool.wait_ge(S["s_copy"], 16 * (1 + 2 * DEC))
            pool.wait_ge(s_kst, 16 * ROUNDS)
            pool.wait_ge(s_vst, 16 * ROUNDS)
            pool.wait_ge(S["s_sst"], 16 * 8)
            pool.wait_ge(S["s_yst0"], 16 * DC // 2)
            pool.wait_ge(S["s_yst1"], 16 * DC // 2)
            pool.wait_ge(S["s_ysst"], 16)

        def later_sums_t(pe, turn):
            pe.wait_ge(S["s_lfr"], 16 * DEC * PAGES)
            turn([(P, h * 32, lf_rows[:, h:PAGE * AH:AH]) for h in range(AH)])
            pe.wait_ge(s_used, USE_LF + 1)
            cols = lfT[:, :, :, :].rearrange("p g s h -> p (g s h)")
            c0, c1 = EARLY_COLS["later"]
            nc.tensor.matmul(pv[0][:, 0:256], early[:, c0:c1], cols, start=True, stop=False)
            for k in range(1, PAGES):
                w = 256 - 64 * k
                last = nc.tensor.matmul(pv[0][:, 0:w], ones, cols[:, 64 * k:256], start=False, stop=k == PAGES - 1)
            last.then_inc(S["s_suf"], 1)

        def sample_rows_t(pe, turn):
            pe.wait_ge(S["s_lga"], 1)
            turn([(DEC * AH, p * P, lg_a[:, p, :, :].rearrange("p s h -> p (s h)")) for p in range(PAGES)])
            at, outs = 0, []
            for g in range(BG):
                outs.append((DEC * BH, at, lg_b[0:SLOTS[g], g, :, :].rearrange("p s h -> p (s h)")))
                at += SLOTS[g] + 1
            turn(outs)

        def sample_probs_t(pe, turn):
            pe.wait_ge(S["s_pn"], 2)
            turn([(P, p * 64, row_a[:, p * P:(p + 1) * P]) for p in range(PAGES)])
            at, outs = 0, []
            for g in range(BG):
                outs.append((SLOTS[g], g * 32, row_b[:, at:at + SLOTS[g]]))
                at += SLOTS[g] + 1
            turn(outs)
            pe.wait_ge(S["s_ds"], 1 + BG)
            nc.tensor.matmul(pv[0][0:DEC, 0:64], dsel_a[:, :], ident[0:64, 0:64], start=True, stop=True)
            for g in range(BG):
                last = nc.tensor.matmul(pv[0][0:DEC, 64 + 32 * g:96 + 32 * g], dsel_b[:, g, :], ident[0:32, 0:32], start=True, stop=True)
            last.then_inc(S["s_dm"], 1)

        def sample_values(pe, s):
            pe.wait_ge(S[f"s_kp{s % 2}"], 64 * (DEC // 2 + s // 2 + 1))
            pe.wait_ge(S[f"s_bk{s % 2}"], 48 * (DEC // 2 + s // 2 + 1))
            pe.wait_ge(s_used, USE_ROW + 4)
            pe.wait_ge(S["s_dv"], 2)
            for p in range(PAGES):
                nc.tensor.matmul(pv[0][0:DEC * AH, :], pTa[:, p, s, :, :].rearrange("p s h -> p (s h)"), kv_a[s % 2][:, p, :],
                                 start=s == 0 and p == 0, stop=False)
            for g in range(BG):
                n = SLOTS[g]
                last = nc.tensor.matmul(pv[1][0:DEC * BH, 0:BO], pTb[0:n, g, s, :, :].rearrange("p s h -> p (s h)"), kv_b[s % 2][0:n, g, :],
                                        start=s == 0 and g == 0, stop=False)
            last.then_inc(S["s_samp"], 1)

        def sample_end(pe):
            pe.wait_ge(S["s_dv"], 2)
            stv = st[:, :, :].rearrange("s (r j) c -> s j r c", j=3)[:, 2]
            nc.tensor.matmul(pv[0][0:DEC * AH, :], d_a[:, :], stv[:, 0:ROUNDS_A, :], start=False, stop=True)
            for g in range(BG):
                r0 = ROUNDS_A + 2 * g
                last = nc.tensor.matmul(pv[1][0:DEC * BH, 0:BO], d_b[:, g, :], stv[:, r0:r0 + 2, :], start=False, stop=g == BG - 1)
            last.then_inc(S["s_os"], 1)

        def sample_channels(pe):
            pe.wait_ge(S["s_osm"], 2)
            for cc in range(AW // P):
                nc.tensor.matmul(pv[0][:, cc * DEC:(cc + 1) * DEC], os_a[:, cc * P:(cc + 1) * P], cst("row_a", 64), start=True, stop=True)
            for cc in range(BO // P):
                last = nc.tensor.matmul(pv[0][:, 32 + cc * DEC:32 + (cc + 1) * DEC], os_b[:, cc * P:(cc + 1) * P], cst("row_b", 32), start=True, stop=True)
            last.then_inc(S["s_ot"], 1)

        @block.tensor
        def _(pe):
            use = Tally(s_use)

            def turn(outs):
                b = tr[use.n % 2]
                if use.n >= 2:
                    pe.wait_ge(s_used, use.n - 1)
                for rows, c0, src in outs:
                    k = src.shape[0]
                    w = 1
                    for x in src.shape[1:]:
                        w *= x
                    last = nc.tensor.transpose(b[0:rows, c0:c0 + k], src, ident[0:k, 0:k])
                use.up(last)

            def product(out, w_slot, k0, x_hi, x_lo, c_x, cols, first, last):
                lo, hi = cols
                pairs = ((w_hi[w_slot], x_hi), (w_hi[w_slot], x_lo), (w_lo[w_slot], x_hi))
                for i, (w, x) in enumerate(pairs):
                    ins = nc.tensor.matmul(out, w[:, k0, :], x[:, c_x, lo:hi], start=first and i == 0, stop=last and i == 2)
                return ins

            def project(n, k, x_hi=h_hi, x_lo=h_lo, each=None, kc=DC):
                half, part = divmod(k, 2)
                if k == 0:
                    wait_parts(pe, n)
                if part == 0 and n > 0:
                    pe.wait_ge(s_free[half], n)
                for c in range(part * kc // 2, (part + 1) * kc // 2):
                    if each is not None and half == 0:
                        pe.wait_ge(S[each], c + 1)
                    ins = product(pj[half][:, 0:HALF], n % RING, c, x_hi, x_lo, c, HALVES[half], c == 0, c == kc - 1)
                if part == 1:
                    ins.then_inc(s_half[half], 1)

            pe.wait_ge(s_const, 16)
            pe.wait_ge(s_xs, 16)
            for c in range(DC):
                last = nc.tensor.transpose(pv[0][:, c * DEC:(c + 1) * DEC], xs_in[:, c * P:(c + 1) * P], ident[0:DEC, 0:DEC])
            last.then_inc(S["s_xst"], 1)
            pe.wait_ge(s_g, 48)
            nc.tensor.transpose(pv[1][:, 256:256 + 3 * DC], g_rows[:, :], ident[0:3 * DC, 0:3 * DC]).then_inc(S["s_gt"], 1)
            for b in range(NB):
                pe.wait_ge(s_x[b], 16)

            def turn_x(c):
                turn([(P, b * P, x_in[:, b, c * P:(c + 1) * P]) for b in range(NB)])

            for c in range(3):
                turn_x(c)
            pe.wait_ge(S["s_rs"], 1)
            for b in range(NB + 1):
                k = P if b < NB else DEC
                lo, hi = b * P, b * P + k
                for half, (h0, h1) in enumerate(HALVES):
                    a, z = max(lo, h0), min(hi, h1)
                    if a < z:
                        last = nc.tensor.matmul(pj[half][:, a - h0:z - h0], rs[0:k, b:b + 1].to_broadcast([k, P]), ident[0:k, a - lo:z - lo], start=True, stop=True)
            last.then_inc(S["s_rsb"], 1)
            for c in range(3, DC):
                turn_x(c)
            pe.wait_ge(S["s_relb"], 4)
            for g in range(BG):
                b = (sc[0], sc[1], pv[1])[g]
                c0, c1 = TABLE_COLS[f"toep{g}"]
                nc.tensor.matmul(b[0:BH, 0:PITCH[g]], relb[:, g * BH:(g + 1) * BH], tables[:, c0:c1], start=True, stop=True).then_inc(S["s_gent"], 1)
            at = DC * DEC
            for g in range(BG):
                c0, c1 = TABLE_COLS[f"slots{g}"]
                last = nc.tensor.matmul(pv[0][0:DEC * BH, at:at + c1 - c0], relb_rows[:, g, :, :], tables[:, c0:c1], start=True, stop=True)
                at += c1 - c0
            last.then_inc(S["s_biasm"], 1)
            pe.wait_ge(S["s_wflo"], 1)
            pe.wait_ge(S["s_gen"], BG)
            pe.wait_ge(S["s_bias"], 1)
            for half, (lo, hi) in enumerate(HALVES):
                for c in range(DC):
                    if half == 0:
                        pe.wait_ge(S["s_hl"], c + 1)
                    for i, (w, x) in enumerate(((wf_hi, h_hi), (wf_hi, h_lo), (wf_lo, h_hi))):
                        last = nc.tensor.matmul(pv[half][0:AH, 0:HALF], w[:, c, :], x[:, c, lo:hi], start=c == 0 and i == 0, stop=c == DC - 1 and i == 2)
            last.then_inc(S["s_fm"], 1)

            def scores(r, i):
                hd, qb = units(r)[i]
                u = unit0[r] + i
                s = (r - 1) % 2
                b = sc[u % 2]
                if i == 0:
                    pe.wait_ge(s_free[0], 3 * r)
                    pe.wait_ge(s_free[1], 3 * r)
                    if is_a(r):
                        pe.wait_ge(s_crow[s], 32 * ((r - 1) // 2 + 1))
                if u >= 2:
                    if u - 2 < unit_a:
                        pe.wait_ge(s_ex, u - 1)
                    else:
                        pe.wait_ge(s_mx, u - 1)
                if is_a(r):
                    n = (qb + 1) * P
                    nc.tensor.matmul(b[:, 0:n], q_aug[s][:, hd, qb * P:n], k_aug[s][:, hd, 0:n], start=True, stop=False)
                    last = nc.tensor.matmul(b[:, qb * P:n], identb[:, :], causalb[:, :], start=False, stop=True)
                elif qb is not None:
                    k0 = max(qb - 1, 0) * P
                    n = (qb + 1) * P - k0
                    last = nc.tensor.matmul(b[:, 0:n], q_aug[s][0:HD, hd, qb * P:(qb + 1) * P], k_aug[s][0:HD, hd, k0:k0 + n], start=True, stop=True)
                else:
                    for c in range(CLS):
                        last = nc.tensor.matmul(b[:, c * P:(c + 1) * P], q_aug[s][0:HD, hd, c:SEQ:CLS], k_aug[s][0:HD, hd, c:SEQ:CLS], start=True, stop=True)
                last.then_inc(s_sc, 1)

            def blocks(r, qb):
                return qb + 1 if is_a(r) else CLS if qb is None else min(qb, 1) + 1

            def probs_t(r, i):
                u = unit0[r] + i
                pe.wait_ge(s_ex, u + 1)
                turn([(P, j * P, prob[u % 2][:, j * P:(j + 1) * P]) for j in range(blocks(r, units(r)[i][1]))])

            def values(r, i):
                hd, qb = units(r)[i]
                u = unit0[r] + i
                pe.wait_ge(s_used, pt_use[u] + 1)
                if u >= 2:
                    pe.wait_ge(s_pve, u - 1)
                n = blocks(r, qb)
                first = 0 if is_a(r) or qb is None else max(qb - 1, 0)
                for j in range(n):
                    v = v_tok[:, first + j, hd * HD:(hd + 1) * HD]
                    p = probT[u % 2][:, j * P:(j + 1) * P]
                    if qb is None:
                        last = nc.tensor.matmul(pv[u % 2][:, j * HD:(j + 1) * HD], p, v, start=True, stop=True)
                    else:
                        last = nc.tensor.matmul(pv[u % 2][:, 0:HD], p, v, start=j == 0, stop=j == n - 1)
                last.then_inc(s_pv, 1)

            for r in range(ROUNDS + 1):
                nu = len(units(r))
                for i in range(12):
                    if r and i == 0:
                        pe.wait_ge(s_free[0], 3 * r)
                        pe.wait_ge(s_free[1], 3 * r)
                        turn([(P, b * P, kT[:, b * P:(b + 1) * P]) for b in range(NB)])
                        if r - 1 < ROUNDS_A + 2:
                            turn([(P, b * P, vT[:, b * P:(b + 1) * P]) for b in range(NB)])
                        else:
                            turn([(P, c * P, vT[:, c:SEQ:CLS]) for c in range(CLS)])
                    if i < nu:
                        scores(r, i)
                    project(3 * r + i // 4, i % 4)
                    if r == 0 and i == 9:
                        pe.wait_ge(S["s_logf"], 1)
                        b = tr[use.n % 2]
                        pe.wait_ge(s_used, use.n - 1)
                        for k in range(NB):
                            nc.tensor.transpose(b[:, k * AH:(k + 1) * AH], logf[:, k * P:(k + 1) * P], ident[0:AH, 0:AH])
                        use.up(nc.tensor.transpose(b[0:DEC, NB * AH:(NB + 1) * AH], logf[:, SEQ:T], ident[0:AH, 0:AH]))
                    if r == 0 and i == 10:
                        later_sums_t(pe, turn)
                    if 1 <= i <= nu:
                        probs_t(r, i - 1)
                    if 2 <= i <= nu + 1:
                        if r == 1 and i == 2:
                            pe.wait_ge(S["s_lsum"], 1)
                        values(r, i - 2)
                    if i == 10 and r and is_a(r):
                        pe.wait_ge(s_pve, unit0[r] + 8)
                        turn([(P, b * P, o_tok[:, b, :]) for b in range(NB)])
                    if r == ROUNDS and i >= 8:
                        for k in range(2 * (i - 8), 2 * (i - 8) + 2):
                            turn([(DEC, (q - 4 * k) * P, samp[:, q, :]) for q in range(4 * k, min(4 * k + 4, 3 * ROUNDS))])
                    if r == ROUNDS and i == 11:
                        assert use.n == USE_COMBINE
                        pe.wait_ge(S["s_comb"], 1)
                        for cc in range(2):
                            turn([(P, c * P, obuf[:, 0, c, cc * P:(cc + 1) * P]) for c in range(CLS)])

            for n in range(TILE_G + 3, TILE_BR):
                for k in range(4):
                    project(n, k)
                t = n - TILE_G - 3
                if t == 10:
                    sample_rows_t(pe, turn)
                if t == 12:
                    sample_probs_t(pe, turn)
                if 13 <= t < 17:
                    sample_values(pe, t - 13)
                if t >= 17:
                    sample_values(pe, 2 * t - 30)
                    sample_values(pe, 2 * t - 29)
            for m in range(DC):
                n = TILE_BR + m
                wait_parts(pe, n)
                for half, cols in enumerate(HALVES):
                    pe.wait_ge(s_free[half], n)
                    if m == 0 and half == 0:
                        sample_end(pe)
                    if m == 0 and half == 1:
                        sample_channels(pe)
                        pe.wait_ge(S["s_ogsl"], 1)
                    for c in range(6):
                        if m == 0 and half == 0:
                            pe.wait_ge(S["s_ogl"], c + 1)
                        out = (pj if c < 4 else sc)[half][:, 0:HALF]
                        ins = product(out, n % RING, c, og_hi, og_lo, c, cols, c in (0, 4), c in (3, 5))
                    ins.then_inc(s_half[half], 1)
                if m == 3:
                    pe.wait_ge(S["s_pin"], 32)
                    for c in range(2):
                        for b in range(NB):
                            last = nc.tensor.transpose(pv[c][:, b * P:(b + 1) * P], p_in[:, b, c * P:(c + 1) * P], ident)
                        last.then_inc(S["s_ptr"], 1)
                    turn([(P, c * DEC, ps_in[:, c * P:(c + 1) * P]) for c in range(2)])

            def mean_square(total_, ready, done):
                pe.wait_ge(S[ready], DC)
                for half, (lo, hi) in enumerate(HALVES):
                    last = nc.tensor.matmul(pv[half][:, 0:HALF], ones, total_[:, lo:hi], start=True, stop=True)
                last.then_inc(S[done], 1)

            for n in range(TILE_OUT, TILE_PLE):
                for k in range(4):
                    project(n, k, h_hi, h_lo, "s_ml" if n == TILE_OUT else None)
            for n in range(TILE_PLE, TILE_GATE):
                for k in range(4):
                    project(n, k, pT_hi, pT_lo, "s_ptl" if n == TILE_PLE else None, 2)
                if n == TILE_PLE + 1:
                    pe.wait_ge(S["s_pte"], 2)
                    mean_square(acc_y, "s_acy", "s_ssy")
            def result(m):
                pe.wait_ge(S["s_fin"], m + 1)
                if m >= 2:
                    pe.wait_ge(S["s_tte"], m - 1)
                for b in range(NB):
                    last = nc.tensor.transpose(sc[m % 2][:, b * P:(b + 1) * P], fin[m % 2][:, b * P:(b + 1) * P], ident)
                last.then_inc(S["s_tt"], 1)
                nc.tensor.transpose(pv[m // 4][0:DEC, m % 4 * P:m % 4 * P + P], fin[m % 2][:, SEQ:T], ident).then_inc(S["s_tts"], 1)

            for m in range(DC):
                if m == 2:
                    pe.wait_ge(S["s_nvy"], 2)
                    mean_square(acc_e, "s_ace", "s_sse")
                    pe.wait_ge(S["s_nve"], 2)
                for k in range(4):
                    project(TILE_GATE + m, k, h_hi, h_lo, "s_x2l" if m == 0 else None)
                if m >= 2:
                    result(m - 2)
            for m in range(DC - 2, DC):
                result(m)

        @block.scalar
        def _(act):
            own = Tally(s_a)

            def hi_part(n):
                act.wait_ge(s_w[n % RING], landed_at[n])
                if n >= RING:
                    act.wait_ge(s_half[1], n - RING + 1)
                k = chunks(n)
                nc.scalar.activation(w_hi[n % RING][:, 0:k, :], w_raw[n % RING][:, 0:k, :], ACT.Copy).then_inc(s_hi, 1)

            for i, name in enumerate(("g_pre", "g_post", "g_ple")):
                act.dma_start(g_rows[i * DC:(i + 1) * DC, :], A[name][0].rearrange("(c p) -> c p", p=P)).then_inc(s_g, 16)
            act.wait_ge(S["s_ssz"], 1)
            act.wait_ge(s_xs, 16)
            nc.scalar.activation(sq_junk[:, :], xs_in[:, :], ACT.Square, accum_out=ss[0:DEC, NB:NB + 1]).then_inc(S["s_sqx"], 1)
            for b in range(NB):
                act.wait_ge(s_x[b], 16)
                nc.scalar.activation(h_raw[:, 2 * b:2 * b + 2, 0:D // 2], x_in[:, b, :].rearrange("p (k n) -> p k n", k=2), ACT.Square, accum_out=ss[:, b:b + 1]).then_inc(S["s_sqx"], 1)
            act.wait_ge(S["s_nv"], 1)
            own.up(nc.scalar.activation(nt[:, :], nv[:, :], ACT.Ln))
            act.wait_ge(s_a, own.n)
            nc.scalar.activation(rs[:, :], nt[:, :], ACT.Exp, scale=-0.5).then_inc(S["s_y0"], 1)
            act.wait_ge(s_wf, 16)
            nc.scalar.activation(wf_hi[:, :, :], wf_raw[:, :, :], ACT.Copy).then_inc(S["s_wfhi"], 1)
            hi_part(0)
            for c in range(DC):
                act.wait_ge(S["s_hraw"], c + 1)
                nc.scalar.activation(h_hi[:, c, :], h_raw[:, c, :], ACT.Copy).then_inc(S["s_hh"], 1)
            hi_part(1)
            hi_part(2)
            act.wait_ge(S["s_fx"], 2)
            own.up(nc.scalar.activation(fa[:, :], fx[:, :], ACT.Abs))
            act.wait_ge(s_a, own.n)
            nc.scalar.activation(fe[:, :], fa[:, :], ACT.Exp, scale=-1.0).then_inc(S["s_fe"], 1)
            act.wait_ge(S["s_fu"], 1)
            nc.scalar.activation(fa[:, :], fu[:, :], ACT.Ln).then_inc(S["s_fl"], 1)
            act.wait_ge(S["s_fl"], 1)
            nc.scalar.activation(fr[:, :], fa[:, :], ACT.Exp, scale=-1.0).then_inc(S["s_fl"], 1)

            def evac0(n):
                act.wait_ge(s_half[0], n + 1)
                ps = pj[0]
                if n < TILE_G:
                    r, j = divmod(n, 3)
                    s = r % 2
                    if j == 0:
                        nc.scalar.activation(q_aug[s][0:HD, 0, 0:HALF], ps[0:HD, 0:HALF], ACT.Copy, scale=SCALE)
                        last = nc.scalar.activation(q_aug[s][0:HD, 1, 0:HALF], ps[HD:P, 0:HALF], ACT.Copy, scale=SCALE)
                    elif j == 1:
                        nc.scalar.activation(k_aug[s][0:HD, 0, 0:HALF], ps[0:HD, 0:HALF], ACT.Copy)
                        nc.scalar.activation(k_aug[s][0:HD, 1, 0:HALF], ps[HD:P, 0:HALF], ACT.Copy)
                        last = nc.scalar.activation(kT[:, 0:HALF], ps[:, 0:HALF], ACT.Copy)
                    else:
                        last = nc.scalar.activation(vT[:, 0:HALF], ps[:, 0:HALF], ACT.Copy)
                    last.then_inc(s_free[0], 1)
                else:
                    gate(n, 0)

            def gate(n, half):
                lo, hi = HALVES[half]
                if n < TILE_Z:
                    dst = gsig[:, n - TILE_G, lo:hi]
                    nc.scalar.activation(dst, pj[half][:, 0:HALF], ACT.Copy if n == TILE_G else ACT.Sigmoid).then_inc(s_free[half], 1)
                else:
                    nc.scalar.activation(zsil[:, n - TILE_Z, lo:hi], pj[half][:, 0:HALF], ACT.Sigmoid).then_inc(S["s_ge"], 1)

            def evac1(n):
                if n < TILE_G:
                    return
                act.wait_ge(s_half[1], n + 1)
                gate(n, 1)

            def exps(r, i):
                hd, qb = units(r)[i]
                u = unit0[r] + i
                act.wait_ge(s_mx, u + 1)
                if u >= 2:
                    act.wait_ge(s_use, pt_use[u - 2] + 1)
                if is_a(r):
                    n = (qb + 1) * P
                    if u >= 8:
                        act.wait_ge(s_rc, u - 7)
                    last = nc.scalar.activation(prob[u % 2][:, 0:n], sc[u % 2][:, 0:n], ACT.Exp, bias=nm_a[:, u % 8:u % 8 + 1], accum_out=l_a[:, u % 8:u % 8 + 1])
                else:
                    g, hp = divmod(r - 1 - ROUNDS_A, 2)
                    h = 2 * hp + hd
                    if qb is not None:
                        n = (min(qb, 1) + 1) * P
                        last = nc.scalar.activation(prob[u % 2][:, 0:n], biased[u % 2][:, 0:n], ACT.Exp, bias=nm_b[:, 4 * (u % 2):4 * (u % 2) + 1],
                                                    accum_out=lbuf[:, g, qb, h:h + 1])
                    else:
                        for c in range(CLS):
                            last = nc.scalar.activation(prob[u % 2][:, c * P:(c + 1) * P], biased[u % 2][:, c * P:(c + 1) * P], ACT.Exp,
                                                        bias=nm_b[:, 4 * (u % 2) + c:4 * (u % 2) + c + 1], accum_out=lbuf[:, g, c, h:h + 1])
                last.then_inc(s_ex, 1)

            def values_out(r, i):
                hd, qb = units(r)[i]
                u = unit0[r] + i
                act.wait_ge(s_pv, u + 1)
                if is_a(r):
                    act.wait_ge(s_rc, u + 1)
                    if i == 0 and r > 1:
                        act.wait_ge(s_use, use0[r])
                    last = nc.scalar.activation(o_tok[:, qb, hd * HD:(hd + 1) * HD], pv[u % 2][:, 0:HD], ACT.Copy, scale=r_a[:, u % 8:u % 8 + 1])
                else:
                    g, hp = divmod(r - 1 - ROUNDS_A, 2)
                    h = 2 * hp + hd
                    if qb is not None:
                        last = nc.scalar.activation(obuf[:, g, qb, h * HD:(h + 1) * HD], pv[u % 2][:, 0:HD], ACT.Copy)
                    else:
                        last = nc.scalar.activation(obuf[:, g, :, h * HD:(h + 1) * HD], pv[u % 2][:, 0:CLS * HD].rearrange("p (c d) -> p c d", d=HD), ACT.Copy)
                last.then_inc(s_pve, 1)

            for r in range(ROUNDS + 1):
                nu = len(units(r))
                for i in range(12):
                    n = 3 * r + i // 4
                    if i < nu:
                        exps(r, i)
                    if i % 4 == 1:
                        evac0(n)
                    if 2 <= i <= nu + 1:
                        values_out(r, i - 2)
                    if r == ROUNDS and i == 4:
                        act.wait_ge(S["s_md"], 1)
                        nc.scalar.activation(mbuf[:, :, :, :], mbuf[:, :, :, :], ACT.Exp).then_inc(S["s_wexp"], 1)
                        act.wait_ge(s_free[0], TILE_G + 1)
                        act.wait_ge(s_free[1], TILE_G + 1)
                        nc.scalar.activation(gsig[:, 0, :], gsig[:, 0, :], ACT.Sigmoid).then_inc(S["s_g3"], 1)
                    if i % 4 == 3:
                        evac1(n)
                        hi_part(n + RING)

            for n in range(TILE_G + 3, TILE_BR):
                t = n - TILE_G - 3
                evac0(n)
                evac1(n)
                hi_part(n + RING)
                if t == 10:
                    act.wait_ge(S["s_nma"], 1)
                    nc.scalar.activation(row_a[:, :], row_a[:, :], ACT.Exp, bias=sm[:, 5:6], accum_out=sm[:, 6:7]).then_inc(S["s_exa"], 1)
                    act.wait_ge(S["s_nmb"], 1)
                    nc.scalar.activation(row_b[:, :], row_b[:, :], ACT.Exp, bias=sm[0:32, 8:9], accum_out=sm[0:32, 9:10]).then_inc(S["s_exb"], 1)
                if n >= TILE_Z:
                    i = n - TILE_Z
                    act.wait_ge(S["s_ogr"], i + 1)
                    nc.scalar.activation(og_hi[:, i, 0:SEQ], og_raw[i % 2][:, :], ACT.Copy).then_inc(S["s_ogh"], 1)
            act.wait_ge(S["s_ogsr"], 1)
            nc.scalar.activation(og_hi[:, :, SEQ:T], og_s[:, :, :], ACT.Copy).then_inc(S["s_ogsh"], 1)
            for m in range(DC):
                hi_part(TILE_BR + m + RING)
                act.wait_ge(s_free[0], TILE_BR + m + 1)
                act.wait_ge(s_free[1], TILE_BR + m + 1)
                nc.scalar.activation(h_hi[:, m, :], gsig[:, m, :], ACT.Copy).then_inc(S["s_mh"], 1)
                if m == 5:
                    act.wait_ge(s_used, USE_ROW + 5)
                    for c in range(2):
                        nc.scalar.activation(pT_hi[:, c, :], acc_y[:, :] if c else acc_e[:, :], ACT.Copy).then_inc(S["s_pth"], 1)
            for m in range(DC):
                n = TILE_OUT + m
                act.wait_ge(s_half[0], n + 1)
                nc.scalar.activation(yT[:, m, 0:HALF], pj[0][:, 0:HALF], ACT.Copy).then_inc(s_free[0], 1)
                act.wait_ge(s_free[0], n + 1)
                act.wait_ge(s_free[1], n + 1)
                if m >= 2:
                    act.wait_ge(S["s_acy"], m - 1)
                nc.scalar.activation(sq2[m % 2][:, :], yT[:, m, :], ACT.Square).then_inc(S["s_sqy"], 1)
                hi_part(n + RING)
            def x_hi(c):
                act.wait_ge(S["s_xsum"], c + 1)
                nc.scalar.activation(h_hi[:, c, :], xT[:, c, :], ACT.Copy).then_inc(S["s_x2h"], 1)

            def ple_square(m):
                act.wait_ge(s_free[0], TILE_PLE + m + 1)
                act.wait_ge(s_free[1], TILE_PLE + m + 1)
                if m >= 2:
                    act.wait_ge(S["s_ace"], m - 1)
                else:
                    act.wait_ge(S["s_acy"], DC)
                nc.scalar.activation(sq2[m % 2][:, :], eT[:, m, :], ACT.Square).then_inc(S["s_sqe"], 1)

            for m in range(DC):
                n = TILE_PLE + m
                act.wait_ge(s_half[0], n + 1)
                nc.scalar.activation(eT[:, m, 0:HALF], pj[0][:, 0:HALF], ACT.Copy).then_inc(s_free[0], 1)
                act.wait_ge(s_half[1], n + 1)
                nc.scalar.activation(eT[:, m, HALF:T], pj[1][:, 0:HALF], ACT.Copy).then_inc(s_free[1], 1)
                hi_part(n + RING)
                if m == 2:
                    act.wait_ge(S["s_nvy"], 2)
                    own.up(nc.scalar.activation(nt2[:, :], nv2[:, :], ACT.Ln))
                    act.wait_ge(s_a, own.n)
                    nc.scalar.activation(rs_y[:, :], nt2[:, :], ACT.Exp, scale=-0.5).then_inc(S["s_y0y"], 1)
                if m == 4:
                    ple_square(0)
                    ple_square(1)
                if m >= 5:
                    x_hi(2 * (m - 5))
                    x_hi(2 * (m - 5) + 1)
            x_hi(6)
            x_hi(7)
            for m in range(2, 5):
                ple_square(m)
            for m in range(DC):
                n = TILE_GATE + m
                if m == 2:
                    act.wait_ge(S["s_nve"], 2)
                    own.up(nc.scalar.activation(nt2[:, :], nv2[:, :], ACT.Ln))
                    act.wait_ge(s_a, own.n)
                    nc.scalar.activation(rs_e[:, :], nt2[:, :], ACT.Exp, scale=-0.5).then_inc(S["s_y0e"], 1)
                if m >= 2:
                    act.wait_ge(S["s_fin"], m - 1)
                for half, (lo, hi) in enumerate(HALVES):
                    act.wait_ge(s_half[half], n + 1)
                    nc.scalar.activation(sg[m % 2][:, lo:hi], pj[half][:, 0:HALF], ACT.Sigmoid).then_inc(s_free[half], 1)
                if n + RING < TILES:
                    hi_part(n + RING)
                if m == 0:
                    for e in range(5, DC):
                        ple_square(e)

        @block.vector
        def _(dve):
            own = Tally(s_v)
            used = Tally(s_used)
            V = nc.vector

            def link(ins):
                own.up(ins)
                dve.wait_ge(s_v, own.n)

            def lo_part(n):
                dve.wait_ge(s_hi, n + 1)
                k = chunks(n)
                V.tensor_tensor(w_lo[n % RING][:, 0:k, :], w_raw[n % RING][:, 0:k, :], w_hi[n % RING][:, 0:k, :].bitcast(F32), ALU.subtract).then_inc(s_lo, 1)

            def out_of_turn(*moves):
                dve.wait_ge(s_use, used.n + 1)
                b = tr[used.n % 2]
                for dst, src in moves:
                    last = V.tensor_copy(dst, src(b))
                used.up(last)

            def rsqrt(y, v, t, done):
                link(V.tensor_tensor(t, y, y, ALU.mult))
                link(V.tensor_tensor(t, t, v, ALU.mult))
                link(V.tensor_scalar(t, t, -0.5, 1.5, ALU.mult, ALU.add))
                V.tensor_tensor(y, y, t, ALU.mult).then_inc(done, 1)

            V.memset(ss[:, :], 1.0).then_inc(S["s_ssz"], 1)
            dve.wait_ge(S["s_xst"], 1)
            V.tensor_copy(xT[:, :, SEQ:T], pv[0][:, 0:DC * DEC].rearrange("p (c s) -> p c s", s=DEC)).then_inc(S["s_xsv"], 1)
            dve.wait_ge(S["s_gt"], 1)
            V.tensor_copy(g_all[:, :], pv[1][:, 256:256 + 3 * DC]).then_inc(S["s_gv"], 1)
            dve.wait_ge(S["s_sqx"], NB + 1)
            V.tensor_scalar(nv[:, :], ss[:, :], 1.0 / D, EPS, ALU.mult, ALU.add).then_inc(S["s_nv"], 1)
            for c in range(2):
                out_of_turn((xT[:, c, 0:SEQ], lambda b: b[:, :]))
            dve.wait_ge(S["s_y0"], 1)
            rsqrt(rs[:, :], nv[:, :], nt[:, :], S["s_rs"])
            for c in range(DC):
                if c + 2 < DC:
                    out_of_turn((xT[:, c + 2, 0:SEQ], lambda b: b[:, :]))
                if c == 0:
                    dve.wait_ge(S["s_rsb"], 1)
                    dve.wait_ge(S["s_gv"], 1)
                    dve.wait_ge(S["s_xsv"], 1)
                dve.wait_ge(s_used, c + 1)
                for half, (lo, hi) in enumerate(HALVES):
                    last = V.scalar_tensor_tensor(h_raw[:, c, lo:hi], xT[:, c, lo:hi], gpre[:, c:c + 1], pj[half][:, 0:HALF], ALU.mult, ALU.mult)
                last.then_inc(S["s_hraw"], 1)
                if c == 3:
                    dve.wait_ge(S["s_wfhi"], 1)
                    V.tensor_tensor(wf_lo[:, :, :], wf_raw[:, :, :], wf_hi[:, :, :].bitcast(F32), ALU.subtract).then_inc(S["s_wflo"], 1)
            for g in range(BG):
                dve.wait_ge(S["s_gent"], g + 1)
                V.tensor_copy(gen[g][:, :], (sc[0], sc[1], pv[1])[g][0:BH, 0:PITCH[g]]).then_inc(S["s_gen"], 1)
            dve.wait_ge(S["s_biasm"], 1)
            V.tensor_copy(bias_s[:, :], pv[0][0:DEC * BH, DC * DEC:DC * DEC + sum(SLOTS) + BG]).then_inc(S["s_bias"], 1)
            lo_part(0)
            lo_part(1)
            lo_part(2)
            dve.wait_ge(S["s_fm"], 1)
            for half, (lo, hi) in enumerate(HALVES):
                V.tensor_scalar(fx[:, lo:hi], pv[half][0:AH, 0:HALF], bf[:, 0:1], None, ALU.add).then_inc(S["s_fx"], 1)
            dve.wait_ge(S["s_fe"], 1)
            V.tensor_scalar(fu[:, :], fe[:, :], 1.0, None, ALU.add).then_inc(S["s_fu"], 1)
            dve.wait_ge(S["s_fu"], 1)
            link(V.tensor_scalar(fd[:, :], fu[:, :], -1.0, None, ALU.add))
            link(V.tensor_tensor(fd[:, :], fe[:, :], fd[:, :], ALU.subtract))
            dve.wait_ge(S["s_fl"], 2)
            link(V.tensor_tensor(fd[:, :], fd[:, :], fr[:, :], ALU.mult))
            link(V.tensor_tensor(fd[:, :], fa[:, :], fd[:, :], ALU.add))
            V.scalar_tensor_tensor(logf[:, :], fx[:, :], 0.0, fd[:, :], ALU.min, ALU.subtract).then_inc(S["s_logf"], 1)
            dve.wait_ge(S["s_logf"], 1)
            V.tensor_tensor_scan(cum[:, :], ones[0:AH, 0:1].to_broadcast([AH, SEQ]), logf[:, 0:SEQ], 0.0, ALU.mult, ALU.add).then_inc(S["s_cum"], 1)
            dve.wait_ge(S["s_cum"], 1)
            V.tensor_scalar(ncum[:, :], cum[:, :], -1.0, None, ALU.mult).then_inc(S["s_cum"], 1)
            def evac1(n):
                dve.wait_ge(s_half[1], n + 1)
                r, j = divmod(n, 3)
                s = r % 2
                ps = pj[1]
                V.tensor_scalar(samp[:, n, :], ps[:, HALF - DEC:HALF], SCALE if j == 0 else 1.0, None, ALU.mult)
                if j == 0:
                    for hd in range(2):
                        last = V.tensor_scalar(q_aug[s][0:HD, hd, HALF:T], ps[hd * HD:(hd + 1) * HD, 0:HALF], SCALE, None, ALU.mult)
                elif j == 1:
                    for hd in range(2):
                        V.tensor_copy(k_aug[s][0:HD, hd, HALF:T], ps[hd * HD:(hd + 1) * HD, 0:HALF])
                    last = V.tensor_copy(kT[:, HALF:T], ps[:, 0:HALF])
                else:
                    last = V.tensor_copy(vT[:, HALF:T], ps[:, 0:HALF])
                last.then_inc(s_free[1], 1)

            def silu(n):
                dve.wait_ge(S["s_ge"], 2 * (n - TILE_Z) + 2)
                for half, (lo, hi) in enumerate(HALVES):
                    buf = zsil[:, n - TILE_Z, lo:hi]
                    V.tensor_tensor(buf, buf, pj[half][:, 0:HALF], ALU.mult).then_inc(s_free[half], 1)

            def maxima(r, i):
                hd, qb = units(r)[i]
                u = unit0[r] + i
                dve.wait_ge(s_sc, u + 1)
                if is_a(r):
                    if u >= 8:
                        dve.wait_ge(s_ex, u - 7)
                    V.tensor_reduce(nm_a[:, u % 8:u % 8 + 1], sc[u % 2][:, 0:(qb + 1) * P], AX.X, ALU.max, negate=True).then_inc(s_mx, 1)
                    return
                g, hp = divmod(r - 1 - ROUNDS_A, 2)
                h = 2 * hp + hd
                dve.wait_ge(s_ex, u - 1)
                if u == unit_a:
                    dve.wait_ge(s_use, use0[r])
                    dve.wait_ge(S["s_toep"], 16 * BG * BH)
                if qb is not None:
                    n = (min(qb, 1) + 1) * P
                    link(V.tensor_tensor_reduce(out=biased[u % 2][:, 0:n], in0=sc[u % 2][:, 0:n], in1=toep[0][:, h, 2 * P - n:2 * P], scale=1.0, scalar=-3e38,
                                                op0=ALU.add, op1=ALU.max, accum_out=mbuf[:, g, qb, h:h + 1]))
                    V.tensor_scalar(nm_b[:, 4 * (u % 2):4 * (u % 2) + 1], mbuf[:, g, qb, h:h + 1], -1.0, None, ALU.mult).then_inc(s_mx, 1)
                else:
                    for c in range(CLS):
                        cols = slice(c * P, (c + 1) * P)
                        ins = V.tensor_tensor_reduce(out=biased[u % 2][:, cols], in0=sc[u % 2][:, cols], in1=toep[g][:, h, :], scale=1.0, scalar=-3e38,
                                                     op0=ALU.add, op1=ALU.max, accum_out=mbuf[:, g, c, h:h + 1])
                    link(ins)
                    V.tensor_scalar(nm_b[:, 4 * (u % 2):4 * (u % 2) + 4], mbuf[:, g, :, h], -1.0, None, ALU.mult).then_inc(s_mx, 1)

            def probs_out(r, i):
                u = unit0[r] + i
                qb = units(r)[i][1]
                n = (qb + 1 if is_a(r) else CLS if qb is None else min(qb, 1) + 1) * P
                if u >= 2:
                    dve.wait_ge(s_pv, u - 1)
                out_of_turn((probT[u % 2][:, 0:n], lambda b: b[:, 0:n]))

            def combine():
                dve.wait_ge(S["s_o0r"], 48)
                dve.wait_ge(s_ex, UNITS)
                flat = lambda b, g: b[:, g, :, :].rearrange("p c h -> p (c h)")
                mm, den = top_m, den_m
                link(V.tensor_tensor(mm[:, :], flat(mbuf, 0), flat(mbuf, 1), ALU.max))
                link(V.tensor_tensor(mm[:, :], mm[:, :], flat(mbuf, 2), ALU.max))
                V.tensor_tensor(mbuf[:, :, :, :].rearrange("p g c h -> p g (c h)"), mbuf[:, :, :, :].rearrange("p g c h -> p g (c h)"),
                                mm[:, :].unsqueeze(1).to_broadcast([P, BG, CLS * BH]), ALU.subtract).then_inc(S["s_md"], 1)
                dve.wait_ge(S["s_wexp"], 1)
                allg = lambda b: b[:, :, :, :].rearrange("p g c h -> p (g c h)")
                link(V.tensor_tensor(allg(lbuf), allg(lbuf), allg(mbuf), ALU.mult))
                link(V.tensor_reduce(den[:, :], lbuf[:, :, :, :].rearrange("p g c h -> p (c h) g"), AX.X, ALU.add))
                link(V.reciprocal(den[:, :], den[:, :]))
                V.tensor_tensor(mbuf[:, :, :, :].rearrange("p g c h -> p g (c h)"), mbuf[:, :, :, :].rearrange("p g c h -> p g (c h)"),
                                den[:, :].unsqueeze(1).to_broadcast([P, BG, CLS * BH]), ALU.mult).then_inc(S["s_cw"], 1)
                dve.wait_ge(S["s_cw"], 1)
                dve.wait_ge(s_pve, UNITS)
                o = obuf[:, 2, :, :].rearrange("p c (h d) -> p (c h) d", d=HD)
                V.tensor_tensor(o, o, flat(mbuf, 2).unsqueeze(2).to_broadcast([P, CLS * BH, HD]), ALU.mult).then_inc(S["s_cw"], 1)

            def sample_selves_logits():
                dve.wait_ge(s_used, used.n)
                stv = st[:, :, :].rearrange("s (r j) c -> s j r c", j=3)
                link(V.tensor_tensor(self_p[:, :, :], stv[:, 0], stv[:, 1], ALU.mult))
                heads = self_p[:, :, :].rearrange("s r (h d) -> s (r h) d", d=HD)
                link(V.tensor_reduce(self_a[:, :], heads[:, 0:AH], AX.X, ALU.add))
                for g in range(BG):
                    ins = V.tensor_reduce(self_b[:, :, g], heads[:, AH + BH * g:AH + BH * (g + 1)], AX.X, ALU.add)
                ins.then_inc(S["s_selfp"], 1)

            for r in range(ROUNDS + 1):
                nu = len(units(r))
                t = r - 1
                for i in range(12):
                    n = 3 * r + i // 4
                    if r and i == 0:
                        if r >= 2:
                            dve.wait_ge(s_kst, 16 * (r - 1))
                        out_of_turn((k_tok[:, :, :].rearrange("p b c -> p (b c)"), lambda b: b[:, :]))
                        if r >= 2:
                            dve.wait_ge(s_vst, 16 * (r - 1))
                            dve.wait_ge(s_pv, unit0[r])
                        out_of_turn((v_tok[:, :, :].rearrange("p b c -> p (b c)"), lambda b: b[:, :]))
                    if i < nu:
                        maxima(r, i)
                    if is_a(r) and 1 <= i <= nu:
                        u = unit0[r] + i - 1
                        dve.wait_ge(s_ex, u + 1)
                        if u >= 8:
                            dve.wait_ge(s_pve, u - 7)
                        V.reciprocal(r_a[:, u % 8:u % 8 + 1], l_a[:, u % 8:u % 8 + 1]).then_inc(s_rc, 1)
                    if r == 0 and i == 9:
                        dve.wait_ge(s_use, used.n + 1)
                        b = tr[used.n % 2]
                        V.tensor_copy(lf_small[:, 0:NB, :].rearrange("p b h -> p (b h)"), b[:, 0:NB * AH])
                        used.up(V.tensor_copy(lf_small[0:DEC, NB, :], b[0:DEC, NB * AH:(NB + 1) * AH]))
                    if r == 0 and i == 10:
                        out_of_turn((lfT[:, :, :, :].rearrange("p g s h -> p h s g"), lambda b: b[:, 0:256].rearrange("p (h s g) -> p h s g", h=AH, g=PAGES)))
                        dve.wait_ge(S["s_suf"], 1)
                        V.tensor_copy(later[:, :], pv[0][:, 0:PAGES * DEC * AH]).then_inc(S["s_lsum"], 1)
                    if 1 <= i <= nu:
                        probs_out(r, i - 1)
                    if i % 4 == 3:
                        if n < TILE_G:
                            evac1(n)
                        lo_part(n + RING)
                    if i == 10 and r and is_a(r):
                        out_of_turn((oaT[:, t, 0:SEQ], lambda b: b[:, :]))
                    if r == ROUNDS and i == 4:
                        combine()
                    if r == ROUNDS and i == 8:
                        dve.wait_ge(s_kst, 16 * ROUNDS)
                        dve.wait_ge(s_vst, 16 * ROUNDS)
                    if r == ROUNDS and i >= 8:
                        for k in range(2 * (i - 8), 2 * (i - 8) + 2):
                            w = min(4, 3 * ROUNDS - 4 * k)
                            out_of_turn((st[:, 4 * k:4 * k + w, :].rearrange("p r c -> p (r c)"), lambda b, w=w: b[0:DEC, 0:w * P]))
                    if r == ROUNDS and i == 11:
                        sample_selves_logits()
                        for cc in range(2):
                            out_of_turn((obT[:, cc, 0:SEQ].rearrange("p (i c) -> p c i", c=CLS), lambda b: b[:, :].rearrange("p (c i) -> p c i", c=CLS)))

            red = [0]

            def sample_logits(s):
                dve.wait_ge(S[f"s_qb{s % 2}"], 16 * (s // 2 + 1))
                dve.wait_ge(S[f"s_kp{s % 2}"], 64 * (s // 2 + 1))
                V.tensor_tensor(prod_v[:, :], kv_a[s % 2][:, PAGES - 1, :], qbc[s % 2][:, 0:AW], ALU.mult).then_inc(S["s_prodv"], 1)
                dve.wait_ge(S["s_prodv"], s + 1)
                V.tensor_reduce(lg_a[:, PAGES - 1, s, :], prod_v[:, :].rearrange("p (h d) -> p h d", d=HD), AX.X, ALU.add)
                for i in range(PAGES + BG):
                    if i == PAGES - 1:
                        continue
                    k = red[0]
                    dve.wait_ge(S["s_prod"], k + 1)
                    if i < PAGES:
                        src, dst = prod[k % PRODS][:, :].rearrange("p (h d) -> p h d", d=HD), lg_a[:, i, s, :]
                    else:
                        n = SLOTS[i - PAGES]
                        src, dst = prod[k % PRODS][0:n, 0:BO].rearrange("p (h d) -> p h d", d=HD), lg_b[0:n, i - PAGES, s, :]
                    V.tensor_reduce(dst, src, AX.X, ALU.add).then_inc(S["s_red"], 1)
                    red[0] += 1

            def sample_softmax():
                dve.wait_ge(S["s_selfr"], 48)
                dve.wait_ge(s_use, used.n + 1)
                used.up(V.tensor_scalar(row_a[:, 0:PAST], tr[used.n % 2][0:DEC * AH, :], sm[:, 0:1], None, ALU.add))
                dve.wait_ge(s_used, used.n)
                V.tensor_reduce(sm[:, 5:6], row_a[:, :], AX.X, ALU.max, negate=True).then_inc(S["s_nma"], 1)
                dve.wait_ge(s_use, used.n + 1)
                b, at = tr[used.n % 2], 0
                for g in range(BG):
                    to = at + SLOTS[g]
                    V.tensor_tensor(row_b[:, to:to + 1], sm[0:32, 1 + g:2 + g], bias_s[:, to:to + 1], ALU.add)
                    last = V.tensor_tensor(row_b[:, at:to], b[0:32, at:to], bias_s[:, at:to], ALU.add)
                    at = to + 1
                used.up(last)
                dve.wait_ge(s_used, used.n)
                V.tensor_reduce(sm[0:32, 8:9], row_b[:, :], AX.X, ALU.max, negate=True).then_inc(S["s_nmb"], 1)
                dve.wait_ge(S["s_exa"], 1)
                link(V.reciprocal(sm[:, 7:8], sm[:, 6:7]))
                V.tensor_scalar(row_a[:, :], row_a[:, :], sm[:, 7:8], None, ALU.mult).then_inc(S["s_pn"], 1)
                dve.wait_ge(S["s_exb"], 1)
                link(V.reciprocal(sm[0:32, 10:11], sm[0:32, 9:10]))
                V.tensor_scalar(row_b[:, :], row_b[:, :], sm[0:32, 10:11], None, ALU.mult).then_inc(S["s_pn"], 1)
                dve.wait_ge(S["s_pn"], 2)
                V.tensor_scalar(dsel_a[:, :], cst("row_a", 64), row_a[:, PAST:PAST + 1], None, ALU.mult).then_inc(S["s_ds"], 1)
                at = 0
                for g in range(BG):
                    at += SLOTS[g]
                    V.tensor_scalar(dsel_b[:, g, :], cst("row_b", 32), row_b[:, at:at + 1], None, ALU.mult).then_inc(S["s_ds"], 1)
                    at += 1

            def sample_selves():
                dve.wait_ge(S["s_pz"], 2)
                rows = lambda b, g0, g1, n, h: b[0:n, g0 * DEC * h:g1 * DEC * h].rearrange("p (g s h) -> p g s h", s=DEC, h=h)
                out_of_turn(*[(pTa[:, :, s, s, :], lambda b, s=s: rows(b, 0, PAGES, P, AH)[:, :, s, :]) for s in range(DEC)])
                out_of_turn(*[(pTb[:, 0:2, s, s, :], lambda b, s=s: rows(b, 0, 2, P, BH)[:, :, s, :]) for s in range(DEC)],
                            *[(pTb[0:SLOTS[2], 2:3, s, s, :], lambda b, s=s: rows(b, 2, 3, SLOTS[2], BH)[:, :, s, :]) for s in range(DEC)])
                dve.wait_ge(S["s_dm"], 1)
                V.tensor_copy(d_a[:, :], pv[0][0:DEC, 0:64]).then_inc(S["s_dv"], 1)
                V.tensor_copy(d_b[:, :, :].rearrange("s g x -> s (g x)"), pv[0][0:DEC, 64:160]).then_inc(S["s_dv"], 1)

            def result_out(m):
                dve.wait_ge(S["s_tt"], m + 1)
                if m >= 2:
                    dve.wait_ge(S[f"s_yst{m % 2}"], 16 * (m // 2))
                V.tensor_copy(tok_out[m % 2][:, :, :].rearrange("p b c -> p (b c)"), sc[m % 2][:, :]).then_inc(S["s_tte"], 1)

            for n in range(TILE_G + 3, TILE_BR):
                t = n - TILE_G - 3
                if n >= TILE_Z:
                    silu(n)
                lo_part(n + RING)
                if n >= TILE_Z:
                    i = n - TILE_Z
                    if i >= 2:
                        dve.wait_ge(S["s_ogl"], i - 1)
                    dve.wait_ge(s_free[1], n + 1)
                    src = oaT[:, i, 0:SEQ] if i < 4 else obT[:, i - 4, 0:SEQ]
                    V.tensor_tensor(og_raw[i % 2][:, :], src, zsil[:, i, 0:SEQ], ALU.mult).then_inc(S["s_ogr"], 1)
                if t < DEC:
                    sample_logits(t)
                if t == DEC - 1:
                    dve.wait_ge(S["s_red"], 6 * DEC)
                    la = lg_a[:, :, :, :].rearrange("p g s h -> p (g s h)")
                    V.tensor_tensor(la, la, later[:, :], ALU.add).then_inc(S["s_lga"], 1)
                if t == 10:
                    sample_softmax()
                if t == 12:
                    sample_selves()

            dve.wait_ge(S["s_os"], 1)
            heads = lambda b, n: b.rearrange("r (h d) -> r h d", h=n)
            V.tensor_tensor(heads(os_a[:, :], AH), heads(pv[0][0:DEC * AH, :], AH), cst("head_a", 64).unsqueeze(2).to_broadcast([64, AH, HD]), ALU.mult).then_inc(S["s_osm"], 1)
            V.tensor_tensor(heads(os_b[:, :], BH), heads(pv[1][0:DEC * BH, 0:BO], BH), cst("head_b", 32).unsqueeze(2).to_broadcast([32, BH, HD]), ALU.mult).then_inc(S["s_osm"], 1)
            dve.wait_ge(S["s_ot"], 1)
            V.tensor_copy(oaT[:, :, SEQ:T], pv[0][:, 0:32].rearrange("p (c s) -> p c s", s=DEC))
            V.tensor_copy(obT[:, :, SEQ:T], pv[0][:, 32:48].rearrange("p (c s) -> p c s", s=DEC)).then_inc(S["s_ov"], 1)
            dve.wait_ge(S["s_ov"], 1)
            V.tensor_tensor(og_s[:, 0:4, :], oaT[:, :, SEQ:T], zsil[:, 0:4, SEQ:T], ALU.mult)
            V.tensor_tensor(og_s[:, 4:6, :], obT[:, :, SEQ:T], zsil[:, 4:6, SEQ:T], ALU.mult).then_inc(S["s_ogsr"], 1)
            dve.wait_ge(S["s_ogsh"], 1)
            V.tensor_tensor(og_lo[:, :, SEQ:T], og_s[:, :, :], og_hi[:, :, SEQ:T].bitcast(F32), ALU.subtract).then_inc(S["s_ogsl"], 1)
            for m in range(DC):
                n = TILE_BR + m
                for half, (lo, hi) in enumerate(HALVES):
                    dve.wait_ge(s_half[half], n + 1)
                    a, b = gsig[:, m, lo:hi], gsig[:, DC + m, lo:hi]
                    V.tensor_tensor(a, a, pj[half][:, 0:HALF], ALU.mult)
                    own.up(V.tensor_tensor(b, b, sc[half][:, 0:HALF], ALU.mult))
                    dve.wait_ge(s_v, own.n)
                    last = V.tensor_tensor(a, a, b, ALU.add)
                    last.then_inc(s_free[half], 1)
                lo_part(n + RING)
                if m == 4:
                    dve.wait_ge(S["s_ptr"], 2)
                    dve.wait_ge(s_use, used.n + 1)
                    V.tensor_copy(acc_e[:, 0:SEQ], pv[0][:, :]).then_inc(S["s_pte"], 1)
                    V.tensor_copy(acc_y[:, 0:SEQ], pv[1][:, :]).then_inc(S["s_pte"], 1)
                    b = tr[used.n % 2]
                    V.tensor_copy(acc_e[:, SEQ:T], b[:, 0:DEC])
                    used.up(V.tensor_copy(acc_y[:, SEQ:T], b[:, DEC:2 * DEC]))
                if m == 6:
                    for c, src in enumerate((acc_e, acc_y)):
                        dve.wait_ge(S["s_pth"], c + 1)
                        V.tensor_tensor(pT_lo[:, c, :], src[:, :], pT_hi[:, c, :].bitcast(F32), ALU.subtract).then_inc(S["s_ptl"], 1)
            for m in range(DC):
                n = TILE_OUT + m
                dve.wait_ge(s_half[1], n + 1)
                V.tensor_copy(yT[:, m, HALF:T], pj[1][:, 0:HALF]).then_inc(s_free[1], 1)
                if n + RING < TILE_PLE:
                    lo_part(n + RING)

            def norm(rs_, nv_done, y0, done, ready):
                dve.wait_ge(S[ready], 1)
                for half, (lo, hi) in enumerate(HALVES):
                    V.tensor_scalar(nv2[:, lo:hi], pv[half][:, 0:HALF], 1.0 / D, EPS, ALU.mult, ALU.add).then_inc(S[nv_done], 1)
                dve.wait_ge(S[y0], 1)
                rsqrt(rs_[:, :], nv2[:, :], nt2[:, :], S[done])
                dve.wait_ge(S[done], 1)

            norm(rs_y, "s_nvy", "s_y0y", "s_rsy", "s_ssy")
            for c in range(DC):
                link(V.scalar_tensor_tensor(yT[:, c, :], yT[:, c, :], gpost[:, c:c + 1], rs_y[:, :], ALU.mult, ALU.mult))
                V.tensor_tensor(xT[:, c, :], xT[:, c, :], yT[:, c, :], ALU.add).then_inc(S["s_xsum"], 1)
                if c == 6:
                    lo_part(TILE_GATE)
            lo_part(TILE_GATE + 1)
            lo_part(TILE_GATE + 2)

            def final(m):
                n = TILE_GATE + m
                link(V.scalar_tensor_tensor(eT[:, m, :], eT[:, m, :], gple[:, m:m + 1], rs_e[:, :], ALU.mult, ALU.mult))
                dve.wait_ge(s_free[0], n + 1)
                dve.wait_ge(s_free[1], n + 1)
                link(V.tensor_tensor(eT[:, m, :], sg[m % 2][:, :], eT[:, m, :], ALU.mult))
                if m >= 2:
                    dve.wait_ge(S["s_tts"], m - 1)
                V.tensor_tensor(fin[m % 2][:, :], xT[:, m, :], eT[:, m, :], ALU.add).then_inc(S["s_fin"], 1)

            for m in range(DC):
                n = TILE_GATE + m
                if m == 2:
                    norm(rs_e, "s_nve", "s_y0e", "s_rse", "s_sse")
                    final(0)
                    final(1)
                if n + RING < TILES:
                    lo_part(n + RING)
                if m >= 2:
                    final(m)
                    result_out(m - 2)
            result_out(DC - 2)
            result_out(DC - 1)
            dve.wait_ge(S["s_tts"], DC)
            for i in range(2):
                V.tensor_copy(toks_out[:, 512 * i:512 * (i + 1)], pv[i][0:DEC, :]).then_inc(S["s_ttse"], 1)


_INS = ["x_prompt", "x_sample", "cache_a_kv", "cache_a_logf", "cache_b0_kv", "cache_b1_kv", "cache_b2_kv", "page_table",
        "p_prompt", "p_sample", "rel_bias", "g_pre", "w_in", "b_f", "w_br_a", "w_br_b", "w_out", "g_post", "w_ple", "g_ple", "w_ple_gate"]
_OUTS = [(1, SEQ, D), (DEC, 1, D), (1, 1, SEQ, 2, AH, HD), (1, 1, SEQ, AH),
         (1, 1, 128, 2, BH, HD), (1, 1, SEQ, 2, BH, HD), (1, 1, SEQ, 2, BH, HD),
         (1, DEC, 1, 2, AH, HD), (1, DEC, 1, AH),
         (1, DEC, 128, 2, BH, HD), (1, DEC, PAST, 2, BH, HD), (1, DEC, PAST, 2, BH, HD)]


def kernel(**inputs):
    import concourse.bacc as _bacc
    from concourse.bass_utils import run_bass_kernel_spmd as _run

    nc = _bacc.Bacc("TRN2", target_bir_lowering=False, num_devices=1)
    arrays, args = {}, {}
    for name in _INS:
        a = np.ascontiguousarray(inputs[name])
        arrays[f"in_{name}_dram"] = a
        args[name] = nc.dram_tensor(f"in_{name}_dram", a.shape, mybir.dt.from_np(a.dtype), kind="ExternalInput").ap()
    consts = []
    for name, a in (("const", CONST), ("tables", TABLES), ("early", EARLY)):
        arrays[f"in_{name}_dram"] = a
        consts.append(nc.dram_tensor(f"in_{name}_dram", a.shape, F32, kind="ExternalInput").ap())
    outs = [nc.dram_tensor(f"out_{i}_dram", shape, F32, kind="ExternalOutput").ap() for i, shape in enumerate(_OUTS)]
    build(nc, args, outs, consts)
    r = _run(nc, [arrays], core_ids=[0])
    return tuple(r.results[0][f"out_{i}_dram"] for i in range(len(_OUTS)))
```
